# Optimizing a Trainium2 kernel written in Bass

```python
import jax, jax.numpy as jnp
from jax import lax
import numpy as np

D_MODEL = 1024
BATCH = 1
SEQ = 2048
DEPTH = 1

D_DELTA = D_MODEL // 2
D_SGU = D_MODEL - D_DELTA
HEAD_DIM = 128
N_HEADS_DELTA = D_DELTA // HEAD_DIM
CONV_WIDTH = 5
DELTA_CHUNK = 64
SGU_CHUNK = 128
SGU_GROUP_DIM = 128
N_HEADS_SGU = D_SGU // SGU_GROUP_DIM
N_EXPERTS = 16
N_EXPERT_GROUPS = 4
EXPERTS_PER_GROUP = N_EXPERTS // N_EXPERT_GROUPS
TOP_K = 2
D_FF_EXPERT = D_MODEL
DEEPNORM_ALPHA = (2.0 * DEPTH) ** 0.25
DEEPNORM_BETA = (8.0 * DEPTH) ** -0.25
LN_EPS = 1e-5
RMS_EPS = 1e-6
L2_EPS = 1e-6
PROJ_SPLITS = (D_DELTA, D_DELTA, D_DELTA, D_DELTA,
               N_HEADS_DELTA, N_HEADS_DELTA, N_HEADS_DELTA, N_HEADS_DELTA,
               D_SGU, D_SGU)
PROJ_COLS = 4 * D_DELTA + 4 * N_HEADS_DELTA + 2 * D_SGU

kernel_name = "hybrid_delta_sgu_moe_deepnorm"

def layer_norm(x, g, b):
    xf = x.astype(jnp.float32)
    mu = jnp.mean(xf, -1, keepdims=True)
    var = jnp.mean(jnp.square(xf - mu), -1, keepdims=True)
    return ((xf - mu) * lax.rsqrt(var + LN_EPS) * g + b).astype(x.dtype)

def l2_normalize(t):
    return t * lax.rsqrt(jnp.sum(jnp.square(t), -1, keepdims=True) + L2_EPS)

def centred_depthwise_conv(x, w):
    pad = CONV_WIDTH // 2
    return lax.conv_general_dilated(
        x, w[:, None, :], window_strides=(1,), padding=[(pad, pad)],
        dimension_numbers=("NWC", "WIO", "NWC"), feature_group_count=x.shape[-1])

def gated_delta_rule_chunked(q, k, v, g, beta):
    b, s, h, dk = q.shape
    dv = v.shape[-1]
    n, c = s // DELTA_CHUNK, DELTA_CHUNK

    def chunk(t):
        t = t.reshape((b, n, c, h) + t.shape[3:])
        return jnp.moveaxis(t, (1, 3), (0, 2))

    qc = chunk(q) * (dk ** -0.5)
    kc, vc, bc = chunk(k), chunk(v), chunk(beta)
    gc = jnp.cumsum(chunk(g), axis=-1)
    idx = jnp.arange(c)
    lower_incl = idx[:, None] >= idx[None, :]
    strict = idx[:, None] > idx[None, :]
    diff = gc[..., :, None] - gc[..., None, :]
    decay = jnp.where(lower_incl, jnp.exp(jnp.where(lower_incl, diff, 0.0)), 0.0)
    kb = kc * bc[..., None]
    a_strict = jnp.where(strict, jnp.einsum("nbhid,nbhjd->nbhij", kb, kc) * decay, 0.0)
    eye = jnp.eye(c, dtype=q.dtype)
    t_mat = lax.linalg.triangular_solve(
        a_strict + eye, jnp.broadcast_to(eye, a_strict.shape),
        left_side=True, lower=True, unit_diagonal=True)
    u = jnp.einsum("nbhij,nbhjd->nbhid", t_mat, vc * bc[..., None])
    w = jnp.einsum("nbhij,nbhjd->nbhid", t_mat, kb * jnp.exp(gc)[..., None])
    qk = jnp.where(lower_incl, jnp.einsum("nbhid,nbhjd->nbhij", qc, kc) * decay, 0.0)

    def step(state, xs):
        q_i, k_i, u_i, w_i, g_i, qk_i = xs
        v_new = u_i - jnp.einsum("bhck,bhkv->bhcv", w_i, state)
        o_i = (jnp.einsum("bhck,bhkv->bhcv", q_i * jnp.exp(g_i)[..., None], state)
               + jnp.einsum("bhij,bhjv->bhiv", qk_i, v_new))
        g_last = g_i[..., -1:]
        k_dec = k_i * jnp.exp(g_last - g_i)[..., None]
        state = state * jnp.exp(g_last)[..., None] + jnp.einsum("bhck,bhcv->bhkv", k_dec, v_new)
        return state, o_i

    state0 = jnp.zeros((b, h, dk, dv), q.dtype)
    _, o = lax.scan(step, state0, (qc, kc, u, w, gc, qk))
    return jnp.moveaxis(o, (0, 2), (1, 3)).reshape(b, s, h, dv)

def delta_mixer(q, k, v, z, a_f, a_b, b_f, b_b, conv_w, a_log_f, dt_bias_f,
                a_log_b, dt_bias_b, norm_w):
    bsz, s, _ = q.shape
    qkv = jax.nn.silu(centred_depthwise_conv(jnp.concatenate([q, k, v], -1), conv_w))
    q, k, v = jnp.split(qkv.astype(jnp.float32), 3, axis=-1)
    heads = lambda t: t.reshape(bsz, s, N_HEADS_DELTA, HEAD_DIM)
    q, k, v = l2_normalize(heads(q)), l2_normalize(heads(k)), heads(v)
    g_f = -jnp.exp(a_log_f.astype(jnp.float32)) * jax.nn.softplus(a_f.astype(jnp.float32) + dt_bias_f)
    g_b = -jnp.exp(a_log_b.astype(jnp.float32)) * jax.nn.softplus(a_b.astype(jnp.float32) + dt_bias_b)
    beta_f = jax.nn.sigmoid(b_f.astype(jnp.float32))
    beta_b = jax.nn.sigmoid(b_b.astype(jnp.float32))
    flip = lambda t: jnp.flip(t, axis=1)
    o_f = gated_delta_rule_chunked(q, k, v, g_f, beta_f)
    o_b = flip(gated_delta_rule_chunked(flip(q), flip(k), flip(v), flip(g_b), flip(beta_b)))
    o = o_f + o_b
    o = o * lax.rsqrt(jnp.mean(jnp.square(o), -1, keepdims=True) + RMS_EPS) * norm_w
    o = o * jax.nn.silu(heads(z).astype(jnp.float32))
    return o.reshape(bsz, s, D_DELTA).astype(z.dtype)

def sgu_mixer(u, v, ln_g, ln_b, w_spatial, b_spatial):
    bsz, s, _ = u.shape
    u = jax.nn.gelu(u, approximate=False)
    v = layer_norm(jax.nn.gelu(v, approximate=False), ln_g, ln_b)
    n = s // SGU_CHUNK
    vc = v.reshape(bsz, n, SGU_CHUNK, N_HEADS_SGU, SGU_GROUP_DIM)
    mixed = jnp.einsum("gpq,bnqgd->bnpgd", w_spatial, vc) + b_spatial.T[:, :, None]
    return u * mixed.reshape(bsz, s, D_SGU)

def moe(x, w_router, router_bias, w_gate, w_up, w_down):
    bsz, s, d = x.shape
    xt = x.reshape(-1, d)
    n_tok = xt.shape[0]
    scores = jax.nn.sigmoid(jnp.dot(xt.astype(jnp.float32), w_router.astype(jnp.float32)))
    sel = (scores + router_bias).reshape(n_tok, N_EXPERT_GROUPS, EXPERTS_PER_GROUP)
    group_score = jnp.sum(lax.top_k(sel, TOP_K)[0], -1)
    best = jnp.argmax(group_score, -1)
    in_group = jnp.arange(N_EXPERT_GROUPS)[None, :] == best[:, None]
    sel = jnp.where(in_group[..., None], sel, -jnp.inf).reshape(n_tok, N_EXPERTS)
    _, top_idx = lax.top_k(sel, TOP_K)
    gates = jnp.take_along_axis(scores, top_idx, -1)
    gates = gates / jnp.sum(gates, -1, keepdims=True)
    expert_ids = top_idx.reshape(-1)
    order = jnp.argsort(expert_ids)
    tok = order // TOP_K
    xs = xt[tok]
    group_sizes = jnp.bincount(expert_ids, length=N_EXPERTS).astype(jnp.int32)
    hdn = jax.nn.silu(lax.ragged_dot(xs, w_gate, group_sizes)) * lax.ragged_dot(xs, w_up, group_sizes)
    y = lax.ragged_dot(hdn, w_down, group_sizes) * gates.reshape(-1)[order][:, None].astype(x.dtype)
    out = jax.ops.segment_sum(y, tok, num_segments=n_tok)
    return out.reshape(bsz, s, d)

def setup_inputs(seed: int = 0) -> dict:
    key = jax.random.key(seed)
    ks = jax.random.split(key, 24)
    f32 = jnp.float32
    nrm = lambda k, shape, scale: jax.random.normal(k, shape, f32) * scale

    def dt_bias(k):
        dt = jnp.exp(jax.random.uniform(k, (DEPTH, N_HEADS_DELTA), f32, np.log(1e-3), np.log(1e-1)))
        return dt + jnp.log(-jnp.expm1(-dt))

    def a_log(k):
        return jnp.log(jax.random.uniform(k, (DEPTH, N_HEADS_DELTA), f32, 1.0, 16.0))

    return {
        "x": nrm(ks[0], (BATCH, SEQ, D_MODEL), 1.0),
        "w_in": nrm(ks[1], (DEPTH, D_MODEL, PROJ_COLS), D_MODEL ** -0.5),
        "conv_w": nrm(ks[2], (DEPTH, CONV_WIDTH, 3 * D_DELTA), CONV_WIDTH ** -0.5),
        "a_log_f": a_log(ks[3]),
        "dt_bias_f": dt_bias(ks[4]),
        "a_log_b": a_log(ks[5]),
        "dt_bias_b": dt_bias(ks[6]),
        "delta_norm_w": 1.0 + nrm(ks[7], (DEPTH, HEAD_DIM), 0.02),
        "sgu_ln_g": 1.0 + nrm(ks[8], (DEPTH, D_SGU), 0.02),
        "sgu_ln_b": nrm(ks[9], (DEPTH, D_SGU), 0.02),
        "w_spatial": nrm(ks[10], (DEPTH, N_HEADS_SGU, SGU_CHUNK, SGU_CHUNK), SGU_CHUNK ** -0.5),
        "b_spatial": 1.0 + nrm(ks[11], (DEPTH, N_HEADS_SGU, SGU_CHUNK), 0.02),
        "w_out": nrm(ks[12], (DEPTH, D_MODEL, D_MODEL), DEEPNORM_BETA * D_MODEL ** -0.5),
        "ln1_g": 1.0 + nrm(ks[13], (DEPTH, D_MODEL), 0.02),
        "ln1_b": nrm(ks[14], (DEPTH, D_MODEL), 0.02),
        "w_router": nrm(ks[15], (D_MODEL, N_EXPERTS), D_MODEL ** -0.5),
        "router_bias": nrm(ks[16], (N_EXPERTS,), 0.01),
        "w_gate": nrm(ks[17], (DEPTH, N_EXPERTS, D_MODEL, D_FF_EXPERT), D_MODEL ** -0.5),
        "w_up": nrm(ks[18], (DEPTH, N_EXPERTS, D_MODEL, D_FF_EXPERT), D_MODEL ** -0.5),
        "w_down": nrm(ks[19], (DEPTH, N_EXPERTS, D_FF_EXPERT, D_MODEL), DEEPNORM_BETA * D_FF_EXPERT ** -0.5),
        "ln2_g": 1.0 + nrm(ks[20], (DEPTH, D_MODEL), 0.02),
        "ln2_b": nrm(ks[21], (DEPTH, D_MODEL), 0.02),
    }

def reference(x, w_in, conv_w, a_log_f, dt_bias_f, a_log_b, dt_bias_b, delta_norm_w,
              sgu_ln_g, sgu_ln_b, w_spatial, b_spatial, w_out, ln1_g, ln1_b,
              w_router, router_bias, w_gate, w_up, w_down, ln2_g, ln2_b):
    offsets = np.cumsum(PROJ_SPLITS)[:-1].tolist()
    for l in range(DEPTH):
        proj = jnp.einsum("bsd,dp->bsp", x, w_in[l])
        q, k, v, z, a_f, a_b, b_f, b_b, u_s, v_s = jnp.split(proj, offsets, axis=-1)
        o_delta = delta_mixer(q, k, v, z, a_f, a_b, b_f, b_b, conv_w[l], a_log_f[l], dt_bias_f[l],
                              a_log_b[l], dt_bias_b[l], delta_norm_w[l])
        o_sgu = sgu_mixer(u_s, v_s, sgu_ln_g[l], sgu_ln_b[l], w_spatial[l], b_spatial[l])
        mix = jnp.einsum("bsc,cd->bsd", jnp.concatenate([o_delta, o_sgu], -1), w_out[l])
        x = layer_norm(DEEPNORM_ALPHA * x + mix, ln1_g[l], ln1_b[l])
        ffn = moe(x, w_router, router_bias, w_gate[l], w_up[l], w_down[l])
        x = layer_norm(DEEPNORM_ALPHA * x + ffn, ln2_g[l], ln2_b[l])
    return x


_drawn_inputs = setup_inputs


def setup_inputs(seed=0):
    import zlib

    import numpy as np

    out = dict(_drawn_inputs(seed))
    spreads = {}
    factors = {'a_log_b': 2.931,
     'delta_norm_w': 5.458,
     'sgu_ln_g': 12.645,
     'sgu_ln_b': 6.017,
     'b_spatial': 5.518,
     'ln2_g': 8.732,
     'ln2_b': 8.12}
    for name, (base, spread) in spreads.items():
        noise = np.random.default_rng([zlib.crc32(name.encode()), seed]).standard_normal(out[name].shape)
        drawn = base * np.exp(spread * noise) if base else spread * noise
        out[name] = __import__('jax').numpy.asarray(drawn.astype(out[name].dtype))
    for name, factor in factors.items():
        out[name] = (out[name] * factor).astype(out[name].dtype)
    return out
```

```python
from contextlib import ExitStack

import concourse.bass as bass
from concourse import mybir

F32 = mybir.dt.float32
I32 = mybir.dt.int32
U32 = mybir.dt.uint32
ALU = mybir.AluOpType
ACT = mybir.ActivationFunctionType
AX = mybir.AxisListType

P = 128
D_MODEL = 1024
SEQ = 2048
HEADS = 4
QUAD = HEADS * P
KC = D_MODEL // P
TILES = SEQ // P
GROUP = 4
GROUPS = TILES // GROUP
TOKENS = GROUP * P
TAPS = 5
HALO = TAPS // 2
N_EXPERTS = 16
EXP_GROUPS = 4
PER_GROUP = N_EXPERTS // EXP_GROUPS
TOP_K = 2
PAIRS = SEQ * TOP_K
SLOTS = PAIRS // P + N_EXPERTS - 1
ALPHA = 2.0 ** 0.25
LN_EPS, RMS_EPS, L2_EPS = 1e-5, 1e-6, 1e-6

Q0, Z0, G0, U0, V0, COLS = 0, 3 * QUAD, 4 * QUAD, 4 * QUAD + 16, 5 * QUAD + 16, 6 * QUAD + 16
CHAINS = 2 * HEADS
KINDS = 6
GC, BETA, NBE, EG, KD, EL = range(KINDS)
BIG = 1e30


class Steps:

    def __init__(self, sem, names):
        self.sem, self.names, self.n = sem, list(names), 0
        self.pos = {name: i for i, name in enumerate(self.names)}
        assert len(self.pos) == len(self.names)

    def mark(self, name):
        assert self.names[self.n % len(self.names)] == name, (self.names[self.n % len(self.names)], name)
        self.n += 1
        return self.sem, 1

    def at(self, turn, name):
        return self.sem, (turn + 1) * len(self.names) + self.pos[name] + 1

    def start(self, engine):
        engine.sem_inc(self.sem, len(self.names))


def wait_alone(engine, met, sem, value):
    if not isinstance(value, int):
        with engine.register() as target:
            engine.reg_mov(target, value)
            engine.wait_ge(*met)
            engine.wait_ge(sem, target)
    else:
        engine.wait_ge(sem, value)


class Scope:

    def __init__(self, nc, stack, tag):
        self.nc, self.stack, self.tag = nc, stack, tag

    def sb(self, name, shape, dt=F32):
        return self.stack.enter_context(self.nc.sbuf_tensor(self.tag + name, shape, dt))

    def ps(self, name, shape, dt=F32):
        return self.stack.enter_context(self.nc.psum_tensor(self.tag + name, shape, dt))

    def sem(self, name):
        return self.stack.enter_context(self.nc.semaphore(self.tag + name))


def bcast(ap, n):
    return ap.unsqueeze(2).to_broadcast([ap.shape[0], ap.shape[1], n])


def over_heads(ap, n=HEADS):
    return ap.unsqueeze(1).to_broadcast([ap.shape[0], n, ap.shape[1]])


def heads(ap):
    return ap.rearrange("p (h m) -> p h m", h=HEADS)


def constants(nc, ident):
    with ExitStack() as stack:
        s = Scope(nc, stack, "k_")
        zeroed, done = s.sem("zeroed"), s.sem("done")
        block = stack.enter_context(nc.Block())

        @block.gpsimd
        def _(pool):
            pool.memset(ident[:], 0.0).then_inc(zeroed, 1)
            pool.wait_ge(zeroed, 1)
            pool.affine_select(out=ident[:], in_=ident[:], pattern=[[-1, P]], compare_op=ALU.not_equal,
                               fill=1.0, base=0, channel_multiplier=1).then_inc(done, 1)
            pool.wait_ge(done, 1)


def project(nc, d, ident, graw):
    with ExitStack() as stack:
        s = Scope(nc, stack, "a_")
        w = s.sb("w", [P, KC, COLS])
        xrow = s.sb("xrow", [P, GROUP, D_MODEL])
        xT = s.sb("xT", [P, KC, TOKENS])
        raw = s.sb("raw", [P, 3, HEADS, TOKENS])
        zero = s.sb("zero", [P, 3 * HEADS * HALO])
        uT = s.sb("uT", [P, HEADS, TOKENS])
        vn = s.sb("vn", [P, GROUP, QUAD])
        zs = s.sb("zs", [P, GROUP, QUAD])
        mixed = s.sb("mixed", [P, QUAD])
        osgu = s.sb("osgu", [P, GROUP, QUAD])
        stats = s.sb("stats", [P, GROUP, 6])
        mv = s.sb("mv", [P, GROUP, 2])
        var = s.sb("var", [P, GROUP])
        std = s.sb("std", [P, GROUP])
        rstd = s.sb("rstd", [P, GROUP])
        wsp = s.sb("wsp", [P, HEADS, P])
        wspT = s.sb("wspT", [P, HEADS, P])
        bsp = s.sb("bsp", [P, QUAD])
        lng = s.sb("lng", [P, QUAD])
        lnb = s.sb("lnb", [P, QUAD])
        spare = s.sb("spare", [P, 1])
        ps = s.ps("ps", [P, 8, QUAD])

        w_loaded = [s.sem(f"w_loaded{i}") for i in range(3)]
        small_loaded, x_loaded = s.sem("small_loaded"), s.sem("x_loaded")
        wsp_turned, wspT_ready = s.sem("wsp_turned"), s.sem("wspT_ready")
        zero_ready, edges_stored = s.sem("zero_ready"), s.sem("edges_stored")
        raw_stored = [s.sem(f"raw_stored{b}") for b in range(3)]
        z_stored, sgu_stored = s.sem("z_stored"), s.sem("sgu_stored")

        pe = Steps(s.sem("pe_done"), [f"xT{c}" for c in range(KC)] + [f"cm{n}" for n in range(16)]
                   + [f"v{j}" for j in range(GROUP)] + ["gates"] + [f"z{j}" for j in range(GROUP)]
                   + [f"sp{j}" for j in range(GROUP)])
        act = Steps(s.sem("act_done"), [f"xT{c}" for c in range(0, KC, 2)] + [f"raw{n}" for n in range(0, 12, 2)]
                    + [f"u{h}" for h in range(HEADS)] + [f"v{j}" for j in range(GROUP)] + ["std"]
                    + [f"z{j}" for j in range(GROUP)])
        dve = Steps(s.sem("dve_done"), [f"xT{c}" for c in range(1, KC, 2)] + [f"raw{n}" for n in range(1, 12, 2)]
                    + [x for j in range(GROUP) for x in (f"stats{j}", f"mv{j}")] + ["gates", "var", "rstd"]
                    + [f"vn{j}" for j in range(GROUP)] + [x for j in range(GROUP) for x in (f"mixed{j}", f"sgu{j}")])
        pool = Steps(s.sem("pool_done"), [x for j in range(GROUP) for x in (f"g{j}", f"b{j}")])

        def copied(n):
            return act if n % 2 == 0 else dve

        block = stack.enter_context(nc.Block())
        raw_d = d["raw"]
        z_d = d["z"]
        sgu_d = d["sgu"]
        x_d = d["x"].rearrange("b (t p) c -> p (b t) c", p=P)
        w_d = d["w_in"].rearrange("l (k p) c -> p (l k) c", p=P)

        @block.sync
        def _(sp):
            sp.dma_start(xrow[:], x_d[:, 0:GROUP, :]).then_inc(x_loaded, 16)
            sp.dma_start(w[:, :, Q0:Z0], w_d[:, :, Q0:Z0]).then_inc(w_loaded[0], 16)
            sp.dma_start(w[:, :, U0:COLS], w_d[:, :, U0:COLS]).then_inc(w_loaded[1], 16)
            sp.dma_start(w[:, :, Z0:U0], w_d[:, :, Z0:U0]).then_inc(w_loaded[2], 16)

            sp.wait_ge(w_loaded[0], 16)
            met = (w_loaded[0], 16)

            def stores(g):
                for b in range(3):
                    for odd, at in enumerate((act.at(g, f"raw{4 * b + 2}"), dve.at(g, f"raw{4 * b + 3}"))):
                        wait_alone(sp, met, *at)
                        sp.dma_start(raw_d[:, b, odd::2, bass.ds(g * TOKENS + HALO, TOKENS)], raw[:, b, odd::2]).then_inc(raw_stored[b], 16)
                wait_alone(sp, met, *act.at(g, f"z{GROUP - 1}"))
                sp.dma_start(z_d[bass.ds(g * GROUP, GROUP)].rearrange("t p c -> p t c"), zs[:]).then_inc(z_stored, 16)
                wait_alone(sp, met, *dve.at(g, f"sgu{GROUP - 1}"))
                sp.dma_start(sgu_d[bass.ds(g * GROUP, GROUP)].rearrange("t p c -> p t c"), osgu[:]).then_inc(sgu_stored, 16)

            with sp.Fori(0, GROUPS - 1) as g:
                wait_alone(sp, met, *pe.at(g, f"xT{KC - 1}"))
                sp.dma_start(xrow[:], x_d[:, bass.ds(g * GROUP + GROUP, GROUP), :]).then_inc(x_loaded, 16)
                stores(g)
            stores(GROUPS - 1)
            for sem in raw_stored:
                sp.wait_ge(sem, 32 * GROUPS)
            for sem in (z_stored, sgu_stored):
                sp.wait_ge(sem, 16 * GROUPS)

        @block.gpsimd
        def _(gp):
            gp.dma_start(wsp[:], d["w_spatial"].rearrange("l g p q -> p (l g) q")).then_inc(small_loaded, 16)
            gp.dma_start(bsp[:], d["b_spatial"].rearrange("l g p -> l (g p)").partition_broadcast(P)).then_inc(small_loaded, 16)
            gp.dma_start(lng[:], d["sgu_ln_g"].partition_broadcast(P)).then_inc(small_loaded, 16)
            gp.dma_start(lnb[:], d["sgu_ln_b"].partition_broadcast(P)).then_inc(small_loaded, 16)
            gp.memset(zero[:], 0.0).then_inc(zero_ready, 1)
            gp.wait_ge(zero_ready, 1)
            for lo in (0, SEQ + HALO):
                gp.dma_start(raw_d[:, :, :, lo:lo + HALO], zero[:].rearrange("p (b h e) -> p b h e", b=3, h=HEADS)).then_inc(edges_stored, 16)
            pool.start(gp)
            gp.wait_ge(small_loaded, 64)
            with gp.Fori(0, GROUPS) as g:
                for j in range(GROUP):
                    gp.wait_ge(*dve.at(g, f"vn{j}"))
                    gp.tensor_tensor(vn[:, j], vn[:, j], lng[:], ALU.mult).then_inc(*pool.mark(f"g{j}"))
                    gp.wait_ge(*pool.at(g, f"g{j}"))
                    gp.tensor_tensor(vn[:, j], vn[:, j], lnb[:], ALU.add).then_inc(*pool.mark(f"b{j}"))
            gp.wait_ge(edges_stored, 32)

        @block.tensor
        def _(te):
            te.wait_ge(small_loaded, 64)
            for h in range(HEADS):
                m = te.transpose(ps[:, 7, h * P:(h + 1) * P], wsp[:, h], ident[:])
            m.then_inc(wsp_turned, 1)
            te.wait_ge(wspT_ready, 1)
            pe.start(te)
            with te.Fori(0, GROUPS) as g:
                te.wait_ge(x_loaded, g * 16 + 16)
                te.wait_ge(*act.at(g - 1, f"z{GROUP - 1}"))
                te.wait_ge(*dve.at(g - 1, f"mixed{GROUP - 1}"))
                for c in range(KC):
                    for j in range(GROUP):
                        m = te.transpose(ps[:, c, j * P:(j + 1) * P], xrow[:, j, c * P:(c + 1) * P], ident[:])
                    m.then_inc(*pe.mark(f"xT{c}"))
                te.wait_ge(*act.at(g, f"xT{KC - 2}"))
                te.wait_ge(*dve.at(g, f"xT{KC - 1}"))
                te.wait_ge(w_loaded[0], 16)
                for n in range(16):
                    if n >= 8:
                        te.wait_ge(*copied(n - 8).at(g, f"raw{n - 8}"))
                    if n == 12:
                        te.wait_ge(w_loaded[1], 16)
                    col = Q0 + n * P if n < 12 else U0 + (n - 12) * P
                    for k in range(KC):
                        m = te.matmul(ps[:, n % 8], w[:, k, col:col + P], xT[:, k], start=(k == 0), stop=(k == KC - 1))
                    m.then_inc(*pe.mark(f"cm{n}"))

                def by_token(bank, j, col, width, at):
                    for k in range(KC):
                        m = te.matmul(ps[:, bank, at:at + width], xT[:, k, j * P:(j + 1) * P], w[:, k, col:col + width],
                                      start=(k == 0), stop=(k == KC - 1))
                    return m

                for j in range(GROUP):
                    te.wait_ge(*copied(8 + j).at(g, f"raw{8 + j}"))
                    by_token(j, j, V0, QUAD, 0).then_inc(*pe.mark(f"v{j}"))
                te.wait_ge(w_loaded[2], 16)
                te.wait_ge(*act.at(g, "v0"))
                for j in range(GROUP):
                    m = by_token(0, j, G0, 16, 16 * j)
                m.then_inc(*pe.mark("gates"))
                for j in range(GROUP):
                    te.wait_ge(*act.at(g, f"u{j}"))
                    by_token(4 + j, j, Z0, QUAD, 0).then_inc(*pe.mark(f"z{j}"))
                for j in range(GROUP):
                    te.wait_ge(*(act.at(g, f"v{j + 1}") if j < 3 else act.at(g, "z0")))
                    te.wait_ge(*pool.at(g, f"b{j}"))
                    for h in range(HEADS):
                        m = te.matmul(ps[:, 1 + j, h * P:(h + 1) * P], vn[:, j, h * P:(h + 1) * P], wspT[:, h],
                                      start=True, stop=True)
                    m.then_inc(*pe.mark(f"sp{j}"))

        @block.scalar
        def _(sc):
            act.start(sc)
            with sc.Fori(0, GROUPS) as g:
                for c in range(0, KC, 2):
                    sc.wait_ge(*pe.at(g, f"xT{c}"))
                    sc.activation(xT[:, c], ps[:, c], ACT.Copy).then_inc(*act.mark(f"xT{c}"))
                for n in range(0, 12, 2):
                    if n % 4 == 0:
                        sc.wait_ge(raw_stored[n // 4], g * 32)
                    sc.wait_ge(*pe.at(g, f"cm{n}"))
                    sc.activation(raw[:, n // 4, n % 4], ps[:, n % 8], ACT.Copy).then_inc(*act.mark(f"raw{n}"))
                sc.wait_ge(*dve.at(g - 1, f"sgu{GROUP - 1}"))
                for h in range(HEADS):
                    sc.wait_ge(*pe.at(g, f"cm{12 + h}"))
                    sc.activation(uT[:, h], ps[:, 4 + h], ACT.Gelu).then_inc(*act.mark(f"u{h}"))
                for j in range(GROUP):
                    sc.wait_ge(*pe.at(g, f"v{j}"))
                    sc.activation(vn[:, j], ps[:, j], ACT.Gelu).then_inc(*act.mark(f"v{j}"))
                sc.wait_ge(*dve.at(g, "var"))
                sc.activation(std[:], var[:], ACT.Sqrt).then_inc(*act.mark("std"))
                sc.wait_ge(z_stored, g * 16)
                for j in range(GROUP):
                    sc.wait_ge(*pe.at(g, f"z{j}"))
                    sc.activation(zs[:, j], ps[:, 4 + j], ACT.Silu).then_inc(*act.mark(f"z{j}"))

        @block.vector
        def _(ve):
            ve.wait_ge(wsp_turned, 1)
            ve.tensor_copy(wspT[:], ps[:, 7].rearrange("p (h m) -> p h m", h=HEADS)).then_inc(wspT_ready, 1)
            ve.wait_ge(small_loaded, 64)
            dve.start(ve)
            with ve.Fori(0, GROUPS) as g:
                for c in range(1, KC, 2):
                    ve.wait_ge(*pe.at(g, f"xT{c}"))
                    ve.tensor_copy(xT[:, c], ps[:, c]).then_inc(*dve.mark(f"xT{c}"))
                for n in range(1, 12, 2):
                    if n % 4 == 1:
                        ve.wait_ge(raw_stored[n // 4], g * 32)
                    ve.wait_ge(*pe.at(g, f"cm{n}"))
                    ve.tensor_copy(raw[:, n // 4, n % 4], ps[:, n % 8]).then_inc(*dve.mark(f"raw{n}"))
                for j in range(GROUP):
                    ve.wait_ge(*act.at(g, f"v{j}"))
                    ve.bn_stats(stats[:, j], vn[:, j]).then_inc(*dve.mark(f"stats{j}"))
                    ve.wait_ge(*dve.at(g, f"stats{j}"))
                    ve.memset(spare[:], 0.0)
                    ve.bn_aggr(mv[:, j], stats[:, j]).then_inc(*dve.mark(f"mv{j}"))
                ve.wait_ge(*pe.at(g, "gates"))
                ve.tensor_copy(graw[:, bass.ds(g * GROUP, GROUP)], ps[:, 0, 0:16 * GROUP].rearrange("p (j c) -> p j c", j=GROUP)).then_inc(*dve.mark("gates"))
                ve.wait_ge(*dve.at(g, f"mv{GROUP - 1}"))
                ve.tensor_scalar(var[:], mv[:, :, 1], LN_EPS, None, ALU.add).then_inc(*dve.mark("var"))
                ve.wait_ge(*act.at(g, "std"))
                ve.reciprocal(rstd[:], std[:]).then_inc(*dve.mark("rstd"))
                ve.wait_ge(*dve.at(g, "rstd"))
                for j in range(GROUP):
                    ve.tensor_scalar(vn[:, j], vn[:, j], mv[:, j, 0:1], rstd[:, j:j + 1], ALU.subtract, ALU.mult).then_inc(*dve.mark(f"vn{j}"))
                ve.wait_ge(sgu_stored, g * 16)
                for j in range(GROUP):
                    ve.wait_ge(*pe.at(g, f"sp{j}"))
                    if j:
                        ve.wait_ge(*dve.at(g, f"sgu{j - 1}"))
                    else:
                        ve.wait_ge(*dve.at(g - 1, f"sgu{GROUP - 1}"))
                    ve.tensor_tensor(mixed[:], ps[:, 1 + j], bsp[:], ALU.add).then_inc(*dve.mark(f"mixed{j}"))
                    ve.wait_ge(*dve.at(g, f"mixed{j}"))
                    ve.tensor_tensor(heads(osgu[:, j]), heads(mixed[:]), uT[:, :, j * P:(j + 1) * P], ALU.mult).then_inc(*dve.mark(f"sgu{j}"))


def gates_and_conv(nc, d, ident, graw, GS):
    with ExitStack() as stack:
        s = Scope(nc, stack, "b_")
        NG = TILES * CHAINS
        dtb, alog, nea = s.sb("dtb", [P, CHAINS]), s.sb("alog", [P, CHAINS]), s.sb("nea", [P, CHAINS])
        a1, ab, e1, u1, d1, c1, r1, l1 = (s.sb(n, [P, TILES, CHAINS]) for n in ("a1", "ab", "e1", "u1", "d1", "c1", "r1", "l1"))
        g, eb, ub, beta = (s.sb(n, [P, TILES, CHAINS]) for n in ("g", "eb", "ub", "beta"))
        gcC, diff, gT = s.sb("gcC", [P, TILES, CHAINS]), s.sb("diff", [P, TILES, CHAINS]), s.sb("gT", [P, P])
        tri_le, tri_ge, ones = s.sb("tri_le", [P, P]), s.sb("tri_ge", [P, P]), s.sb("ones", [P, P])
        cwT, cw = s.sb("cwT", [TAPS * 12, P]), s.sb("cw", [P, TAPS, 12])
        diag = s.sb("diag", [P, 8, TAPS, P])
        rawin = s.sb("rawin", [P, 12, TOKENS + 2 * HALO])
        acc = s.sb("acc", [P, HEADS, TOKENS])
        sil = s.sb("sil", [P, 12, TOKENS])
        sq = s.sb("sq", [P, 8, TOKENS])
        ss, nrm, rn = (s.sb(n, [P, 2, GROUP, HEADS]) for n in ("ss", "nrm", "rn"))
        qt = s.sb("qt", [P, GROUP, QUAD])
        pk = s.sb("pk", [P, GROUP, 4, QUAD])
        ps = s.ps("ps", [P, 8, QUAD])

        loaded, cw_loaded, raw_loaded, packed_stored, gT_stored = (s.sem(n) for n in ("loaded", "cw_loaded", "raw_loaded", "packed_stored", "gT_stored"))
        shapes, sums, act_gate, dve_gate = s.sem("shapes"), s.sem("sums"), s.sem("act_gate"), s.sem("dve_gate")
        conv_turned, conv_ready, diag_ready = s.sem("conv_turned"), s.sem("conv_ready"), s.sem("diag_ready")

        turns = [f"v{j}" for j in range(GROUP)] + [f"{x}{j}" for j in range(GROUP) for x in "qk"] + [f"{x}{j}" for j in range(GROUP) for x in "QK"]
        banks = [5, 6, 7, 0, 1, 2, 3]
        pe = Steps(s.sem("pe_done"), [f"cv{n}" for n in range(8)] + ["ss"] + turns)
        act = Steps(s.sem("act_done"), [f"silu{n}" for n in range(12)] + ["nrm"] + [f"v{j}" for j in range(GROUP)] + [f"Q{j}" for j in range(GROUP)])
        dve = Steps(s.sem("dve_done"), [f"cv{n}.{t}" for n in range(8, 12) for t in range(TAPS)] + ["ss", "rn", "rq"]
                    + [f"{x}{j}" for j in range(GROUP) for x in "qk"] + [f"K{j}" for j in range(GROUP)])
        pool = Steps(s.sem("pool_done"), [f"sq{n}" for n in range(8)])

        def copied(job):
            return act if job[0] in "vQ" else dve

        block = stack.enter_context(nc.Block())
        raw_d = d["raw"].rearrange("p b h t -> p (b h) t")
        pk_d = d["pk"]
        gb_d = d["gb"]

        @block.sync
        def _(sp):
            sp.dma_start(dtb[:, 0:HEADS], d["dt_bias_f"].partition_broadcast(P)).then_inc(loaded, 16)
            sp.dma_start(dtb[:, HEADS:], d["dt_bias_b"].partition_broadcast(P)).then_inc(loaded, 16)
            sp.dma_start(alog[:, 0:HEADS], d["a_log_f"].partition_broadcast(P)).then_inc(loaded, 16)
            sp.dma_start(alog[:, HEADS:], d["a_log_b"].partition_broadcast(P)).then_inc(loaded, 16)
            sp.wait_ge(loaded, 64)
            sp.dma_start(cwT[:], d["conv_w"].rearrange("l t (n p) -> (l t n) p", p=P)).then_inc(cw_loaded, 16)
            sp.wait_ge(dve_gate, 19)
            sp.dma_start(gb_d, gT[:]).then_inc(gT_stored, 16)
            sp.wait_ge(gT_stored, 16)
            with sp.Fori(0, GROUPS) as gi:
                wait_alone(sp, (loaded, 64), *pe.at(gi - 1, "cv7"))
                wait_alone(sp, (loaded, 64), *dve.at(gi - 1, f"cv11.{TAPS - 1}"))
                sp.dma_start(rawin[:], raw_d[:, :, bass.ds(gi * TOKENS, TOKENS + 2 * HALO)]).then_inc(raw_loaded, 16)

        @block.gpsimd
        def _(gp):
            gp.memset(ones[:], 1.0).then_inc(shapes, 1)
            gp.wait_ge(shapes, 1)
            gp.affine_select(out=tri_le[:], in_=ones[:], pattern=[[1, P]], compare_op=ALU.is_ge, fill=0.0, base=0, channel_multiplier=-1).then_inc(shapes, 1)
            gp.affine_select(out=tri_ge[:], in_=ones[:], pattern=[[-1, P]], compare_op=ALU.is_ge, fill=0.0, base=0, channel_multiplier=1).then_inc(shapes, 1)
            pool.start(gp)
            with gp.Fori(0, GROUPS) as gi:
                gp.wait_ge(*pe.at(gi - 1, "ss"))
                for n in range(8):
                    gp.wait_ge(*act.at(gi, f"silu{n}"))
                    gp.tensor_tensor(sq[:, n], sil[:, n], sil[:, n], ALU.mult).then_inc(*pool.mark(f"sq{n}"))


        @block.tensor
        def _(te):
            te.wait_ge(cw_loaded, 16)
            te.transpose(ps[:, 1, 0:TAPS * 12], cwT[:], ident[0:TAPS * 12, 0:TAPS * 12]).then_inc(conv_turned, 1)
            te.wait_ge(shapes, 3)
            te.wait_ge(dve_gate, 12)
            te.matmul(ps[:, 0, 0:NG // 2], tri_le[:], g[:, :, 0:HEADS], start=True, stop=True)
            te.matmul(ps[:, 0, NG // 2:NG], tri_ge[:], g[:, :, HEADS:], start=True, stop=True)
            te.matmul(ps[:, 0, NG:2 * NG], ones[:], g[:], start=True, stop=True).then_inc(sums, 1)
            te.wait_ge(dve_gate, 16)
            te.transpose(ps[:, 2, 0:P], gcC[:].rearrange("p t c -> p (t c)"), ident[:]).then_inc(sums, 1)
            te.wait_ge(dve_gate, 19)
            te.wait_ge(diag_ready, 8 * TAPS)
            pe.start(te)
            with te.Fori(0, GROUPS) as gi:
                te.wait_ge(raw_loaded, gi * 16 + 16)
                te.wait_ge(*act.at(gi - 1, f"Q{GROUP - 1}"))
                te.wait_ge(*dve.at(gi - 1, f"K{GROUP - 1}"))
                for n in range(8):
                    if n >= 4:
                        te.wait_ge(*act.at(gi, f"silu{n - 4}"))
                    for t in range(TAPS):
                        m = te.matmul(ps[:, n % 4], diag[:, n, t], rawin[:, n, t:t + TOKENS], start=(t == 0), stop=(t == TAPS - 1))
                    m.then_inc(*pe.mark(f"cv{n}"))
                te.wait_ge(*pool.at(gi, "sq7"))
                for n in range(8):
                    for j in range(GROUP):
                        at = (n // 4) * 16 + j * HEADS + n % 4
                        m = te.matmul(ps[:, 4, at:at + 1], sq[:, n, j * P:(j + 1) * P], ones[:, 0:1], start=True, stop=True)
                m.then_inc(*pe.mark("ss"))
                for i, job in enumerate(turns):
                    kind, j = job[0], int(job[1])
                    if i >= len(banks):
                        last = turns[i - len(banks)]
                        te.wait_ge(*copied(last).at(gi, last))
                    elif banks[i] < 4:
                        te.wait_ge(*act.at(gi, f"silu{4 + banks[i]}"))
                    if i == 0:
                        te.wait_ge(*act.at(gi, "silu11"))
                    if kind in "QK":
                        te.wait_ge(*dve.at(gi, kind.lower() + job[1]))
                        src = [(qt if kind == "Q" else pk[:, :, 2])[:, j, h * P:(h + 1) * P] for h in range(HEADS)]
                    else:
                        base = "qkv".index(kind) * HEADS
                        src = [sil[:, base + h, j * P:(j + 1) * P] for h in range(HEADS)]
                    for h in range(HEADS):
                        m = te.transpose(ps[:, banks[i % len(banks)], h * P:(h + 1) * P], src[h], ident[:])
                    m.then_inc(*pe.mark(job))

        @block.scalar
        def _(sc):
            sc.wait_ge(loaded, 64)
            sc.activation(nea[:], alog[:], ACT.Exp).then_inc(act_gate, 1)
            sc.activation(eb[:], graw[:, :, CHAINS:], ACT.Exp, scale=-1.0).then_inc(act_gate, 1)
            sc.wait_ge(dve_gate, 2)
            sc.activation(e1[:], ab[:], ACT.Exp, scale=-1.0).then_inc(act_gate, 1)
            sc.wait_ge(dve_gate, 3)
            sc.activation(l1[:], u1[:], ACT.Ln).then_inc(act_gate, 1)
            sc.wait_ge(dve_gate, 17)
            sc.activation(GS[:, :, EG], gcC[:], ACT.Exp).then_inc(act_gate, 1)
            sc.activation(GS[:, :, KD], diff[:], ACT.Exp).then_inc(act_gate, 1)
            sc.activation(GS[:, :, EL], ps[:, 0, NG:2 * NG].rearrange("p (t c) -> p t c", c=CHAINS), ACT.Exp).then_inc(act_gate, 1)
            act.start(sc)
            with sc.Fori(0, GROUPS) as gi:
                for n in range(12):
                    if n < 8:
                        sc.wait_ge(*pe.at(gi, f"cv{n}"))
                        sc.activation(sil[:, n], ps[:, n % 4], ACT.Silu).then_inc(*act.mark(f"silu{n}"))
                    else:
                        sc.wait_ge(*dve.at(gi, f"cv{n}.{TAPS - 1}"))
                        sc.activation(sil[:, n], acc[:, n - 8], ACT.Silu).then_inc(*act.mark(f"silu{n}"))
                sc.wait_ge(*dve.at(gi, "ss"))
                sc.activation(nrm[:], ss[:], ACT.Sqrt).then_inc(*act.mark("nrm"))
                sc.wait_ge(packed_stored, gi * 16)
                for j in range(GROUP):
                    sc.wait_ge(*pe.at(gi, f"v{j}"))
                    sc.activation(pk[:, j, 3], ps[:, banks[j]], ACT.Copy).then_inc(*act.mark(f"v{j}"))
                for j in range(GROUP):
                    sc.wait_ge(*pe.at(gi, f"Q{j}"))
                    sc.activation(pk[:, j, 1], ps[:, banks[turns.index(f"Q{j}") % len(banks)]], ACT.Copy).then_inc(*act.mark(f"Q{j}"))
                wait_alone(sc, (loaded, 64), *act.at(gi, f"Q{GROUP - 1}"))
                wait_alone(sc, (loaded, 64), *dve.at(gi, f"K{GROUP - 1}"))
                sc.dma_start(pk_d[bass.ds(gi * GROUP, GROUP)].rearrange("t p k c -> p t k c"), pk[:]).then_inc(packed_stored, 16)
            sc.wait_ge(packed_stored, 16 * GROUPS)

        @block.vector
        def _(ve):
            count = [0]

            def gate(ins):
                count[0] += 1
                ins.then_inc(dve_gate, 1)
                ve.wait_ge(dve_gate, count[0])

            ve.wait_ge(loaded, 64)
            over_tiles = lambda ap: over_heads(ap, TILES)
            gate(ve.tensor_tensor(a1[:], graw[:, :, 0:CHAINS], over_tiles(dtb[:]), ALU.add))
            gate(ve.scalar_tensor_tensor(out=ab[:], in0=a1[:], scalar=-1.0, in1=a1[:], op0=ALU.mult, op1=ALU.max))
            ve.wait_ge(act_gate, 3)
            gate(ve.tensor_scalar(u1[:], e1[:], 1.0, None, ALU.add))
            gate(ve.tensor_scalar(d1[:], u1[:], -1.0, None, ALU.add))
            gate(ve.tensor_tensor(c1[:], e1[:], d1[:], ALU.subtract))
            gate(ve.reciprocal(r1[:], u1[:]))
            gate(ve.tensor_tensor(c1[:], c1[:], r1[:], ALU.mult))
            ve.wait_ge(act_gate, 4)
            gate(ve.tensor_tensor(l1[:], l1[:], c1[:], ALU.add))
            gate(ve.tensor_scalar(a1[:], a1[:], 0.0, None, ALU.max))
            gate(ve.tensor_tensor(a1[:], a1[:], l1[:], ALU.add))
            gate(ve.tensor_scalar(nea[:], nea[:], -1.0, None, ALU.mult))
            gate(ve.tensor_tensor(g[:], a1[:], over_tiles(nea[:]), ALU.mult))
            gate(ve.tensor_scalar(ub[:], eb[:], 1.0, None, ALU.add))
            gate(ve.reciprocal(beta[:], ub[:]))
            gate(ve.tensor_copy(GS[:, :, BETA], beta[:]))
            ve.wait_ge(sums, 1)
            ve.tensor_copy(gcC[:, :, 0:HEADS], ps[:, 0, 0:NG // 2].rearrange("p (t c) -> p t c", c=HEADS))
            gate(ve.tensor_copy(gcC[:, :, HEADS:], ps[:, 0, NG // 2:NG].rearrange("p (t c) -> p t c", c=HEADS)))
            gate(ve.tensor_tensor(diff[:], ps[:, 0, NG:2 * NG].rearrange("p (t c) -> p t c", c=CHAINS), gcC[:], ALU.subtract))
            gate(ve.tensor_copy(GS[:, :, GC], gcC[:]))
            ve.wait_ge(sums, 2)
            gate(ve.tensor_copy(gT[:], ps[:, 2, 0:P]))
            ve.wait_ge(act_gate, 7)
            gate(ve.scalar_tensor_tensor(out=GS[:, :, NBE], in0=beta[:], scalar=-1.0, in1=GS[:, :, EG], op0=ALU.mult, op1=ALU.mult))
            ve.wait_ge(conv_turned, 1)
            ve.tensor_copy(cw[:], ps[:, 1, 0:TAPS * 12].rearrange("p (t n) -> p t n", n=12)).then_inc(conv_ready, 1)
            ve.wait_ge(conv_ready, 1)
            for n in range(8):
                for t in range(TAPS):
                    ve.tensor_scalar(diag[:, n, t], ident[:], cw[:, t, n:n + 1], None, ALU.mult).then_inc(diag_ready, 1)
            dve.start(ve)
            with ve.Fori(0, GROUPS) as gi:
                ve.wait_ge(raw_loaded, gi * 16 + 16)
                for n in range(8, 12):
                    for t in range(TAPS):
                        if t == 0:
                            ve.tensor_scalar(acc[:, n - 8], rawin[:, n, 0:TOKENS], cw[:, 0, n:n + 1], None, ALU.mult).then_inc(*dve.mark(f"cv{n}.0"))
                        else:
                            ve.wait_ge(*dve.at(gi, f"cv{n}.{t - 1}"))
                            ve.scalar_tensor_tensor(out=acc[:, n - 8], in0=rawin[:, n, t:t + TOKENS], scalar=cw[:, t, n:n + 1],
                                                    in1=acc[:, n - 8], op0=ALU.mult, op1=ALU.add).then_inc(*dve.mark(f"cv{n}.{t}"))
                ve.wait_ge(*pe.at(gi, "ss"))
                ve.tensor_scalar(ss[:], ps[:, 4, 0:32].rearrange("p (b j h) -> p b j h", b=2, j=GROUP), L2_EPS, None, ALU.add).then_inc(*dve.mark("ss"))
                ve.wait_ge(*act.at(gi, "nrm"))
                ve.reciprocal(rn[:], nrm[:]).then_inc(*dve.mark("rn"))
                ve.wait_ge(*dve.at(gi, "rn"))
                ve.tensor_scalar(rn[:, 0], rn[:, 0], float(P) ** -0.5, None, ALU.mult).then_inc(*dve.mark("rq"))
                ve.wait_ge(*dve.at(gi, "rq"))
                ve.wait_ge(packed_stored, gi * 16)
                for j in range(GROUP):
                    for b, kind in enumerate("qk"):
                        ve.wait_ge(*pe.at(gi, f"{kind}{j}"))
                        bank = banks[turns.index(f"{kind}{j}") % len(banks)]
                        ve.tensor_tensor(heads(qt[:, j] if b == 0 else pk[:, j, 2]), heads(ps[:, bank]), bcast(rn[:, b, j], P), ALU.mult).then_inc(*dve.mark(f"{kind}{j}"))
                for j in range(GROUP):
                    ve.wait_ge(*pe.at(gi, f"K{j}"))
                    ve.tensor_copy(pk[:, j, 0], ps[:, banks[turns.index(f"K{j}") % len(banks)]]).then_inc(*dve.mark(f"K{j}"))


MASK_OPS = 4 * 7 + 8
LEVELS = 7


def delta(nc, d, ident, GS, outs):
    with ExitStack() as stack:
        s = Scope(nc, stack, "d_")
        D2 = range(2)
        inp = [[s.sb(f"in{c}{b}", [P, 4, QUAD]) for b in D2] for c in D2]
        gb = [[s.sb(f"gb{c}{b}", [P, QUAD]) for b in D2] for c in D2]
        per = lambda name, shape=(P, QUAD): [s.sb(f"{name}{c}", list(shape)) for c in D2]
        sc_ = per("sc", (P, KINDS, HEADS))
        tmp1, tmp2, A, QK = per("tmp1"), per("tmp2"), per("A"), per("QK")
        AL = per("AL", (P, LEVELS, QUAD))
        T, Tt, Pm = per("T"), per("Tt"), per("Pm")
        kbe, vb, kd, wT, vn, qv, S = per("kbe"), per("vb"), per("kd"), per("wT"), per("vn"), per("qv"), per("S")
        M = [s.sb(f"M{c}", [P, LEVELS, P]) for c in D2]
        far = [s.sb(f"far{c}", [P, P]) for c in D2]
        rowi, coli = s.sb("rowi", [P, 1], I32), s.sb("coli", [P, P], I32)
        shr, bit = s.sb("shr", [P, LEVELS], I32), s.sb("bit", [P, LEVELS], I32)
        shrf, bitf = s.sb("shrf", [P, LEVELS]), s.sb("bitf", [P, LEVELS])
        shc, shcf = AL[0][:, :, 0:P].bitcast(I32), AL[1][:, :, 0:P]
        side, keep = s.sb("side", [P, 2, LEVELS]), s.sb("keep", [P, 2, LEVELS])
        ps = s.ps("ps", [P, 8, QUAD])

        loaded = [[s.sem(f"loaded{c}{b}") for b in D2] for c in D2]
        iotas, masks, far_ready, s_zero = s.sem("iotas"), s.sem("masks"), s.sem("far_ready"), s.sem("s_zero")
        H4 = range(HEADS)
        L = range(1, LEVELS)
        pe = Steps(s.sem("pe_done"), [f"{x}{c}" for x in ("G", "KQ", "Tt0.") for c in D2]
                   + [f"{x}{l}.{c}" for l in L for x in (("P", "X", "T") if l < LEVELS - 1 else ("P", "X")) for c in D2]
                   + [f"{x}{c}" for x in ("wT", "U", "qS", "QV", "S") for c in D2])
        act = Steps(s.sem("act_done"), [f"{x}{c}" for c in D2 for x in ("E1.", "E2.")] + [f"Tt0.{c}" for c in D2]
                    + [f"{x}{l}.{c}" for l in L for x in (("P", "T") if l < LEVELS - 1 else ("P",)) for c in D2]
                    + [f"{x}{c}" for x in ("wT", "vn", "qv") for c in D2])
        dve = Steps(s.sem("dve_done"), [f"sc{c}" for c in D2] + [f"{x}{c}.{h}" for c in D2 for x in ("tmp1.", "tmp2.") for h in H4]
                    + [f"A{c}.{h}" for c in D2 for h in H4] + [f"QK{c}" for c in D2] + [f"T0.{c}" for c in D2]
                    + [f"X{l}.{c}" for l in L for c in D2] + [f"S{c}.{h}" for c in D2 for h in H4] + [f"o{c}.{h}" for c in D2 for h in H4])
        pool = Steps(s.sem("pool_done"), [f"{x}{c}" for c in D2 for x in ("kbe", "vb", "kd")] + [f"AL{l}.{c}" for l in range(LEVELS) for c in D2])

        block = stack.enter_context(nc.Block())
        pk_d, gb_d = d["pk"], d["gb"].rearrange("(t c h) i -> t c (h i)", c=2, h=HEADS)
        chunk = lambda c, t: t if c == 0 else TILES - 1 - t
        col = lambda h: slice(h * P, (h + 1) * P)

        @block.sync
        def _(sp):
            def load(t, b):
                for c in D2:
                    sp.dma_start(inp[c][b][:], pk_d[bass.ds(chunk(c, t), 1)].rearrange("t p k c -> p (t k) c")).then_inc(loaded[c][b], 16)
                    sp.dma_start(gb[c][b][:], gb_d[bass.ds(chunk(c, t), 1), c].partition_broadcast(P)).then_inc(loaded[c][b], 16)

            load(0, 0)
            load(1, 1)
            sp.wait_ge(loaded[0][0], 32)
            with sp.Fori(1, TILES // 2) as i:
                for b in D2:
                    wait_alone(sp, (loaded[0][0], 32), *pe.at(2 * i + b - 2, "S1"))
                    load(2 * i + b, b)

        @block.gpsimd
        def _(gp):
            gp.iota(rowi[:], pattern=[[0, 1]], base=0, channel_multiplier=1).then_inc(iotas, 1)
            gp.iota(coli[:], pattern=[[1, P]], base=0, channel_multiplier=0).then_inc(iotas, 1)
            gp.memset(far[0][:], 0.0).then_inc(iotas, 1)
            gp.memset(far[1][:], 0.0).then_inc(iotas, 1)
            gp.wait_ge(iotas, 4)
            gp.affine_select(out=far[0][:], in_=far[0][:], pattern=[[-1, P]], compare_op=ALU.is_ge, fill=BIG, base=0, channel_multiplier=1).then_inc(far_ready, 1)
            gp.affine_select(out=far[1][:], in_=far[1][:], pattern=[[1, P]], compare_op=ALU.is_ge, fill=BIG, base=0, channel_multiplier=-1).then_inc(far_ready, 1)
            gp.wait_ge(masks, MASK_OPS)
            pool.start(gp)
            with gp.Fori(0, TILES // 2) as i:
                for b in D2:
                    t = 2 * i + b
                    gp.wait_ge(*pe.at(t - 1, "S1"))
                    for c in D2:
                        gp.wait_ge(*dve.at(t, f"sc{c}"))
                        gp.wait_ge(loaded[c][b], 32 * i + 32)
                        for name, out, kind, by in (("kbe", kbe, 2, NBE), ("vb", vb, 3, BETA), ("kd", kd, 2, KD)):
                            gp.tensor_tensor(heads(out[c][:]), heads(inp[c][b][:, kind]), bcast(sc_[c][:, by], P), ALU.mult).then_inc(*pool.mark(f"{name}{c}"))
                    for l in range(LEVELS):
                        for c in D2:
                            if l == 0:
                                gp.wait_ge(*dve.at(t, f"A{c}.{HEADS - 1}"))
                            gp.tensor_tensor(heads(AL[c][:, l]), heads(A[c][:]), over_heads(M[c][:, l]), ALU.mult).then_inc(*pool.mark(f"AL{l}.{c}"))

        @block.tensor
        def _(te):
            pe.start(te)
            te.wait_ge(s_zero, 2)
            with te.Fori(0, TILES // 2) as i:
                for b in D2:
                    t = 2 * i + b

                    def quad(c, bank, name, lhsT, rhs):
                        for h in H4:
                            m = te.matmul(ps[:, 4 * c + bank, col(h)], lhsT[:, col(h)], rhs[:, col(h)], start=True, stop=True)
                        m.then_inc(*pe.mark(name))

                    def turn(c, name, src):
                        for h in H4:
                            m = te.transpose(ps[:, 4 * c + 2, col(h)], src[:, col(h)], ident[:])
                        m.then_inc(*pe.mark(name))

                    for c in D2:
                        te.wait_ge(loaded[c][b], 32 * i + 32)
                        te.wait_ge(*act.at(t - 1, f"vn{c}"))
                        quad(c, 0, f"G{c}", inp[c][b][:, 0], inp[c][b][:, 0])
                    for c in D2:
                        te.wait_ge(*act.at(t - 1, f"qv{c}"))
                        quad(c, 1, f"KQ{c}", inp[c][b][:, 0], inp[c][b][:, 1])
                    for c in D2:
                        te.wait_ge(*dve.at(t - 1, f"S{c}.3"))
                        te.wait_ge(*dve.at(t, f"T0.{c}"))
                        turn(c, f"Tt0.{c}", T[c])
                    for l in L:
                        for c in D2:
                            te.wait_ge(*act.at(t, f"Tt0.{c}" if l == 1 else f"T{l - 1}.{c}"))
                            te.wait_ge(*pool.at(t, f"AL{l}.{c}"))
                            quad(c, 0, f"P{l}.{c}", AL[c][:, l], Tt[c])
                        for c in D2:
                            te.wait_ge(*act.at(t, f"P{l}.{c}"))
                            if l == 1:
                                te.wait_ge(*dve.at(t, f"QK{c}"))
                            quad(c, 1, f"X{l}.{c}", T[c], Pm[c])
                        if l < LEVELS - 1:
                            for c in D2:
                                te.wait_ge(*dve.at(t, f"X{l}.{c}"))
                                turn(c, f"T{l}.{c}", Tt[c])
                    for c in D2:
                        te.wait_ge(*dve.at(t, f"X{LEVELS - 1}.{c}"))
                        te.wait_ge(*pool.at(t, f"kd{c}"))
                        te.wait_ge(*dve.at(t - 1, f"o{c}.3"))
                        quad(c, 3, f"wT{c}", kbe[c], Tt[c])
                    for c in D2:
                        te.wait_ge(*act.at(t, f"wT{c}"))
                        te.wait_ge(*dve.at(t - 1, f"S{c}.3"))
                        for h in H4:
                            te.matmul(ps[:, 4 * c, col(h)], Tt[c][:, col(h)], vb[c][:, col(h)], start=True, stop=False)
                            m = te.matmul(ps[:, 4 * c, col(h)], wT[c][:, col(h)], S[c][:, col(h)], start=False, stop=True)
                        m.then_inc(*pe.mark(f"U{c}"))
                    for c in D2:
                        quad(c, 3, f"qS{c}", inp[c][b][:, 1], S[c])
                    for c in D2:
                        te.wait_ge(*act.at(t, f"vn{c}"))
                        quad(c, 1, f"QV{c}", QK[c], vn[c])
                    for c in D2:
                        quad(c, 2, f"S{c}", kd[c], vn[c])

        @block.scalar
        def _(sc):
            act.start(sc)
            with sc.Fori(0, TILES // 2) as i:
                for b in D2:
                    t = 2 * i + b
                    for c in D2:
                        sc.wait_ge(*dve.at(t, f"tmp1.{c}.3"))
                        sc.activation(tmp1[c][:], tmp1[c][:], ACT.Exp, scale=-1.0).then_inc(*act.mark(f"E1.{c}"))
                        sc.wait_ge(*dve.at(t, f"tmp2.{c}.3"))
                        sc.activation(tmp2[c][:], tmp2[c][:], ACT.Exp).then_inc(*act.mark(f"E2.{c}"))

                    def copy(c, bank, out, name):
                        sc.wait_ge(*pe.at(t, name))
                        sc.activation(out[:], ps[:, 4 * c + bank], ACT.Copy).then_inc(*act.mark(name))

                    for c in D2:
                        copy(c, 2, Tt[c], f"Tt0.{c}")
                    for l in L:
                        for c in D2:
                            copy(c, 0, Pm[c], f"P{l}.{c}")
                        if l < LEVELS - 1:
                            for c in D2:
                                copy(c, 2, T[c], f"T{l}.{c}")
                    for c in D2:
                        copy(c, 3, wT[c], f"wT{c}")
                    for c in D2:
                        sc.wait_ge(*pe.at(t, f"U{c}"))
                        sc.activation(vn[c][:], ps[:, 4 * c], ACT.Copy).then_inc(*act.mark(f"vn{c}"))
                    for c in D2:
                        sc.wait_ge(*dve.at(t - 1, f"o{c}.3"))
                        sc.wait_ge(*pe.at(t, f"QV{c}"))
                        sc.activation(qv[c][:], ps[:, 4 * c + 1], ACT.Copy).then_inc(*act.mark(f"qv{c}"))

        @block.vector
        def _(ve):
            for c in D2:
                ve.memset(S[c][:], 0.0).then_inc(s_zero, 1)
            ve.wait_ge(iotas, 4)
            n = [0]

            def made(ins, need=True):
                n[0] += 1
                ins.then_inc(masks, 1)
                if need:
                    ve.wait_ge(masks, n[0])

            for l in range(LEVELS):
                made(ve.tensor_scalar(shr[:, l:l + 1], rowi[:], l, None, ALU.logical_shift_right), False)
                made(ve.tensor_scalar(shc[:, l], coli[:], l, None, ALU.logical_shift_right), l == LEVELS - 1)
            made(ve.tensor_scalar(bit[:], shr[:], 1, None, ALU.bitwise_and))
            ve.tensor_copy(bitf[:], bit[:])
            made(ve.tensor_copy(shrf[:], shr[:]), False)
            made(ve.tensor_copy(shcf[:], shc[:]))
            made(ve.tensor_scalar(side[:, 0], shrf[:], -1.0, None, ALU.add), False)
            made(ve.tensor_scalar(side[:, 1], shrf[:], 1.0, None, ALU.add), False)
            ve.tensor_copy(keep[:, 0], bitf[:])
            made(ve.tensor_scalar(keep[:, 1], bitf[:], -1.0, 1.0, ALU.mult, ALU.add))
            for c in D2:
                for l in range(LEVELS):
                    made(ve.tensor_scalar(M[c][:, l], shcf[:, l], side[:, c, l:l + 1], keep[:, c, l:l + 1], ALU.is_equal, ALU.mult), l == LEVELS - 1)
            for c in D2:
                made(ve.tensor_scalar(M[c][:, 0], M[c][:, 0], -1.0, None, ALU.mult), False)
            assert n[0] == MASK_OPS
            ve.wait_ge(far_ready, 2)
            dve.start(ve)
            with ve.Fori(0, TILES // 2) as i:
                for b in D2:
                    t = 2 * i + b
                    for c in D2:
                        if c == 0:
                            ve.wait_ge(*pool.at(t - 1, "kd1"))
                            ve.wait_ge(*dve.at(t - 1, "o1.3"))
                        ve.tensor_copy(sc_[c][:], GS[:, bass.ds(chunk(c, t), 1), :, c * HEADS:(c + 1) * HEADS].rearrange("p t k h -> p (t k) h")).then_inc(*dve.mark(f"sc{c}"))
                    for c in D2:
                        ve.wait_ge(*dve.at(t, f"sc{c}"))
                        ve.wait_ge(loaded[c][b], 32 * i + 32)
                        for x, out, mask, op in (("tmp1.", tmp1, far[c], ALU.add), ("tmp2.", tmp2, far[1 - c], ALU.subtract)):
                            for h in H4:
                                ve.scalar_tensor_tensor(out=out[c][:, col(h)], in0=gb[c][b][:, col(h)], scalar=sc_[c][:, GC, h:h + 1], in1=mask[:],
                                                        op0=ALU.subtract, op1=op).then_inc(*dve.mark(f"{x}{c}.{h}"))
                    for c in D2:
                        ve.wait_ge(*pe.at(t, f"G{c}"))
                        ve.wait_ge(*act.at(t, f"E1.{c}"))
                        for h in H4:
                            ve.scalar_tensor_tensor(out=A[c][:, col(h)], in0=ps[:, 4 * c, col(h)], scalar=sc_[c][:, BETA, h:h + 1], in1=tmp1[c][:, col(h)],
                                                    op0=ALU.mult, op1=ALU.mult).then_inc(*dve.mark(f"A{c}.{h}"))
                    for c in D2:
                        ve.wait_ge(*pe.at(t, f"KQ{c}"))
                        ve.wait_ge(*act.at(t, f"E2.{c}"))
                        ve.tensor_tensor(QK[c][:], ps[:, 4 * c + 1], tmp2[c][:], ALU.mult).then_inc(*dve.mark(f"QK{c}"))
                    for c in D2:
                        ve.wait_ge(*pool.at(t, f"AL0.{c}"))
                        ve.tensor_tensor(heads(T[c][:]), heads(AL[c][:, 0]), over_heads(ident[:]), ALU.add).then_inc(*dve.mark(f"T0.{c}"))
                    for l in L:
                        for c in D2:
                            ve.wait_ge(*pe.at(t, f"X{l}.{c}"))
                            ve.tensor_tensor(Tt[c][:], Tt[c][:], ps[:, 4 * c + 1], ALU.subtract).then_inc(*dve.mark(f"X{l}.{c}"))
                    for c in D2:
                        ve.wait_ge(*pe.at(t, f"S{c}"))
                        for h in H4:
                            ve.scalar_tensor_tensor(out=S[c][:, col(h)], in0=S[c][:, col(h)], scalar=sc_[c][:, EL, h:h + 1], in1=ps[:, 4 * c + 2, col(h)],
                                                    op0=ALU.mult, op1=ALU.add).then_inc(*dve.mark(f"S{c}.{h}"))
                    for c in D2:
                        ve.wait_ge(*act.at(t, f"qv{c}"))
                        for h in H4:
                            ve.scalar_tensor_tensor(out=outs[c][:, bass.ds(chunk(c, t), 1), col(h)].rearrange("p t m -> p (t m)"), in0=ps[:, 4 * c + 3, col(h)],
                                                    scalar=sc_[c][:, EG, h:h + 1], in1=qv[c][:, col(h)], op0=ALU.mult, op1=ALU.add).then_inc(*dve.mark(f"o{c}.{h}"))


def mix(nc, d, ident, outs, logits):
    with ExitStack() as stack:
        s = Scope(nc, stack, "m_")
        w = s.sb("w", [P, KC, D_MODEL])
        wr = s.sb("wr", [P, KC, N_EXPERTS])
        x, z, sgu = s.sb("x", [P, D_MODEL]), s.sb("z", [P, QUAD]), s.sb("sgu", [P, QUAD])
        nw, lng, lnb = s.sb("nw", [P, P]), s.sb("lng", [P, D_MODEL]), s.sb("lnb", [P, D_MODEL])
        osum, sq, zn, oz, oT = (s.sb(n, [P, QUAD]) for n in ("osum", "sq", "zn", "oz", "oT"))
        ss, rms, rr = (s.sb(n, [P, HEADS]) for n in ("ss", "rms", "rr"))
        y, x1, x1T = s.sb("y", [P, D_MODEL]), s.sb("x1", [P, D_MODEL]), s.sb("x1T", [P, D_MODEL])
        stats, mv, var, std, rs = s.sb("stats", [P, 2, 6]), s.sb("mv", [P, 2]), s.sb("var", [P, 1]), s.sb("std", [P, 1]), s.sb("rs", [P, 1])
        spare = s.sb("spare", [P, 1])
        ps = s.ps("ps", [P, 8, QUAD])
        w_loaded, small_loaded = s.sem("w_loaded"), s.sem("small_loaded")
        x_loaded, z_loaded, sgu_loaded, x1_stored = (s.sem(n) for n in ("x_loaded", "z_loaded", "sgu_loaded", "x1_stored"))
        pre_dve = Steps(s.sem("pre_dve"), ["add", "ss", "ms", "rr", "on", "oz"])
        pre_act = Steps(s.sem("pre_act"), ["sq", "rms"])
        pre_pool = Steps(s.sem("pre_pool"), ["zn"])
        pe_y = Steps(s.sem("pe_y"), ["oT", "sgu", "y0", "y1"])
        act_oT = Steps(s.sem("act_oT"), ["oT"])
        post_dve = Steps(s.sem("post_dve"), ["y0", "y1", "st0", "st1", "mv", "ve", "rs", "nm"])
        post_act = Steps(s.sem("post_act"), ["std"])
        post_pool = Steps(s.sem("post_pool"), ["g", "b"])
        pe_r = Steps(s.sem("pe_r"), ["x1T0", "x1T1", "rt"])
        act_r = Steps(s.sem("act_r"), ["x1T0", "x1T1"])
        dve_r = Steps(s.sem("dve_r"), ["lg"])
        block = stack.enter_context(nc.Block())
        x_d = d["x"].rearrange("b (t p) c -> p (b t) c", p=P)
        row = lambda t: bass.ds(t, 1)

        @block.sync
        def _(sp):
            def loads(t):
                wait_alone(sp, (small_loaded, 64), *pre_pool.at(t - 1, "zn"))
                sp.dma_start(z[:], d["z"][row(t)].rearrange("t p c -> p (t c)")).then_inc(z_loaded, 16)
                wait_alone(sp, (small_loaded, 64), *pe_y.at(t - 1, "sgu"))
                sp.dma_start(sgu[:], d["sgu"][row(t)].rearrange("t p c -> p (t c)")).then_inc(sgu_loaded, 16)
                wait_alone(sp, (small_loaded, 64), *post_dve.at(t - 1, "y1"))
                sp.dma_start(x[:], x_d[:, row(t)].rearrange("p t c -> p (t c)")).then_inc(x_loaded, 16)

            def store(t):
                wait_alone(sp, (small_loaded, 64), *post_pool.at(t, "b"))
                sp.dma_start(d["x1"][row(t)].rearrange("t p c -> p (t c)"), x1[:]).then_inc(x1_stored, 16)

            sp.wait_ge(small_loaded, 64)
            loads(0)
            with sp.Fori(1, TILES) as t:
                loads(t)
                store(t - 1)
            store(TILES - 1)
            sp.wait_ge(x1_stored, 16 * TILES)

        @block.gpsimd
        def _(gp):
            gp.dma_start(nw[:], d["delta_norm_w"].partition_broadcast(P)).then_inc(small_loaded, 16)
            gp.dma_start(lng[:], d["ln1_g"].partition_broadcast(P)).then_inc(small_loaded, 16)
            gp.dma_start(lnb[:], d["ln1_b"].partition_broadcast(P)).then_inc(small_loaded, 16)
            gp.dma_start(wr[:], d["w_router"].rearrange("(k p) e -> p k e", p=P)).then_inc(small_loaded, 16)
            gp.dma_start(w[:], d["w_out"].rearrange("l (k p) c -> p (l k) c", p=P)).then_inc(w_loaded, 16)
            for steps in (pre_pool, post_pool):
                steps.start(gp)
            gp.wait_ge(small_loaded, 64)

            def pre(t):
                gp.wait_ge(z_loaded, t * 16 + 16)
                gp.wait_ge(*pre_dve.at(t - 1, "oz"))
                gp.tensor_tensor(heads(zn[:]), heads(z[:]), over_heads(nw[:]), ALU.mult).then_inc(*pre_pool.mark("zn"))

            def post(t):
                gp.wait_ge(*post_dve.at(t, "nm"))
                gp.tensor_tensor(x1[:], x1[:], lng[:], ALU.mult).then_inc(*post_pool.mark("g"))
                gp.wait_ge(*post_pool.at(t, "g"))
                gp.tensor_tensor(x1[:], x1[:], lnb[:], ALU.add).then_inc(*post_pool.mark("b"))

            pre(0)
            with gp.Fori(1, TILES) as t:
                pre(t)
                post(t - 1)
            post(TILES - 1)

        @block.tensor
        def _(te):
            pe_y.start(te)
            pe_r.start(te)
            te.wait_ge(w_loaded, 16)
            te.wait_ge(small_loaded, 64)

            def main(t):
                te.wait_ge(*pre_dve.at(t, "oz"))
                te.wait_ge(*act_oT.at(t - 1, "oT"))
                for h in range(HEADS):
                    m = te.transpose(ps[:, 0, h * P:(h + 1) * P], oz[:, h * P:(h + 1) * P], ident[:])
                m.then_inc(*pe_y.mark("oT"))
                te.wait_ge(sgu_loaded, t * 16 + 16)
                te.wait_ge(*post_dve.at(t - 1, "y1"))
                for half in range(2):
                    for h in range(HEADS):
                        m = te.matmul(ps[:, 1 + half], sgu[:, h * P:(h + 1) * P], w[:, HEADS + h, half * QUAD:(half + 1) * QUAD], start=(h == 0), stop=False)
                m.then_inc(*pe_y.mark("sgu"))
                te.wait_ge(*act_oT.at(t, "oT"))
                for half in range(2):
                    for h in range(HEADS):
                        m = te.matmul(ps[:, 1 + half], oT[:, h * P:(h + 1) * P], w[:, h, half * QUAD:(half + 1) * QUAD], start=False, stop=(h == HEADS - 1))
                    m.then_inc(*pe_y.mark(f"y{half}"))

            def router(t):
                te.wait_ge(*post_pool.at(t, "b"))
                te.wait_ge(*act_r.at(t - 1, "x1T1"))
                for half in range(2):
                    for k in range(4):
                        c = half * 4 + k
                        m = te.transpose(ps[:, 5 + half, k * P:(k + 1) * P], x1[:, c * P:(c + 1) * P], ident[:])
                    m.then_inc(*pe_r.mark(f"x1T{half}"))
                te.wait_ge(*act_r.at(t, "x1T1"))
                te.wait_ge(*dve_r.at(t - 1, "lg"))
                for k in range(KC):
                    m = te.matmul(ps[:, 7, 0:N_EXPERTS], x1T[:, k * P:(k + 1) * P], wr[:, k], start=(k == 0), stop=(k == KC - 1))
                m.then_inc(*pe_r.mark("rt"))

            main(0)
            with te.Fori(1, TILES) as t:
                main(t)
                router(t - 1)
            router(TILES - 1)

        @block.scalar
        def _(sc):
            for steps in (pre_act, act_oT, post_act, act_r):
                steps.start(sc)

            def pre(t):
                sc.wait_ge(*pre_dve.at(t, "add"))
                sc.activation(sq[:], osum[:], ACT.Square).then_inc(*pre_act.mark("sq"))
                sc.wait_ge(*pre_dve.at(t, "ms"))
                sc.activation(rms[:], ss[:], ACT.Sqrt).then_inc(*pre_act.mark("rms"))

            def turned(t):
                sc.wait_ge(*pe_y.at(t, "oT"))
                sc.activation(oT[:], ps[:, 0], ACT.Copy).then_inc(*act_oT.mark("oT"))

            def router(t):
                for half in range(2):
                    sc.wait_ge(*pe_r.at(t, f"x1T{half}"))
                    sc.activation(x1T[:, half * QUAD:(half + 1) * QUAD], ps[:, 5 + half], ACT.Copy).then_inc(*act_r.mark(f"x1T{half}"))

            def post(t):
                sc.wait_ge(*post_dve.at(t, "ve"))
                sc.activation(std[:], var[:], ACT.Sqrt).then_inc(*post_act.mark("std"))

            pre(0)
            turned(0)
            pre(1)
            post(0)
            with sc.Fori(1, TILES - 1) as t:
                turned(t)
                pre(t + 1)
                router(t - 1)
                post(t)
            turned(TILES - 1)
            router(TILES - 2)
            post(TILES - 1)
            router(TILES - 1)

        @block.vector
        def _(ve):
            for steps in (pre_dve, post_dve, dve_r):
                steps.start(ve)
            ve.wait_ge(small_loaded, 64)

            def pre(t):
                ve.wait_ge(*pre_dve.at(t - 1, "oz"))
                ve.wait_ge(*pre_act.at(t - 1, "sq"))
                ve.tensor_tensor(osum[:], outs[0][:, row(t)].rearrange("p t c -> p (t c)"), outs[1][:, row(t)].rearrange("p t c -> p (t c)"), ALU.add).then_inc(*pre_dve.mark("add"))
                ve.wait_ge(*pre_act.at(t, "sq"))
                ve.tensor_reduce(ss[:], heads(sq[:]), AX.X, ALU.add).then_inc(*pre_dve.mark("ss"))
                ve.wait_ge(*pre_dve.at(t, "ss"))
                ve.tensor_scalar(ss[:], ss[:], 1.0 / P, RMS_EPS, ALU.mult, ALU.add).then_inc(*pre_dve.mark("ms"))
                ve.wait_ge(*pre_act.at(t, "rms"))
                ve.reciprocal(rr[:], rms[:]).then_inc(*pre_dve.mark("rr"))
                ve.wait_ge(*pre_dve.at(t, "rr"))
                ve.tensor_tensor(heads(osum[:]), heads(osum[:]), bcast(rr[:], P), ALU.mult).then_inc(*pre_dve.mark("on"))
                ve.wait_ge(*pre_dve.at(t, "on"))
                ve.wait_ge(*pre_pool.at(t, "zn"))
                ve.wait_ge(*pe_y.at(t - 1, "oT"))
                ve.tensor_tensor(oz[:], osum[:], zn[:], ALU.mult).then_inc(*pre_dve.mark("oz"))

            def post(t):
                ve.wait_ge(x_loaded, t * 16 + 16)
                ve.wait_ge(*post_dve.at(t - 1, "nm"))
                for half in range(2):
                    cols = slice(half * QUAD, (half + 1) * QUAD)
                    ve.wait_ge(*pe_y.at(t, f"y{half}"))
                    ve.scalar_tensor_tensor(out=y[:, cols], in0=x[:, cols], scalar=ALPHA, in1=ps[:, 1 + half], op0=ALU.mult, op1=ALU.add).then_inc(*post_dve.mark(f"y{half}"))
                for half in range(2):
                    ve.wait_ge(*post_dve.at(t, f"y{half}"))
                    ve.bn_stats(stats[:, half], y[:, half * QUAD:(half + 1) * QUAD]).then_inc(*post_dve.mark(f"st{half}"))
                ve.wait_ge(*post_dve.at(t, "st1"))
                ve.memset(spare[:], 0.0)
                ve.bn_aggr(mv[:], stats[:]).then_inc(*post_dve.mark("mv"))
                ve.wait_ge(*post_dve.at(t, "mv"))
                ve.tensor_scalar(var[:], mv[:, 1:2], LN_EPS, None, ALU.add).then_inc(*post_dve.mark("ve"))
                ve.wait_ge(*post_act.at(t, "std"))
                ve.reciprocal(rs[:], std[:]).then_inc(*post_dve.mark("rs"))
                ve.wait_ge(*post_dve.at(t, "rs"))
                ve.wait_ge(*pe_r.at(t - 1, "x1T1"))
                ve.wait_ge(x1_stored, t * 16)
                ve.tensor_scalar(x1[:], y[:], mv[:, 0:1], rs[:], ALU.subtract, ALU.mult).then_inc(*post_dve.mark("nm"))

            def router(t):
                ve.wait_ge(*pe_r.at(t, "rt"))
                ve.tensor_copy(logits[:, row(t)].rearrange("p t e -> p (t e)"), ps[:, 7, 0:N_EXPERTS]).then_inc(*dve_r.mark("lg"))

            pre(0)
            pre(1)
            post(0)
            with ve.Fori(1, TILES - 1) as t:
                pre(t + 1)
                post(t)
                router(t - 1)
            post(TILES - 1)
            router(TILES - 2)
            router(TILES - 1)


COLS_T = SLOTS + 1
E_NOW, E_NEXT, LOAD_D, LOAD_GU, PARITY, FIELDS = 0, 1, 2, 3, 4, 5


def route(nc, d, logits, gates, scatter, gather, plan, n_slots):
    with ExitStack() as stack:
        s = Scope(nc, stack, "r_")
        E = N_EXPERTS
        full = lambda name: s.sb(name, [P, TILES, E])
        sc, sel, cand, eq, mul, oh1, oh2, member, pos, inc, inc2, work = map(full, ("sc", "sel", "cand", "eq", "mul", "oh1", "oh2", "member", "pos", "inc", "inc2", "work"))
        rb = s.sb("rb", [P, E])
        pairmax, pairsum = s.sb("pairmax", [P, TILES * EXP_GROUPS]), s.sb("pairsum", [P, TILES * EXP_GROUPS])
        gsel, geq = s.sb("gsel", [P, TILES, EXP_GROUPS]), s.sb("geq", [P, TILES, EXP_GROUPS])
        gmax = s.sb("gmax", [P, TILES])
        wt16, wt4 = s.sb("wt16", [P, E]), s.sb("wt4", [P, EXP_GROUPS])
        iota_i = s.sb("iota_i", [P, P], I32)
        cols_f, cols_i = s.sb("cols_f", [P, P]), iota_i
        pid_i, pid = s.sb("pid_i", [P, TOP_K, TILES], I32), s.sb("pid", [P, TOP_K, TILES])
        part_i, part = s.sb("part_i", [P, 1], I32), s.sb("part", [P, 1])
        tri_lt, ones = s.sb("tri_lt", [P, P]), s.sb("ones", [P, P])
        s12 = s.sb("s12", [P, TOP_K, TILES])
        den, rden = s.sb("den", [P, TILES]), s.sb("rden", [P, TILES])
        cnt_i, cnt = s.sb("cnt_i", [P, E], I32), s.sb("cnt", [P, E])
        tiles_n, slot_inc, slot_inc2, slot_base = (s.sb(n, [P, E]) for n in ("tiles_n", "slot_inc", "slot_inc2", "slot_base"))
        posk, posk_i, row_i, slot_i = s.sb("posk", [P, TOP_K, TILES]), *(s.sb(n, [P, TOP_K, TILES], I32) for n in ("posk_i", "row_i", "slot_i"))
        row_f, slot_f = s.sb("row_f", [P, TOP_K * TILES]), s.sb("slot_f", [P, TOP_K * TILES])
        in_row, in_slot = s.sb("in_row", [P, TOP_K * TILES, P]), s.sb("in_slot", [P, TOP_K * TILES, COLS_T])
        empty, val, sc_f = s.sb("empty", [P, COLS_T]), s.sb("val", [P, COLS_T]), s.sb("sc_f", [P, COLS_T])
        past, held, ends, nonempty = s.sb("past", [P, COLS_T, E]), s.sb("held", [P, COLS_T, E]), s.sb("ends", [P, COLS_T]), s.sb("nonempty", [P, E])
        fields = s.sb("fields", [P, COLS_T, FIELDS])
        tmp, tmp2 = s.sb("tmp", [P, COLS_T]), s.sb("tmp2", [P, COLS_T])
        tmp_i, par_i = s.sb("tmp_i", [P, COLS_T], I32), s.sb("par_i", [P, COLS_T], I32)
        ps = s.ps("ps", [P, 3, QUAD])
        loaded, shapes, scores_ready, step, sums, lists = (s.sem(n) for n in ("loaded", "shapes", "scores_ready", "step", "sums", "lists"))
        READY_MEMBER, READY_HOT = [None], [None]
        block = stack.enter_context(nc.Block())

        @block.sync
        def _(sp):
            sp.dma_start(rb[:], d["router_bias"].rearrange("(o e) -> o e", o=1).partition_broadcast(P)).then_inc(loaded, 16)
            sp.wait_ge(loaded, 16)

        @block.gpsimd
        def _(gp):
            gp.iota(iota_i[:], pattern=[[1, P]], base=0, channel_multiplier=0).then_inc(shapes, 1)
            gp.iota(pid_i[:], pattern=[[SEQ, TOP_K], [P, TILES]], base=1, channel_multiplier=1).then_inc(shapes, 1)
            gp.iota(part_i[:], pattern=[[0, 1]], base=PAIRS + 1, channel_multiplier=1).then_inc(shapes, 1)
            gp.memset(ones[:], 1.0).then_inc(shapes, 1)
            gp.wait_ge(shapes, 4)
            gp.affine_select(out=tri_lt[:], in_=ones[:], pattern=[[1, P]], compare_op=ALU.is_gt, fill=0.0, base=0, channel_multiplier=-1).then_inc(shapes, 1)

        @block.scalar
        def _(ac):
            ac.activation(sc[:], logits[:], ACT.Sigmoid).then_inc(scores_ready, 1)

        @block.vector
        def _(ve):
            n = [0]

            def do(ins):
                n[0] += 1
                ins.then_inc(step, 1)
                ve.wait_ge(step, n[0])

            def tt(out, a, b, op):
                do(ve.tensor_tensor(out, a, b, op))

            def ts(out, a, s1, op0, s2=None, op1=None):
                do(ve.tensor_scalar(out, a, s1, s2, op0) if op1 is None else ve.tensor_scalar(out, a, s1, s2, op0, op1))

            tiled = lambda ap: over_heads(ap, TILES)
            ve.wait_ge(shapes, 5)
            ve.wait_ge(loaded, 16)
            do(ve.tensor_copy(cols_f[:], cols_i[:]))
            do(ve.tensor_copy(pid[:], pid_i[:]))
            do(ve.tensor_copy(part[:], part_i[:]))
            ts(wt16[:], cols_f[:, 0:E], -1.0, ALU.mult, float(E), ALU.add)
            ts(wt4[:], cols_f[:, 0:EXP_GROUPS], -1.0, ALU.mult, float(EXP_GROUPS), ALU.add)
            ve.wait_ge(scores_ready, 1)
            tt(sel[:], sc[:], tiled(rb[:]), ALU.add)
            member4 = sel[:].rearrange("p t (g m) -> p (t g) m", m=PER_GROUP)
            first = True
            for i in range(PER_GROUP):
                for j in range(i + 1, PER_GROUP):
                    out = pairmax if first else pairsum
                    tt(out[:], member4[:, :, i], member4[:, :, j], ALU.add)
                    if not first:
                        tt(pairmax[:], pairmax[:], pairsum[:], ALU.max)
                    first = False
            group4 = pairmax[:].rearrange("p (t g) -> p t g", g=EXP_GROUPS)

            def first_max(values, weights, width, eq_, out, top):
                do(ve.tensor_reduce(top[:], values, AX.X, ALU.max))
                tt(eq_, values, bcast(top[:], width), ALU.is_equal)
                tt(eq_, eq_, tiled(weights), ALU.mult)
                do(ve.tensor_reduce(top[:], eq_, AX.X, ALU.max))
                tt(out, eq_, bcast(top[:], width), ALU.is_equal)

            first_max(group4, wt4[:], EXP_GROUPS, geq[:], gsel[:], gmax)
            in_group = bcast(gsel[:].rearrange("p t g -> p (t g)"), PER_GROUP)
            flat4 = lambda ap: ap.rearrange("p t (g m) -> p (t g) m", m=PER_GROUP)
            tt(flat4(cand[:]), flat4(sel[:]), in_group, ALU.mult)
            do(ve.tensor_copy(flat4(mul[:]), in_group))
            ts(mul[:], mul[:], BIG, ALU.mult, -BIG, ALU.add)
            tt(cand[:], cand[:], mul[:], ALU.add)
            first_max(cand[:], wt16[:], E, eq[:], oh1[:], gmax)
            do(ve.scalar_tensor_tensor(out=cand[:], in0=oh1[:], scalar=-4.0 * BIG, in1=cand[:], op0=ALU.mult, op1=ALU.add))
            first_max(cand[:], wt16[:], E, eq[:], oh2[:], gmax)
            for k, oh in enumerate((oh1, oh2)):
                tt(work[:], sc[:], oh[:], ALU.mult)
                do(ve.tensor_reduce(s12[:, k], work[:], AX.X, ALU.add))
            tt(den[:], s12[:, 0], s12[:, 1], ALU.add)
            do(ve.reciprocal(rden[:], den[:]))
            for k in range(TOP_K):
                tt(gates[:, k], s12[:, k], rden[:], ALU.mult)
            tt(member[:], oh1[:], oh2[:], ALU.add)
            READY_MEMBER[0] = n[0]
            ve.wait_ge(sums, 1)
            do(ve.tensor_copy(inc[:].rearrange("p t e -> p (t e)"), ps[:, 1, 0:TILES * E]))
            a, b = inc, inc2
            shift = 1
            while shift < TILES:
                do(ve.tensor_copy(b[:, 0:shift], a[:, 0:shift]))
                tt(b[:, shift:], a[:, shift:], a[:, 0:TILES - shift], ALU.add)
                a, b = b, a
                shift *= 2
            ts(cnt[:], a[:, TILES - 1], float(P - 1), ALU.add)
            do(ve.tensor_copy(cnt_i[:], cnt[:]))
            ts(cnt_i[:], cnt_i[:], 7, ALU.logical_shift_right)
            do(ve.tensor_copy(tiles_n[:], cnt_i[:]))
            do(ve.tensor_copy(slot_inc[:], tiles_n[:]))
            c, c2 = slot_inc, slot_inc2
            shift = 1
            while shift < E:
                do(ve.tensor_copy(c2[:, 0:shift], c[:, 0:shift]))
                tt(c2[:, shift:], c[:, shift:], c[:, 0:E - shift], ALU.add)
                c, c2 = c2, c
                shift *= 2
            tt(slot_base[:], c[:], tiles_n[:], ALU.subtract)
            ts(slot_base[:], slot_base[:], float(P), ALU.mult)
            tt(pos[:].rearrange("p t e -> p (t e)"), a[:].rearrange("p t e -> p (t e)"), ps[:, 1, 0:TILES * E], ALU.subtract)
            tt(pos[:].rearrange("p t e -> p (t e)"), pos[:].rearrange("p t e -> p (t e)"), ps[:, 0, 0:TILES * E], ALU.add)
            tt(pos[:], pos[:], tiled(slot_base[:]), ALU.add)
            for k, oh in enumerate((oh1, oh2)):
                tt(work[:], pos[:], oh[:], ALU.mult)
                do(ve.tensor_reduce(posk[:, k], work[:], AX.X, ALU.add))
            do(ve.tensor_copy(posk_i[:], posk[:]))
            ts(row_i[:], posk_i[:], P - 1, ALU.bitwise_and)
            ts(slot_i[:], posk_i[:], 7, ALU.logical_shift_right)
            do(ve.tensor_copy(row_f[:], row_i[:].rearrange("p k t -> p (k t)")))
            do(ve.tensor_copy(slot_f[:], slot_i[:].rearrange("p k t -> p (k t)")))
            every = TOP_K * TILES
            tt(in_row[:], over_heads(cols_f[:], every), bcast(row_f[:], P), ALU.is_equal)
            tt(in_slot[:], over_heads(cols_f[:, 0:COLS_T], every), bcast(slot_f[:], COLS_T), ALU.is_equal)
            tt(in_slot[:], in_slot[:], bcast(pid[:].rearrange("p k t -> p (k t)"), COLS_T), ALU.mult)
            READY_HOT[0] = n[0]
            slots = bcast(cols_f[:, 0:COLS_T], E)
            expert_ends = over_heads(c[:], COLS_T)
            tt(past[:], expert_ends, slots, ALU.is_le)
            do(ve.tensor_reduce(tmp[:], past[:], AX.X, ALU.add))
            ts(fields[:, :, E_NOW], tmp[:], float(E - 1), ALU.min)
            do(ve.scalar_tensor_tensor(out=held[:], in0=past[:], scalar=BIG, in1=expert_ends, op0=ALU.mult, op1=ALU.add))
            do(ve.tensor_reduce(ends[:], held[:], AX.X, ALU.min))
            tt(held[:], expert_ends, bcast(ends[:], E), ALU.is_le)
            do(ve.tensor_reduce(tmp2[:], held[:], AX.X, ALU.add))
            ts(fields[:, :, E_NEXT], tmp2[:], float(E - 1), ALU.min)
            tt(held[:], past[:], expert_ends, ALU.mult)
            do(ve.tensor_reduce(ends[:], held[:], AX.X, ALU.max))
            tt(fields[:, :, LOAD_D], ends[:], cols_f[:, 0:COLS_T], ALU.is_equal)
            ts(tmp2[:], tmp2[:], float(E), ALU.is_lt)
            tt(fields[:, :, LOAD_GU], fields[:, :, LOAD_D], tmp2[:], ALU.mult)
            ts(nonempty[:], tiles_n[:], 0.0, ALU.is_gt)
            tt(held[:], past[:], over_heads(nonempty[:], COLS_T), ALU.mult)
            do(ve.tensor_reduce(tmp[:], held[:], AX.X, ALU.add))
            do(ve.tensor_copy(tmp_i[:], tmp[:]))
            ts(par_i[:], tmp_i[:], 1, ALU.bitwise_and)
            do(ve.tensor_copy(fields[:, :, PARITY], par_i[:]))
            do(ve.tensor_copy(plan[:], fields[:]))
            do(ve.tensor_copy(n_slots[:], c[:, E - 1:E]))
            ve.wait_ge(lists, 1)
            do(ve.tensor_copy(val[:], ps[:, 2, 0:COLS_T]))
            ts(empty[:], val[:], 0.0, ALU.is_equal)
            ts(val[:], val[:], -1.0, ALU.add)
            do(ve.scalar_tensor_tensor(out=sc_f[:], in0=empty[:], scalar=part[:], in1=val[:], op0=ALU.mult, op1=ALU.add))
            do(ve.tensor_copy(scatter[:], sc_f[:]))
            ts(gather[:], scatter[:], SEQ - 1, ALU.bitwise_and)

        @block.tensor
        def _(te):
            te.wait_ge(shapes, 5)
            te.wait_ge(step, ROUTE_MEMBER)
            te.matmul(ps[:, 0, 0:TILES * E], tri_lt[:], member[:], start=True, stop=True)
            te.matmul(ps[:, 1, 0:TILES * E], ones[:], member[:], start=True, stop=True).then_inc(sums, 1)
            te.wait_ge(step, ROUTE_HOT)
            every = TOP_K * TILES
            for i in range(every):
                m = te.matmul(ps[:, 2, 0:COLS_T], in_row[:, i], in_slot[:, i], start=(i == 0), stop=(i == every - 1))
            m.then_inc(lists, 1)

        assert (READY_MEMBER[0], READY_HOT[0]) == (ROUTE_MEMBER, ROUTE_HOT), (READY_MEMBER, READY_HOT)


ROUTE_MEMBER, ROUTE_HOT = 46, 85


def experts(nc, d, ident, scatter, gather, plan, n_slots):
    with ExitStack() as stack:
        s = Scope(nc, stack, "e_")
        gu = s.sb("gu", [P, 2, 2, KC, D_MODEL])
        wd = s.sb("wd", [P, KC, D_MODEL])
        xg, xT, hs, h, hT, y = (s.sb(n, [P, D_MODEL]) for n in ("xg", "xT", "hs", "h", "hT", "y"))
        spare = s.sb("spare", [P, 2])
        g_now, s_now = s.sb("g_now", [P, 1], I32), s.sb("s_now", [P, 1], I32)
        ps = s.ps("ps", [P, 8, QUAD])
        first_loaded, gu_loaded, d_loaded = s.sem("first_loaded"), s.sem("gu_loaded"), s.sem("d_loaded")
        gathered, scattered, idx_g, idx_s = (s.sem(n) for n in ("gathered", "scattered", "idx_g", "idx_s"))
        pe = Steps(s.sem("pe_done"), ["gate0", "gate1", "up0", "up1", "xT0", "xT1", "hT0", "hT1", "y0", "y1"])
        act = Steps(s.sem("act_done"), ["silu0", "silu1", "xT0", "hT0", "y0"])
        dve = Steps(s.sem("dve_done"), ["h0", "h1", "xT1", "hT1", "y1"])
        pe_first, act_first, dve_first = s.sem("pe_first"), s.sem("act_first"), s.sem("dve_first")
        block = stack.enter_context(nc.Block())
        wg_d = d["w_gate"].rearrange("l e (k p) f -> p (l e) k f", p=P)
        wu_d = d["w_up"].rearrange("l e (k p) f -> p (l e) k f", p=P)
        wd_d = d["w_down"].rearrange("l e (k p) c -> p (l e) k c", p=P)
        x1_d = d["x1"].rearrange("t p c -> (t p) c")
        half = lambda i: slice(i * QUAD, (i + 1) * QUAD)

        def count(engine):
            return engine.value_load(n_slots[0:1, 0:1], min_val=1, max_val=SLOTS)

        def field(engine, t, f, top):
            return engine.value_load(plan[0:1, bass.ds(t, 1), f:f + 1].rearrange("p t f -> p (t f)"), min_val=0, max_val=top)

        @block.sync
        def _(sp):
            slots = count(sp)
            e0 = field(sp, 0, E_NOW, N_EXPERTS - 1)
            for i, src in enumerate((wg_d, wu_d)):
                sp.dma_start(gu[:, 0, i], src[:, bass.ds(e0, 1)].rearrange("p e k f -> p (e k) f")).then_inc(gu_loaded, 16)
            first = (gu_loaded, 32)
            sp.wait_ge(*first)
            with sp.Fori(0, slots) as t:
                now, nxt = field(sp, t, E_NOW, N_EXPERTS - 1), field(sp, t, E_NEXT, N_EXPERTS - 1)
                load_d, load_gu, par = field(sp, t, LOAD_D, 1), field(sp, t, LOAD_GU, 1), field(sp, t, PARITY, 1)
                wait_alone(sp, first, *pe.at(t - 1, "y1"))
                sp.dma_start(wd[:], wd_d[:, bass.ds(now, 1)].rearrange("p e k f -> p (e k) f"), cond=load_d).then_inc(d_loaded, 16)
                wait_alone(sp, first, *pe.at(t, "gate0"))
                for i, src in enumerate((wg_d, wu_d)):
                    sp.dma_start(gu[:, bass.ds(1 - par, 1), i].rearrange("p b k f -> p (b k) f"), src[:, bass.ds(nxt, 1)].rearrange("p e k f -> p (e k) f"), cond=load_gu).then_inc(gu_loaded, 16)

        @block.gpsimd
        def _(gp):
            slots = count(gp)
            gp.tensor_copy(g_now[:], gather[:, 0:1]).then_inc(idx_g, 1)
            gp.wait_ge(idx_g, 1)
            gp.indirect_dma_start(out=xg[:], out_offset=None, in_=x1_d, in_offset=bass.IndirectOffsetOnAxis(ap=g_now[:, 0:1], axis=0)).then_inc(gathered, 16)
            first = (pe_first, 1)
            gp.wait_ge(*first)
            with gp.Fori(0, slots) as t:
                wait_alone(gp, first, gathered, t * 16 + 16)
                gp.tensor_copy(g_now[:], gather[:, bass.ds(t + 1, 1)]).then_inc(idx_g, 1)
                wait_alone(gp, first, *pe.at(t - 1, "xT1"))
                wait_alone(gp, first, idx_g, t + 2)
                gp.indirect_dma_start(out=xg[:], out_offset=None, in_=x1_d, in_offset=bass.IndirectOffsetOnAxis(ap=g_now[:, 0:1], axis=0)).then_inc(gathered, 16)
                wait_alone(gp, first, scattered, t * 16)
                gp.tensor_copy(s_now[:], scatter[:, bass.ds(t, 1)]).then_inc(idx_s, 1)
                wait_alone(gp, first, idx_s, t + 1)
                wait_alone(gp, first, *act.at(t, "y0"))
                wait_alone(gp, first, *dve.at(t, "y1"))
                gp.indirect_dma_start(out=d["ybuf"], out_offset=bass.IndirectOffsetOnAxis(ap=s_now[:, 0:1], axis=0), in_=y[:], in_offset=None).then_inc(scattered, 16)

        @block.tensor
        def _(te):
            slots = count(te)
            pe.start(te)

            def turn_x(done):
                for i in range(2):
                    for k in range(4):
                        c = i * 4 + k
                        m = te.transpose(ps[:, 4 + i, k * P:(k + 1) * P], xg[:, c * P:(c + 1) * P], ident[:])
                    done(m, i)

            te.wait_ge(gathered, 16)
            turn_x(lambda m, i: m.then_inc(pe_first, 1) if i else None)
            te.wait_ge(act_first, 1)
            te.wait_ge(dve_first, 1)
            with te.Fori(0, slots) as t:
                par = field(te, t, PARITY, 1)
                te.wait_ge(gu_loaded, t * 32 + 32)
                te.wait_ge(*act.at(t - 1, "xT0"))
                te.wait_ge(*dve.at(t - 1, "xT1"))
                for i, name in enumerate(("gate", "up")):
                    for n in range(2):
                        te.wait_ge(*(act.at(t - 1, f"silu{n}") if i == 0 else dve.at(t - 1, f"h{n}")))
                        for k in range(KC):
                            m = te.matmul(ps[:, 2 * i + n], xT[:, k * P:(k + 1) * P], gu[:, bass.ds(par, 1), i, k, half(n)].rearrange("p b f -> p (b f)"),
                                          start=(k == 0), stop=(k == KC - 1))
                        m.then_inc(*pe.mark(f"{name}{n}"))
                te.wait_ge(gathered, t * 16 + 32)
                te.wait_ge(*act.at(t - 1, "y0"))
                te.wait_ge(*dve.at(t - 1, "y1"))
                turn_x(lambda m, i: m.then_inc(*pe.mark(f"xT{i}")))
                for i in range(2):
                    te.wait_ge(*dve.at(t, f"h{i}"))
                    if i == 0:
                        te.wait_ge(*act.at(t - 1, "hT0"))
                        te.wait_ge(*dve.at(t - 1, "hT1"))
                    for k in range(4):
                        c = i * 4 + k
                        m = te.transpose(ps[:, 6 + i, k * P:(k + 1) * P], h[:, c * P:(c + 1) * P], ident[:])
                    m.then_inc(*pe.mark(f"hT{i}"))
                te.wait_ge(d_loaded, t * 16 + 16)
                te.wait_ge(*act.at(t, "hT0"))
                te.wait_ge(*dve.at(t, "hT1"))
                te.wait_ge(*act.at(t, "xT0"))
                te.wait_ge(*dve.at(t, "xT1"))
                for n in range(2):
                    for k in range(KC):
                        m = te.matmul(ps[:, 4 + n], hT[:, k * P:(k + 1) * P], wd[:, k, half(n)], start=(k == 0), stop=(k == KC - 1))
                    m.then_inc(*pe.mark(f"y{n}"))

        @block.scalar
        def _(sc):
            slots = count(sc)
            act.start(sc)
            sc.wait_ge(pe_first, 1)
            sc.activation(xT[:, half(0)], ps[:, 4], ACT.Copy).then_inc(act_first, 1)
            with sc.Fori(0, slots) as t:
                for n in range(2):
                    sc.wait_ge(*pe.at(t, f"gate{n}"))
                    sc.wait_ge(*dve.at(t - 1, f"h{n}"))
                    sc.activation(hs[:, half(n)], ps[:, n], ACT.Silu).then_inc(*act.mark(f"silu{n}"))
                sc.wait_ge(*pe.at(t, "xT0"))
                sc.activation(xT[:, half(0)], ps[:, 4], ACT.Copy).then_inc(*act.mark("xT0"))
                sc.wait_ge(*pe.at(t, "hT0"))
                sc.activation(hT[:, half(0)], ps[:, 6], ACT.Copy).then_inc(*act.mark("hT0"))
                sc.wait_ge(*pe.at(t, "y0"))
                sc.wait_ge(scattered, t * 16)
                sc.activation(y[:, half(0)], ps[:, 4], ACT.Copy).then_inc(*act.mark("y0"))

        @block.vector
        def _(ve):
            slots = count(ve)
            dve.start(ve)
            ve.wait_ge(pe_first, 1)
            ve.tensor_copy(xT[:, half(1)], ps[:, 5]).then_inc(dve_first, 1)
            with ve.Fori(0, slots) as t:
                for n in range(2):
                    ve.wait_ge(*pe.at(t, f"up{n}"))
                    ve.wait_ge(*act.at(t, f"silu{n}"))
                    ve.tensor_tensor(h[:, half(n)], hs[:, half(n)], ps[:, 2 + n], ALU.mult).then_inc(*dve.mark(f"h{n}"))
                ve.wait_ge(*pe.at(t, "xT1"))
                ve.tensor_copy(xT[:, half(1)], ps[:, 5]).then_inc(*dve.mark("xT1"))
                ve.wait_ge(*pe.at(t, "hT1"))
                ve.tensor_copy(hT[:, half(1)], ps[:, 7]).then_inc(*dve.mark("hT1"))
                ve.wait_ge(*pe.at(t, "y1"))
                ve.wait_ge(scattered, t * 16)
                ve.tensor_copy(y[:, half(1)], ps[:, 5]).then_inc(*dve.mark("y1"))
            ve.wait_ge(scattered, slots * 16)
            ve.memset(spare[:, 0:1], 0.0)
            ve.wait_ge(gu_loaded, slots * 32 + 32)
            ve.memset(spare[:, 1:2], 0.0)


def combine(nc, d, gates, out):
    with ExitStack() as stack:
        s = Scope(nc, stack, "c_")
        B2 = range(2)
        buf = lambda name, shape: [s.sb(f"{name}{b}", shape) for b in B2]
        x1, y0, y1, acc, res = (buf(n, [P, D_MODEL]) for n in ("x1", "y0", "y1", "acc", "res"))
        stats, mv, var, std, rs = (buf(n, sh) for n, sh in (("stats", [P, 2, 6]), ("mv", [P, 2]), ("var", [P, 1]), ("std", [P, 1]), ("rs", [P, 1])))
        lng, lnb = s.sb("lng", [P, D_MODEL]), s.sb("lnb", [P, D_MODEL])
        spare = s.sb("spare", [P, 1])
        small_loaded = s.sem("small_loaded")
        loaded, stored = [s.sem(f"loaded{b}") for b in B2], [s.sem(f"stored{b}") for b in B2]
        act = Steps(s.sem("act_done"), ["gated0", "std"])
        dve = Steps(s.sem("dve_done"), ["gated1", "sum", "st0", "st1", "mv", "ve", "rs", "nm"])
        pool = Steps(s.sem("pool_done"), ["g", "b"])
        block = stack.enter_context(nc.Block())
        out_d = out.rearrange("b (t p) c -> (b t) p c", p=P)
        y_d = d["ybuf"][0:PAIRS].rearrange("(k t p) c -> k t p c", k=TOP_K, p=P)
        row = lambda t: bass.ds(t, 1)

        @block.sync
        def _(sp):
            def load(t, b):
                for dst, src in ((x1, d["x1"]), (y0, y_d[0]), (y1, y_d[1])):
                    sp.dma_start(dst[b][:], src[row(t)].rearrange("t p c -> p (t c)")).then_inc(loaded[b], 16)

            load(0, 0)
            load(1, 1)
            sp.wait_ge(small_loaded, 32)
            with sp.Fori(1, TILES // 2) as i:
                for b in B2:
                    wait_alone(sp, (small_loaded, 32), *dve.at(2 * i + b - 2, "sum"))
                    load(2 * i + b, b)

        @block.gpsimd
        def _(gp):
            gp.dma_start(lng[:], d["ln2_g"].partition_broadcast(P)).then_inc(small_loaded, 16)
            gp.dma_start(lnb[:], d["ln2_b"].partition_broadcast(P)).then_inc(small_loaded, 16)
            pool.start(gp)
            gp.wait_ge(small_loaded, 32)
            with gp.Fori(0, TILES // 2) as i:
                for b in B2:
                    t = 2 * i + b
                    gp.wait_ge(*dve.at(t, "nm"))
                    gp.tensor_tensor(res[b][:], res[b][:], lng[:], ALU.mult).then_inc(*pool.mark("g"))
                    gp.wait_ge(*pool.at(t, "g"))
                    gp.tensor_tensor(res[b][:], res[b][:], lnb[:], ALU.add).then_inc(*pool.mark("b"))

        @block.scalar
        def _(sc):
            act.start(sc)
            sc.wait_ge(small_loaded, 32)
            with sc.Fori(0, TILES // 2) as i:
                for b in B2:
                    t = 2 * i + b
                    sc.wait_ge(loaded[b], i * 48 + 48)
                    sc.activation(y0[b][:], y0[b][:], ACT.Copy, scale=gates[:, 0, row(t)]).then_inc(*act.mark("gated0"))
                    sc.wait_ge(*dve.at(t, "ve"))
                    sc.activation(std[b][:], var[b][:], ACT.Sqrt).then_inc(*act.mark("std"))
                    wait_alone(sc, (small_loaded, 32), *pool.at(t, "b"))
                    sc.dma_start(out_d[row(t)].rearrange("t p c -> p (t c)"), res[b][:]).then_inc(stored[b], 16)
            for b in B2:
                sc.wait_ge(stored[b], 8 * TILES)

        @block.vector
        def _(ve):
            dve.start(ve)
            with ve.Fori(0, TILES // 2) as i:
                for b in B2:
                    t = 2 * i + b
                    ve.wait_ge(*act.at(t, "gated0"))
                    ve.wait_ge(*dve.at(t - 1, "nm"))
                    ve.scalar_tensor_tensor(out=acc[b][:], in0=y1[b][:], scalar=gates[:, 1, row(t)], in1=y0[b][:], op0=ALU.mult, op1=ALU.add).then_inc(*dve.mark("gated1"))
                    ve.wait_ge(*dve.at(t, "gated1"))
                    ve.scalar_tensor_tensor(out=acc[b][:], in0=x1[b][:], scalar=ALPHA, in1=acc[b][:], op0=ALU.mult, op1=ALU.add).then_inc(*dve.mark("sum"))
                    ve.wait_ge(*dve.at(t, "sum"))
                    for half in range(2):
                        ve.bn_stats(stats[b][:, half], acc[b][:, half * QUAD:(half + 1) * QUAD]).then_inc(*dve.mark(f"st{half}"))
                    ve.wait_ge(*dve.at(t, "st1"))
                    ve.memset(spare[:], 0.0)
                    ve.bn_aggr(mv[b][:], stats[b][:]).then_inc(*dve.mark("mv"))
                    ve.wait_ge(*dve.at(t, "mv"))
                    ve.tensor_scalar(var[b][:], mv[b][:, 1:2], LN_EPS, None, ALU.add).then_inc(*dve.mark("ve"))
                    ve.wait_ge(*act.at(t, "std"))
                    ve.reciprocal(rs[b][:], std[b][:]).then_inc(*dve.mark("rs"))
                    ve.wait_ge(*dve.at(t, "rs"))
                    ve.wait_ge(stored[b], i * 16)
                    ve.tensor_scalar(res[b][:], acc[b][:], mv[b][:, 0:1], rs[b][:], ALU.subtract, ALU.mult).then_inc(*dve.mark("nm"))


INPUTS = ["x", "w_in", "conv_w", "a_log_f", "dt_bias_f", "a_log_b", "dt_bias_b", "delta_norm_w", "sgu_ln_g", "sgu_ln_b",
          "w_spatial", "b_spatial", "w_out", "ln1_g", "ln1_b", "w_router", "router_bias", "w_gate", "w_up", "w_down",
          "ln2_g", "ln2_b"]


def build(nc, d, out):
    scratch = {
        "raw": [P, 3, HEADS, SEQ + 2 * HALO], "z": [TILES, P, QUAD], "sgu": [TILES, P, QUAD],
        "pk": [TILES, P, 4, QUAD], "gb": [TILES * CHAINS, P], "x1": [TILES, P, D_MODEL],
        "ybuf": [PAIRS + P, D_MODEL],
    }
    for name, shape in scratch.items():
        d[name] = nc.dram_tensor("s_" + name, shape, F32, kind="Internal").ap()
    with ExitStack() as stack:
        sb = lambda name, shape, dt=F32: stack.enter_context(nc.sbuf_tensor(name, shape, dt))
        ident = sb("ident", [P, P])
        gates = sb("gates", [P, TOP_K, TILES])
        logits = sb("logits", [P, TILES, N_EXPERTS])
        scatter, gather = sb("scatter", [P, COLS_T], I32), sb("gather", [P, COLS_T], I32)
        plan, n_slots = sb("plan", [P, COLS_T, FIELDS], I32), sb("n_slots", [P, 1], I32)
        constants(nc, ident)
        with ExitStack() as first:
            sb1 = lambda name, shape: first.enter_context(nc.sbuf_tensor(name, shape, F32))
            GS = sb1("gate_scalars", [P, TILES, KINDS, CHAINS])
            with nc.sbuf_tensor("gates_raw", [P, TILES, 16], F32) as graw:
                project(nc, d, ident, graw)
                gates_and_conv(nc, d, ident, graw, GS)
            outs = [sb1("out_f", [P, TILES, QUAD]), sb1("out_b", [P, TILES, QUAD])]
            delta(nc, d, ident, GS, outs)
            mix(nc, d, ident, outs, logits)
        route(nc, d, logits, gates, scatter, gather, plan, n_slots)
        experts(nc, d, ident, scatter, gather, plan, n_slots)
        combine(nc, d, gates, out)


def kernel(**inputs):
    import numpy as np
    import concourse.bacc as bacc
    from concourse.bass_utils import run_bass_kernel_spmd

    nc = bacc.Bacc("TRN2", target_bir_lowering=False, num_devices=1)
    arrays, d = {}, {}
    for name in INPUTS:
        a = np.ascontiguousarray(inputs[name])
        arrays["in_" + name] = a
        d[name] = nc.dram_tensor("in_" + name, a.shape, mybir.dt.from_np(a.dtype), kind="ExternalInput").ap()
    out = nc.dram_tensor("out", (1, SEQ, D_MODEL), F32, kind="ExternalOutput").ap()
    build(nc, d, out)
    return run_bass_kernel_spmd(nc, [arrays], core_ids=[0]).results[0]["out"]
```

```python
from contextlib import ExitStack

import concourse.bass as bass
from concourse import mybir

F32 = mybir.dt.float32
F32R = mybir.dt.float32r
I32 = mybir.dt.int32
U32 = mybir.dt.uint32
ALU = mybir.AluOpType
ACT = mybir.ActivationFunctionType
AX = mybir.AxisListType

P = 128
D_MODEL = 1024
SEQ = 2048
HEADS = 4
QUAD = HEADS * P
KC = D_MODEL // P
TILES = SEQ // P
GROUP = 4
GROUPS = TILES // GROUP
TOKENS = GROUP * P
TAPS = 5
HALO = TAPS // 2
N_EXPERTS = 16
EXP_GROUPS = 4
PER_GROUP = N_EXPERTS // EXP_GROUPS
TOP_K = 2
PAIRS = SEQ * TOP_K
ALPHA = 2.0 ** 0.25
LN_EPS, RMS_EPS, L2_EPS = 1e-5, 1e-6, 1e-6

Q0, Z0, G0, U0, V0, COLS = 0, 3 * QUAD, 4 * QUAD, 4 * QUAD + 16, 5 * QUAD + 16, 6 * QUAD + 16
CHAINS = 2 * HEADS
KINDS = 6
GC, BETA, NBE, EG, KD, EL = range(KINDS)
BIG = 1e30


class Steps:

    def __init__(self, sem, names):
        self.sem, self.names, self.n = sem, list(names), 0
        self.pos = {name: i for i, name in enumerate(self.names)}
        assert len(self.pos) == len(self.names)

    def mark(self, name):
        assert self.names[self.n % len(self.names)] == name, (self.names[self.n % len(self.names)], name)
        self.n += 1
        return self.sem, 1

    def at(self, turn, name):
        return self.sem, (turn + 1) * len(self.names) + self.pos[name] + 1

    def start(self, engine, but=0):
        engine.sem_inc(self.sem, len(self.names) - but)
        self.n = len(self.names) - but


def wait_alone(engine, met, sem, value):
    if not isinstance(value, int):
        with engine.register() as target:
            engine.reg_mov(target, value)
            engine.wait_ge(*met)
            engine.wait_ge(sem, target)
    else:
        engine.wait_ge(sem, value)


class Scope:

    def __init__(self, nc, stack, tag):
        self.nc, self.stack, self.tag = nc, stack, tag

    def sb(self, name, shape, dt=F32):
        return self.stack.enter_context(self.nc.sbuf_tensor(self.tag + name, shape, dt))

    def ps(self, name, shape, dt=F32):
        return self.stack.enter_context(self.nc.psum_tensor(self.tag + name, shape, dt))

    def sem(self, name):
        return self.stack.enter_context(self.nc.semaphore(self.tag + name))


def bcast(ap, n):
    return ap.unsqueeze(2).to_broadcast([ap.shape[0], ap.shape[1], n])


def over_heads(ap, n=HEADS):
    return ap.unsqueeze(1).to_broadcast([ap.shape[0], n, ap.shape[1]])


def heads(ap):
    return ap.rearrange("p (h m) -> p h m", h=HEADS)


def constants(nc, ident):
    with ExitStack() as stack:
        s = Scope(nc, stack, "k_")
        zeroed, done = s.sem("zeroed"), s.sem("done")
        block = stack.enter_context(nc.Block())

        @block.gpsimd
        def _(pool):
            pool.memset(ident[:], 0.0).then_inc(zeroed, 1)
            pool.wait_ge(zeroed, 1)
            pool.affine_select(out=ident[:], in_=ident[:], pattern=[[-1, P]], compare_op=ALU.not_equal,
                               fill=1.0, base=0, channel_multiplier=1).then_inc(done, 1)
            pool.wait_ge(done, 1)


def three_passes(te, out, a_hi, a_lo, b_hi, b_lo, first, last):
    te.matmul(out, a_hi, b_hi, start=first, stop=False)
    te.matmul(out, a_hi, b_lo, start=False, stop=False)
    return te.matmul(out, a_lo, b_hi, start=False, stop=last)


def project(nc, d, ident, graw):
    with ExitStack() as stack:
        s = Scope(nc, stack, "a_")
        CW = 2 * P
        starts = [Q0 + c * CW for c in range(6)] + [m + c * CW for m in (U0, V0, Z0) for c in range(2)]
        CHUNKS = len(starts)
        BY_CHANNEL = 8
        RAW, SPLIT, OUT = 4, 3, 3
        K8, J4 = range(KC), range(GROUP)
        w = [s.sb(f"w{r}", [P, KC, CW]) for r in range(RAW)]
        whi = [s.sb(f"whi{r}", [P, KC, CW], F32R) for r in range(SPLIT)]
        wlo = [s.sb(f"wlo{r}", [P, KC, CW], F32R) for r in range(SPLIT)]
        wg, wghi, wglo = s.sb("wg", [P, KC, P]), s.sb("wghi", [P, KC, P], F32R), s.sb("wglo", [P, KC, P], F32R)
        gatesT = s.sb("gatesT", [P, TOKENS])
        xrow = s.sb("xrow", [P, GROUP, D_MODEL])
        xhi, xlo = s.sb("xhi", [P, KC, TOKENS], F32R), s.sb("xlo", [P, KC, TOKENS], F32R)
        raw = [s.sb(f"raw{r}", [P, 2, TOKENS]) for r in range(OUT)]
        zero = s.sb("zero", [P, 3 * HEADS * HALO])
        uT = s.sb("uT", [P, HEADS, TOKENS])
        vn = s.sb("vn", [P, GROUP, QUAD])
        zs = s.sb("zs", [P, GROUP, QUAD])
        osgu = s.sb("osgu", [P, GROUP, QUAD])
        stats, mv = s.sb("stats", [P, GROUP, 6]), s.sb("mv", [P, GROUP, 2])
        var, std, rstd = (s.sb(n, [P, GROUP]) for n in ("var", "std", "rstd"))
        wsp, wspT = s.sb("wsp", [P, HEADS, P]), s.sb("wspT", [P, HEADS, P])
        bsp, lng, lnb = (s.sb(n, [P, QUAD]) for n in ("bsp", "lng", "lnb"))
        spare = s.sb("spare", [P, 1])
        ps = s.ps("ps", [P, 8, QUAD])

        w_loaded = [s.sem(f"w_loaded{r}") for r in range(RAW)]
        small_loaded, wg_loaded, x_loaded = s.sem("small_loaded"), s.sem("wg_loaded"), s.sem("x_loaded")
        wsp_turned, wspT_ready, wghi_ready, wglo_ready = (s.sem(n) for n in ("wsp_turned", "wspT_ready", "wghi_ready", "wglo_ready"))
        zero_ready, edges_stored = s.sem("zero_ready"), s.sem("edges_stored")
        raw_stored = [s.sem(f"raw_stored{r}") for r in range(OUT)]
        z_stored, sgu_stored = s.sem("z_stored"), s.sem("sgu_stored")

        xs = [f"x{c}" for c in K8]
        order = [*range(SPLIT, CHUNKS), *range(SPLIT)]
        pe = Steps(s.sem("pe_done"), [f"cm{n}" for n in range(2 * BY_CHANNEL)] + ["v"] + [f"v{j}" for j in J4] + ["z", "gatesT"]
                   + [f"z{j}" for j in J4] + ["gates"] + [f"sp{j}" for j in J4])
        pe_x, act_x, dve_x = (Steps(s.sem(n), xs) for n in ("pe_x", "act_x", "dve_x"))
        act_split, dve_split = (Steps(s.sem(n), [f"w{i}" for i in order]) for n in ("act_split", "dve_split"))
        act = Steps(s.sem("act_done"), [f"raw{n}" for n in range(0, 12, 2)] + [f"u{h}" for h in range(HEADS)]
                    + [f"v{j}" for j in J4] + ["std"] + [f"z{j}" for j in J4])
        dve = Steps(s.sem("dve_done"), [f"raw{n}" for n in range(1, 12, 2)]
                    + [x for j in J4 for x in (f"stats{j}", f"mv{j}")] + ["var", "rstd"]
                    + [f"vn{j}" for j in J4] + ["gatesT", "gates"] + [f"mixed{j}" for j in J4] + [f"sgu{j}" for j in J4])
        pool = Steps(s.sem("pool_done"), [x for j in J4 for x in (f"g{j}", f"b{j}")])

        block = stack.enter_context(nc.Block())
        raw_d = d["raw"]
        z_d = d["z"]
        sgu_d = d["sgu"]
        x_d = d["x"].rearrange("b (t p) c -> p (b t) c", p=P)
        w_d = d["w_in"].rearrange("l (k p) c -> p (l k) c", p=P)

        def groups(engine, body):
            with engine.Fori(0, GROUPS - 1) as g:
                body(g, False)
            body(GROUPS - 1, True)

        def turn_of(g, i):
            return g - 1 if i < SPLIT else g

        def before(g, i, ring):
            return (g, i - ring) if i >= ring else (g - 1, i + CHUNKS - ring)

        def used(g, i):
            return pe.at(g, f"cm{2 * i + 1}" if i < BY_CHANNEL else ("v", "v3", "z", "z3")[i - BY_CHANNEL])

        def stored_before(engine, g, i):
            engine.wait_ge(raw_stored[i % OUT], (g * 2 + i // OUT + 1) * 16)

        @block.sync
        def _(sp):
            def load(i):
                sp.dma_start(w[i % RAW][:], w_d[:, :, starts[i]:starts[i] + CW]).then_inc(w_loaded[i % RAW], 16)

            load(0)
            sp.dma_start(xrow[:], x_d[:, 0:GROUP, :]).then_inc(x_loaded, 16)
            for i in range(1, RAW):
                load(i)
            for sem in (*raw_stored, z_stored, sgu_stored):
                sp.sem_inc(sem, 16)
            met = (x_loaded, 16)
            sp.wait_ge(*met)

            def body(g, last):
                if not last:
                    wait_alone(sp, met, *pe_x.at(g - 1, f"x{KC - 1}"))
                    sp.dma_start(xrow[:], x_d[:, bass.ds(g * GROUP + GROUP, GROUP), :]).then_inc(x_loaded, 16)
                for i in range(CHUNKS):
                    if not last or i + RAW < CHUNKS:
                        for half in (act_split, dve_split):
                            wait_alone(sp, met, *half.at(turn_of(g, i), f"w{i}"))
                        load((i + RAW) % CHUNKS)
                    if i < 6:
                        wait_alone(sp, met, *act.at(g, f"raw{2 * i}"))
                        wait_alone(sp, met, *dve.at(g, f"raw{2 * i + 1}"))
                        h = 2 * (i % 2)
                        sp.dma_start(raw_d[:, i // 2, h:h + 2, bass.ds(g * TOKENS + HALO, TOKENS)], raw[i % OUT][:]).then_inc(raw_stored[i % OUT], 16)
                wait_alone(sp, met, *act.at(g, f"z{GROUP - 1}"))
                sp.dma_start(z_d[bass.ds(g * GROUP, GROUP)].rearrange("t p c -> p t c"), zs[:]).then_inc(z_stored, 16)
                wait_alone(sp, met, *dve.at(g, f"sgu{GROUP - 1}"))
                sp.dma_start(sgu_d[bass.ds(g * GROUP, GROUP)].rearrange("t p c -> p t c"), osgu[:]).then_inc(sgu_stored, 16)

            groups(sp, body)
            for sem in raw_stored:
                sp.wait_ge(sem, (2 * GROUPS + 1) * 16)
            for sem in (z_stored, sgu_stored):
                sp.wait_ge(sem, (GROUPS + 1) * 16)

        @block.gpsimd
        def _(gp):
            gp.memset(zero[:], 0.0).then_inc(zero_ready, 1)
            gp.wait_ge(zero_ready, 1)
            for lo in (0, SEQ + HALO):
                gp.dma_start(raw_d[:, :, :, lo:lo + HALO], zero[:].rearrange("p (b h e) -> p b h e", b=3, h=HEADS)).then_inc(edges_stored, 16)
            pool.start(gp)
            gp.wait_ge(small_loaded, 64)
            with gp.Fori(0, GROUPS) as g:
                for j in J4:
                    gp.wait_ge(*dve.at(g, f"vn{j}"))
                    gp.tensor_tensor(vn[:, j], vn[:, j], lng[:], ALU.mult).then_inc(*pool.mark(f"g{j}"))
                    gp.wait_ge(*pool.at(g, f"g{j}"))
                    gp.tensor_tensor(vn[:, j], vn[:, j], lnb[:], ALU.add).then_inc(*pool.mark(f"b{j}"))
            gp.wait_ge(edges_stored, 32)

        @block.tensor
        def _(te):
            pe.start(te)

            def turn_x(cs):
                for c in cs:
                    for j in J4:
                        m = te.transpose(ps[:, c, j * P:(j + 1) * P], xrow[:, j, c * P:(c + 1) * P], ident[:])
                    m.then_inc(*pe_x.mark(f"x{c}"))

            def split_ready(g, i):
                for half in (act_split, dve_split):
                    te.wait_ge(*half.at(turn_of(g, i), f"w{i}"))

            te.wait_ge(small_loaded, 64)
            for h in range(HEADS):
                m = te.transpose(ps[:, 7, h * P:(h + 1) * P], wsp[:, h], ident[:])
            m.then_inc(wsp_turned, 1)
            te.wait_ge(x_loaded, 16)
            turn_x(K8[:-1])
            te.wait_ge(wspT_ready, 1)
            turn_x(K8[-1:])

            def body(g, last):
                for n in range(2 * BY_CHANNEL):
                    i = n // 2
                    if n % 2 == 0:
                        split_ready(g, i)
                    if n >= 4:
                        te.wait_ge(*(act if n % 2 == 0 else dve).at(g, f"raw{n - 4}"))
                    cols = slice((n % 2) * P, (n % 2 + 1) * P)
                    for k in K8:
                        if n == 0:
                            te.wait_ge(*act_x.at(g - 1, f"x{k}"))
                            te.wait_ge(*dve_x.at(g - 1, f"x{k}"))
                        m = three_passes(te, ps[:, n % 4], whi[i % SPLIT][:, k, cols], wlo[i % SPLIT][:, k, cols], xhi[:, k], xlo[:, k], k == 0, k == KC - 1)
                    m.then_inc(*pe.mark(f"cm{n}"))

                def by_token(bank, at, j, hi, lo):
                    for k in K8:
                        rows = slice(j * P, (j + 1) * P)
                        m = three_passes(te, ps[:, bank, at:at + CW], xhi[:, k, rows], xlo[:, k, rows], hi[:, k], lo[:, k], k == 0, k == KC - 1)
                    return m

                def pair(i, bank, name, free):
                    split_ready(g, i)
                    for j in J4:
                        for wait in free(j):
                            te.wait_ge(*wait)
                        m = by_token(bank + j, 0, j, whi[i % SPLIT], wlo[i % SPLIT])
                    m.then_inc(*pe.mark(name))
                    if name == "z":
                        te.wait_ge(*act.at(g, "v0"))
                        te.wait_ge(wghi_ready, 1)
                        te.wait_ge(wglo_ready, 1)
                        for k in K8:
                            m = three_passes(te, ps[:, 4], wghi[:, k], wglo[:, k], xhi[:, k], xlo[:, k], k == 0, k == KC - 1)
                        m.then_inc(*pe.mark("gatesT"))
                    split_ready(g, i + 1)
                    for j in J4:
                        by_token(bank + j, CW, j, whi[(i + 1) % SPLIT], wlo[(i + 1) % SPLIT]).then_inc(*pe.mark(f"{name}{j}"))

                pair(BY_CHANNEL, 4, "v", lambda j: [])
                pair(BY_CHANNEL + 2, 0, "z", lambda j: [act.at(g, f"u{j}")])
                te.wait_ge(*dve.at(g, "gatesT"))
                for j in J4:
                    m = te.transpose(ps[:, 4, j * P:(j + 1) * P], gatesT[:, j * P:(j + 1) * P], ident[:])
                m.then_inc(*pe.mark("gates"))
                for j in J4:
                    te.wait_ge(*(act.at(g, f"v{j}") if j else dve.at(g, "gates")))
                    te.wait_ge(*pool.at(g, f"b{j}"))
                    for h in range(HEADS):
                        m = te.matmul(ps[:, 4 + j, h * P:(h + 1) * P], vn[:, j, h * P:(h + 1) * P], wspT[:, h], start=True, stop=True)
                    m.then_inc(*pe.mark(f"sp{j}"))
                if not last:
                    te.wait_ge(x_loaded, g * 16 + 32)
                    for c in K8:
                        te.wait_ge(*(act.at(g, f"z{c}") if c < 4 else dve.at(g, f"mixed{c - 4}")))
                        turn_x([c])

            groups(te, body)

        def chunk_loaded(engine, g, i):
            engine.wait_ge(w_loaded[i % RAW], (g * (CHUNKS // RAW) + i // RAW + 1) * 16)
            engine.wait_ge(*used(*before(g, i, SPLIT)))

        @block.scalar
        def _(sc):
            sc.dma_start(wsp[:], d["w_spatial"].rearrange("l g p q -> p (l g) q")).then_inc(small_loaded, 16)
            sc.dma_start(bsp[:], d["b_spatial"].rearrange("l g p -> l (g p)").partition_broadcast(P)).then_inc(small_loaded, 16)
            sc.dma_start(lng[:], d["sgu_ln_g"].partition_broadcast(P)).then_inc(small_loaded, 16)
            sc.dma_start(lnb[:], d["sgu_ln_b"].partition_broadcast(P)).then_inc(small_loaded, 16)
            sc.dma_start(wg[:], w_d[:, :, G0:G0 + P]).then_inc(wg_loaded, 16)
            act.start(sc)
            act_split.start(sc, but=SPLIT)

            def split(g, i):
                chunk_loaded(sc, g, i)
                q, j = before(g, i, SPLIT)
                sc.wait_ge(*dve_split.at(turn_of(q, j), f"w{j}"))
                sc.activation(whi[i % SPLIT][:], w[i % RAW][:], ACT.Copy).then_inc(*act_split.mark(f"w{i}"))

            def split_x(g):
                for c in K8:
                    sc.wait_ge(*pe_x.at(g, f"x{c}"))
                    sc.activation(xhi[:, c], ps[:, c], ACT.Copy).then_inc(*act_x.mark(f"x{c}"))

            for i in range(SPLIT):
                if i == 1:
                    split_x(-1)
                sc.wait_ge(w_loaded[i], 16)
                sc.activation(whi[i][:], w[i][:], ACT.Copy).then_inc(*act_split.mark(f"w{i}"))
            sc.wait_ge(wg_loaded, 16)
            sc.activation(wghi[:], wg[:], ACT.Copy).then_inc(wghi_ready, 1)

            def body(g, last):
                for i in range(6):
                    sc.wait_ge(*pe.at(g, f"cm{2 * i}"))
                    stored_before(sc, g, i)
                    sc.activation(raw[i % OUT][:, 0], ps[:, 2 * i % 4], ACT.Copy).then_inc(*act.mark(f"raw{2 * i}"))
                    split(g, i + SPLIT)
                sc.wait_ge(*dve.at(g - 1, f"sgu{GROUP - 1}"))
                for h in range(HEADS):
                    sc.wait_ge(*pe.at(g, f"cm{12 + h}"))
                    sc.activation(uT[:, h], ps[:, h], ACT.Gelu).then_inc(*act.mark(f"u{h}"))
                    if h % 2:
                        split(g, 9 + h // 2)
                split(g, 11)
                for j in J4:
                    sc.wait_ge(*pe.at(g, f"v{j}"))
                    sc.activation(vn[:, j], ps[:, 4 + j], ACT.Gelu).then_inc(*act.mark(f"v{j}"))
                if not last:
                    split(g + 1, 0)
                sc.wait_ge(*dve.at(g, "var"))
                sc.activation(std[:], var[:], ACT.Sqrt).then_inc(*act.mark("std"))
                if not last:
                    split(g + 1, 1)
                sc.wait_ge(z_stored, g * 16 + 16)
                for j in J4:
                    sc.wait_ge(*pe.at(g, f"z{j}"))
                    sc.activation(zs[:, j], ps[:, j], ACT.Silu).then_inc(*act.mark(f"z{j}"))
                if not last:
                    split_x(g)
                    split(g + 1, 2)

            groups(sc, body)

        @block.vector
        def _(ve):
            dve.start(ve)
            dve_split.start(ve, but=SPLIT)

            def split(g, i):
                chunk_loaded(ve, g, i)
                ve.wait_ge(*act_split.at(turn_of(g, i), f"w{i}"))
                ve.tensor_tensor(wlo[i % SPLIT][:], w[i % RAW][:], whi[i % SPLIT][:], ALU.subtract).then_inc(*dve_split.mark(f"w{i}"))

            def split_x(g, cs):
                for c in cs:
                    ve.wait_ge(*act_x.at(g, f"x{c}"))
                    ve.tensor_tensor(xlo[:, c], ps[:, c], xhi[:, c], ALU.subtract).then_inc(*dve_x.mark(f"x{c}"))

            ve.wait_ge(wsp_turned, 1)
            ve.tensor_copy(wspT[:], ps[:, 7].rearrange("p (h m) -> p h m", h=HEADS)).then_inc(wspT_ready, 1)
            for i in range(SPLIT):
                if i == 1:
                    split_x(-1, K8)
                ve.wait_ge(*act_split.at(-1, f"w{i}"))
                ve.tensor_tensor(wlo[i][:], w[i][:], whi[i][:], ALU.subtract).then_inc(*dve_split.mark(f"w{i}"))
            ve.wait_ge(wghi_ready, 1)
            ve.tensor_tensor(wglo[:], wg[:], wghi[:], ALU.subtract).then_inc(wglo_ready, 1)
            ve.wait_ge(small_loaded, 64)

            def body(g, last):
                for i in range(6):
                    ve.wait_ge(*pe.at(g, f"cm{2 * i + 1}"))
                    stored_before(ve, g, i)
                    ve.tensor_copy(raw[i % OUT][:, 1], ps[:, (2 * i + 1) % 4]).then_inc(*dve.mark(f"raw{2 * i + 1}"))
                    split(g, i + SPLIT)
                for i in (9, 10, 11):
                    split(g, i)
                for j in J4:
                    ve.wait_ge(*act.at(g, f"v{j}"))
                    ve.bn_stats(stats[:, j], vn[:, j]).then_inc(*dve.mark(f"stats{j}"))
                    ve.wait_ge(*dve.at(g, f"stats{j}"))
                    ve.memset(spare[:], 0.0)
                    ve.bn_aggr(mv[:, j], stats[:, j]).then_inc(*dve.mark(f"mv{j}"))
                ve.wait_ge(*dve.at(g, f"mv{GROUP - 1}"))
                ve.tensor_scalar(var[:], mv[:, :, 1], LN_EPS, None, ALU.add).then_inc(*dve.mark("var"))
                if not last:
                    split(g + 1, 0)
                ve.wait_ge(*act.at(g, "std"))
                ve.reciprocal(rstd[:], std[:]).then_inc(*dve.mark("rstd"))
                ve.wait_ge(*dve.at(g, "rstd"))
                for j in J4:
                    ve.tensor_scalar(vn[:, j], vn[:, j], mv[:, j, 0:1], rstd[:, j:j + 1], ALU.subtract, ALU.mult).then_inc(*dve.mark(f"vn{j}"))
                ve.wait_ge(*pe.at(g, "gatesT"))
                ve.tensor_copy(gatesT[:], ps[:, 4]).then_inc(*dve.mark("gatesT"))
                if not last:
                    split(g + 1, 1)
                ve.wait_ge(*pe.at(g, "gates"))
                ve.tensor_copy(graw[:, bass.ds(g * GROUP, GROUP)], ps[:, 4].rearrange("p (j c) -> p j c", j=GROUP)[:, :, 0:16]).then_inc(*dve.mark("gates"))
                ve.wait_ge(sgu_stored, g * 16 + 16)
                for j in J4:
                    ve.wait_ge(*pe.at(g, f"sp{j}"))
                    ve.tensor_tensor(osgu[:, j], ps[:, 4 + j], bsp[:], ALU.add).then_inc(*dve.mark(f"mixed{j}"))
                if not last:
                    split_x(g, K8)
                    split(g + 1, 2)
                for j in J4:
                    ve.wait_ge(*dve.at(g, f"mixed{j}"))
                    ve.tensor_tensor(heads(osgu[:, j]), heads(osgu[:, j]), uT[:, :, j * P:(j + 1) * P], ALU.mult).then_inc(*dve.mark(f"sgu{j}"))

            groups(ve, body)


def gates_and_conv(nc, d, ident, graw, GS):
    with ExitStack() as stack:
        s = Scope(nc, stack, "b_")
        NG = TILES * CHAINS
        BY_PE = 5
        dtb, alog, nea = s.sb("dtb", [P, CHAINS]), s.sb("alog", [P, CHAINS]), s.sb("nea", [P, CHAINS])
        a1, ab, e1, u1, d1, c1, r1, l1 = (s.sb(n, [P, TILES, CHAINS]) for n in ("a1", "ab", "e1", "u1", "d1", "c1", "r1", "l1"))
        g, eb, ub, beta = (s.sb(n, [P, TILES, CHAINS]) for n in ("g", "eb", "ub", "beta"))
        gcC, diff, gT = s.sb("gcC", [P, TILES, CHAINS]), s.sb("diff", [P, TILES, CHAINS]), s.sb("gT", [P, P])
        tri_le, tri_ge, ones = s.sb("tri_le", [P, P]), s.sb("tri_ge", [P, P]), s.sb("ones", [P, P])
        cwT, cw = s.sb("cwT", [TAPS * 12, P]), s.sb("cw", [P, TAPS, 12])
        diag = s.sb("diag", [P, BY_PE, TAPS, P])
        rawin = s.sb("rawin", [P, 12, TOKENS + 2 * HALO])
        acc = s.sb("acc", [P, 12 - BY_PE, TOKENS])
        sil = s.sb("sil", [P, 12, TOKENS])
        sq = s.sb("sq", [P, 8, TOKENS])
        ss, nrm, rn = (s.sb(n, [P, 2, GROUP, HEADS]) for n in ("ss", "nrm", "rn"))
        qt = s.sb("qt", [P, GROUP, QUAD])
        pk = s.sb("pk", [P, GROUP, 4, QUAD])
        ps = s.ps("ps", [P, 8, QUAD])

        loaded, cw_loaded, raw_loaded, packed_stored, gT_stored = (s.sem(n) for n in ("loaded", "cw_loaded", "raw_loaded", "packed_stored", "gT_stored"))
        shapes, sums, act_gate, dve_gate = s.sem("shapes"), s.sem("sums"), s.sem("act_gate"), s.sem("dve_gate")
        conv_turned, conv_ready, diag_ready = s.sem("conv_turned"), s.sem("conv_ready"), s.sem("diag_ready")

        turns = [f"v{j}" for j in range(GROUP)] + [f"{x}{j}" for j in range(GROUP) for x in "qk"] + [f"{x}{j}" for j in range(GROUP) for x in "QK"]
        banks = [5, 6, 7, 0, 1, 2, 3]
        SILU = [5, 0, 6, 1, 7, 2, 8, 3, 9, 10, 4, 11]
        SQ = [n for n in SILU if n < 8]
        assert sorted(SILU) == [*range(12)]
        pe = Steps(s.sem("pe_done"), [f"cv{n}" for n in range(BY_PE)] + ["ss"] + turns)
        act = Steps(s.sem("act_done"), [f"silu{n}" for n in SILU] + ["nrm"] + [f"v{j}" for j in range(GROUP)] + [f"Q{j}" for j in range(GROUP)])
        dve = Steps(s.sem("dve_done"), [f"cv{n}.{t}" for n in range(BY_PE, 12) for t in range(TAPS)] + ["ss", "rn", "rq"]
                    + [f"{x}{j}" for j in range(GROUP) for x in "qk"] + [f"K{j}" for j in range(GROUP)])
        pool = Steps(s.sem("pool_done"), [f"sq{n}" for n in SQ])

        def copied(job):
            return act if job[0] in "vQ" else dve

        block = stack.enter_context(nc.Block())
        raw_d = d["raw"].rearrange("p b h t -> p (b h) t")
        pk_d = d["pk"]
        gb_d = d["gb"]

        @block.sync
        def _(sp):
            sp.dma_start(rawin[:], raw_d[:, :, 0:TOKENS + 2 * HALO]).then_inc(raw_loaded, 16)
            sp.dma_start(dtb[:, 0:HEADS], d["dt_bias_f"].partition_broadcast(P)).then_inc(loaded, 16)
            sp.dma_start(dtb[:, HEADS:], d["dt_bias_b"].partition_broadcast(P)).then_inc(loaded, 16)
            sp.dma_start(alog[:, 0:HEADS], d["a_log_f"].partition_broadcast(P)).then_inc(loaded, 16)
            sp.dma_start(alog[:, HEADS:], d["a_log_b"].partition_broadcast(P)).then_inc(loaded, 16)
            sp.wait_ge(loaded, 64)
            sp.dma_start(cwT[:], d["conv_w"].rearrange("l t (n p) -> (l t n) p", p=P)).then_inc(cw_loaded, 16)
            sp.wait_ge(dve_gate, 19)
            sp.dma_start(gb_d, gT[:]).then_inc(gT_stored, 16)
            sp.wait_ge(gT_stored, 16)
            with sp.Fori(1, GROUPS) as gi:
                wait_alone(sp, (loaded, 64), *pe.at(gi - 1, f"cv{BY_PE - 1}"))
                wait_alone(sp, (loaded, 64), *dve.at(gi - 1, f"cv11.{TAPS - 1}"))
                sp.dma_start(rawin[:], raw_d[:, :, bass.ds(gi * TOKENS, TOKENS + 2 * HALO)]).then_inc(raw_loaded, 16)

        @block.gpsimd
        def _(gp):
            gp.memset(ones[:], 1.0).then_inc(shapes, 1)
            gp.wait_ge(shapes, 1)
            gp.affine_select(out=tri_le[:], in_=ones[:], pattern=[[1, P]], compare_op=ALU.is_ge, fill=0.0, base=0, channel_multiplier=-1).then_inc(shapes, 1)
            gp.affine_select(out=tri_ge[:], in_=ones[:], pattern=[[-1, P]], compare_op=ALU.is_ge, fill=0.0, base=0, channel_multiplier=1).then_inc(shapes, 1)
            pool.start(gp)
            with gp.Fori(0, GROUPS) as gi:
                gp.wait_ge(*pe.at(gi - 1, "ss"))
                for n in SQ:
                    gp.wait_ge(*act.at(gi, f"silu{n}"))
                    gp.tensor_tensor(sq[:, n], sil[:, n], sil[:, n], ALU.mult).then_inc(*pool.mark(f"sq{n}"))


        @block.tensor
        def _(te):
            te.wait_ge(cw_loaded, 16)
            te.transpose(ps[:, 1, 0:TAPS * 12], cwT[:], ident[0:TAPS * 12, 0:TAPS * 12]).then_inc(conv_turned, 1)
            te.wait_ge(shapes, 3)
            te.wait_ge(dve_gate, 12)
            te.matmul(ps[:, 0, 0:NG // 2], tri_le[:], g[:, :, 0:HEADS], start=True, stop=True)
            te.matmul(ps[:, 0, NG // 2:NG], tri_ge[:], g[:, :, HEADS:], start=True, stop=True)
            te.matmul(ps[:, 0, NG:2 * NG], ones[:], g[:], start=True, stop=True).then_inc(sums, 1)
            te.wait_ge(dve_gate, 16)
            te.transpose(ps[:, 2, 0:P], gcC[:].rearrange("p t c -> p (t c)"), ident[:]).then_inc(sums, 1)
            te.wait_ge(dve_gate, 19)
            te.wait_ge(diag_ready, BY_PE * TAPS)
            pe.start(te)
            with te.Fori(0, GROUPS) as gi:
                te.wait_ge(raw_loaded, gi * 16 + 16)
                te.wait_ge(*act.at(gi - 1, f"Q{GROUP - 1}"))
                te.wait_ge(*dve.at(gi - 1, f"K{GROUP - 1}"))
                for n in range(BY_PE):
                    if n >= 4:
                        te.wait_ge(*act.at(gi, f"silu{n - 4}"))
                    for t in range(TAPS):
                        m = te.matmul(ps[:, n % 4], diag[:, n, t], rawin[:, n, t:t + TOKENS], start=(t == 0), stop=(t == TAPS - 1))
                    m.then_inc(*pe.mark(f"cv{n}"))
                te.wait_ge(*pool.at(gi, f"sq{SQ[-1]}"))
                for n in range(8):
                    for j in range(GROUP):
                        at = (n // 4) * 16 + j * HEADS + n % 4
                        m = te.matmul(ps[:, 4, at:at + 1], sq[:, n, j * P:(j + 1) * P], ones[:, 0:1], start=True, stop=True)
                m.then_inc(*pe.mark("ss"))
                for i, job in enumerate(turns):
                    kind, j = job[0], int(job[1])
                    if i >= len(banks):
                        last = turns[i - len(banks)]
                        te.wait_ge(*copied(last).at(gi, last))
                    if i == 0:
                        te.wait_ge(*act.at(gi, f"silu{SILU[-1]}"))
                    if kind in "QK":
                        te.wait_ge(*dve.at(gi, kind.lower() + job[1]))
                        src = [(qt if kind == "Q" else pk[:, :, 2])[:, j, h * P:(h + 1) * P] for h in range(HEADS)]
                    else:
                        base = "qkv".index(kind) * HEADS
                        src = [sil[:, base + h, j * P:(j + 1) * P] for h in range(HEADS)]
                    for h in range(HEADS):
                        m = te.transpose(ps[:, banks[i % len(banks)], h * P:(h + 1) * P], src[h], ident[:])
                    m.then_inc(*pe.mark(job))

        @block.scalar
        def _(sc):
            sc.wait_ge(loaded, 64)
            sc.activation(nea[:], alog[:], ACT.Exp).then_inc(act_gate, 1)
            sc.activation(eb[:], graw[:, :, CHAINS:], ACT.Exp, scale=-1.0).then_inc(act_gate, 1)
            sc.wait_ge(dve_gate, 2)
            sc.activation(e1[:], ab[:], ACT.Exp, scale=-1.0).then_inc(act_gate, 1)
            sc.wait_ge(dve_gate, 3)
            sc.activation(l1[:], u1[:], ACT.Ln).then_inc(act_gate, 1)
            sc.wait_ge(dve_gate, 17)
            sc.activation(GS[:, :, EG], gcC[:], ACT.Exp).then_inc(act_gate, 1)
            sc.activation(GS[:, :, KD], diff[:], ACT.Exp).then_inc(act_gate, 1)
            sc.activation(GS[:, :, EL], ps[:, 0, NG:2 * NG].rearrange("p (t c) -> p t c", c=CHAINS), ACT.Exp).then_inc(act_gate, 1)
            act.start(sc)
            sc.sem_inc(packed_stored, 16)
            with sc.Fori(0, GROUPS) as gi:
                for n in SILU:
                    if n < BY_PE:
                        sc.wait_ge(*pe.at(gi, f"cv{n}"))
                        sc.activation(sil[:, n], ps[:, n % 4], ACT.Silu).then_inc(*act.mark(f"silu{n}"))
                    else:
                        sc.wait_ge(*dve.at(gi, f"cv{n}.{TAPS - 1}"))
                        sc.activation(sil[:, n], acc[:, n - BY_PE], ACT.Silu).then_inc(*act.mark(f"silu{n}"))
                sc.wait_ge(*dve.at(gi, "ss"))
                sc.activation(nrm[:], ss[:], ACT.Sqrt).then_inc(*act.mark("nrm"))
                sc.wait_ge(packed_stored, gi * 16 + 16)
                for j in range(GROUP):
                    sc.wait_ge(*pe.at(gi, f"v{j}"))
                    sc.activation(pk[:, j, 3], ps[:, banks[j]], ACT.Copy).then_inc(*act.mark(f"v{j}"))
                for j in range(GROUP):
                    sc.wait_ge(*pe.at(gi, f"Q{j}"))
                    sc.activation(pk[:, j, 1], ps[:, banks[turns.index(f"Q{j}") % len(banks)]], ACT.Copy).then_inc(*act.mark(f"Q{j}"))
                wait_alone(sc, (loaded, 64), *act.at(gi, f"Q{GROUP - 1}"))
                wait_alone(sc, (loaded, 64), *dve.at(gi, f"K{GROUP - 1}"))
                sc.dma_start(pk_d[bass.ds(gi * GROUP, GROUP)].rearrange("t p k c -> p t k c"), pk[:]).then_inc(packed_stored, 16)
            sc.wait_ge(packed_stored, 16 * GROUPS + 16)

        @block.vector
        def _(ve):
            count = [0]

            def gate(ins):
                count[0] += 1
                ins.then_inc(dve_gate, 1)
                ve.wait_ge(dve_gate, count[0])

            ve.wait_ge(loaded, 64)
            over_tiles = lambda ap: over_heads(ap, TILES)
            gate(ve.tensor_tensor(a1[:], graw[:, :, 0:CHAINS], over_tiles(dtb[:]), ALU.add))
            gate(ve.scalar_tensor_tensor(out=ab[:], in0=a1[:], scalar=-1.0, in1=a1[:], op0=ALU.mult, op1=ALU.max))
            ve.wait_ge(act_gate, 3)
            gate(ve.tensor_scalar(u1[:], e1[:], 1.0, None, ALU.add))
            gate(ve.tensor_scalar(d1[:], u1[:], -1.0, None, ALU.add))
            gate(ve.tensor_tensor(c1[:], e1[:], d1[:], ALU.subtract))
            gate(ve.reciprocal(r1[:], u1[:]))
            gate(ve.tensor_tensor(c1[:], c1[:], r1[:], ALU.mult))
            ve.wait_ge(act_gate, 4)
            gate(ve.tensor_tensor(l1[:], l1[:], c1[:], ALU.add))
            gate(ve.tensor_scalar(a1[:], a1[:], 0.0, None, ALU.max))
            gate(ve.tensor_tensor(a1[:], a1[:], l1[:], ALU.add))
            gate(ve.tensor_scalar(nea[:], nea[:], -1.0, None, ALU.mult))
            gate(ve.tensor_tensor(g[:], a1[:], over_tiles(nea[:]), ALU.mult))
            gate(ve.tensor_scalar(ub[:], eb[:], 1.0, None, ALU.add))
            gate(ve.reciprocal(beta[:], ub[:]))
            gate(ve.tensor_copy(GS[:, :, BETA], beta[:]))
            ve.wait_ge(sums, 1)
            ve.tensor_copy(gcC[:, :, 0:HEADS], ps[:, 0, 0:NG // 2].rearrange("p (t c) -> p t c", c=HEADS))
            gate(ve.tensor_copy(gcC[:, :, HEADS:], ps[:, 0, NG // 2:NG].rearrange("p (t c) -> p t c", c=HEADS)))
            gate(ve.tensor_tensor(diff[:], ps[:, 0, NG:2 * NG].rearrange("p (t c) -> p t c", c=CHAINS), gcC[:], ALU.subtract))
            gate(ve.tensor_copy(GS[:, :, GC], gcC[:]))
            ve.wait_ge(sums, 2)
            gate(ve.tensor_copy(gT[:], ps[:, 2, 0:P]))
            ve.wait_ge(act_gate, 7)
            gate(ve.scalar_tensor_tensor(out=GS[:, :, NBE], in0=beta[:], scalar=-1.0, in1=GS[:, :, EG], op0=ALU.mult, op1=ALU.mult))
            ve.wait_ge(conv_turned, 1)
            ve.tensor_copy(cw[:], ps[:, 1, 0:TAPS * 12].rearrange("p (t n) -> p t n", n=12)).then_inc(conv_ready, 1)
            ve.wait_ge(conv_ready, 1)
            for n in range(BY_PE):
                for t in range(TAPS):
                    ve.tensor_scalar(diag[:, n, t], ident[:], cw[:, t, n:n + 1], None, ALU.mult).then_inc(diag_ready, 1)
            dve.start(ve)
            with ve.Fori(0, GROUPS) as gi:
                ve.wait_ge(raw_loaded, gi * 16 + 16)
                for n in range(BY_PE, 12):
                    for t in range(TAPS):
                        if t == 0:
                            ve.tensor_scalar(acc[:, n - BY_PE], rawin[:, n, 0:TOKENS], cw[:, 0, n:n + 1], None, ALU.mult).then_inc(*dve.mark(f"cv{n}.0"))
                        else:
                            ve.wait_ge(*dve.at(gi, f"cv{n}.{t - 1}"))
                            ve.scalar_tensor_tensor(out=acc[:, n - BY_PE], in0=rawin[:, n, t:t + TOKENS], scalar=cw[:, t, n:n + 1],
                                                    in1=acc[:, n - BY_PE], op0=ALU.mult, op1=ALU.add).then_inc(*dve.mark(f"cv{n}.{t}"))
                ve.wait_ge(*pe.at(gi, "ss"))
                ve.tensor_scalar(ss[:], ps[:, 4, 0:32].rearrange("p (b j h) -> p b j h", b=2, j=GROUP), L2_EPS, None, ALU.add).then_inc(*dve.mark("ss"))
                ve.wait_ge(*act.at(gi, "nrm"))
                ve.reciprocal(rn[:], nrm[:]).then_inc(*dve.mark("rn"))
                ve.wait_ge(*dve.at(gi, "rn"))
                ve.tensor_scalar(rn[:, 0], rn[:, 0], float(P) ** -0.5, None, ALU.mult).then_inc(*dve.mark("rq"))
                ve.wait_ge(*dve.at(gi, "rq"))
                ve.wait_ge(packed_stored, gi * 16 + 16)
                for j in range(GROUP):
                    for b, kind in enumerate("qk"):
                        ve.wait_ge(*pe.at(gi, f"{kind}{j}"))
                        bank = banks[turns.index(f"{kind}{j}") % len(banks)]
                        ve.tensor_tensor(heads(qt[:, j] if b == 0 else pk[:, j, 2]), heads(ps[:, bank]), bcast(rn[:, b, j], P), ALU.mult).then_inc(*dve.mark(f"{kind}{j}"))
                for j in range(GROUP):
                    ve.wait_ge(*pe.at(gi, f"K{j}"))
                    ve.tensor_copy(pk[:, j, 0], ps[:, banks[turns.index(f"K{j}") % len(banks)]]).then_inc(*dve.mark(f"K{j}"))


MASK_OPS = 4 * 7 + 8
LEVELS = 7


def delta(nc, d, ident, GS, outs):
    with ExitStack() as stack:
        s = Scope(nc, stack, "d_")
        D2 = range(2)
        inp = [[s.sb(f"in{c}{b}", [P, 4, QUAD]) for b in D2] for c in D2]
        gb = [[s.sb(f"gb{c}{b}", [P, QUAD]) for b in D2] for c in D2]
        per = lambda name, shape=(P, QUAD): [s.sb(f"{name}{c}", list(shape)) for c in D2]
        twice = lambda name, shape=(P, QUAD): [[s.sb(f"{name}{c}{b}", list(shape)) for b in D2] for c in D2]
        sc_, A, QK = twice("sc", (P, KINDS, HEADS)), twice("A"), twice("QK")
        tmp1, tmp2, T0, Tt0 = per("tmp1"), per("tmp2"), per("T0"), per("Tt0")
        T, Tt, Pm = per("T"), per("Tt"), per("Pm")
        kbe, vb, kd, wT, vn, qv, S = per("kbe"), per("vb"), per("kd"), per("wT"), per("vn"), per("qv"), per("S")
        M = [s.sb(f"M{c}", [P, LEVELS, P]) for c in D2]
        far = [s.sb(f"far{c}", [P, P]) for c in D2]
        rowi, coli = s.sb("rowi", [P, 1], I32), s.sb("coli", [P, P], I32)
        shr, bit = s.sb("shr", [P, LEVELS], I32), s.sb("bit", [P, LEVELS], I32)
        shrf, bitf = s.sb("shrf", [P, LEVELS]), s.sb("bitf", [P, LEVELS])
        shcf, shc = (o[:].rearrange("p t m -> p (t m)")[:, 0:LEVELS * P].rearrange("p (l m) -> p l m", m=P) for o in outs)
        shc = shc.bitcast(I32)
        side, keep = s.sb("side", [P, 2, LEVELS]), s.sb("keep", [P, 2, LEVELS])
        ps = s.ps("ps", [P, 8, QUAD])

        loaded = [[s.sem(f"loaded{c}{b}") for b in D2] for c in D2]
        iotas, masks, far_ready, s_zero = s.sem("iotas"), s.sem("masks"), s.sem("far_ready"), s.sem("s_zero")
        H4 = range(HEADS)
        L = range(1, LEVELS)
        pe_prep = Steps(s.sem("pe_prep"), [f"{x}{c}" for x in ("G", "KQ", "Tt") for c in D2])
        act_prep = Steps(s.sem("act_prep"), [f"{x}{c}" for x in ("E1.", "E2.", "Tt") for c in D2])
        dve_prep = Steps(s.sem("dve_prep"), [f"sc{c}" for c in D2] + [f"{x}{c}.{h}" for x in ("tmp1.", "tmp2.", "A") for c in D2 for h in H4]
                         + [f"{x}{c}" for x in ("T0.", "QK") for c in D2])
        pool_prep = Steps(s.sem("pool_prep"), [f"A0.{c}" for c in D2])
        pe = Steps(s.sem("pe_done"), [f"{x}{l}.{c}" for l in L for x in (("P", "X", "T") if l < LEVELS - 1 else ("P", "X")) for c in D2]
                   + [f"{x}{c}" for x in ("wT", "U", "qS", "QV", "S") for c in D2])
        act = Steps(s.sem("act_done"), [f"T{l}.{c}" for l in L[:-1] for c in D2] + [f"{x}{c}" for x in ("wT", "vn", "qv") for c in D2])
        dve = Steps(s.sem("dve_done"), [f"{x}{l}.{c}" for l in L for x in ("P", "X") for c in D2])
        dve_end = Steps(s.sem("dve_end"), [f"{x}{c}.{h}" for x in ("S", "o") for c in D2 for h in H4])
        pool = Steps(s.sem("pool_done"), [f"{x}{c}" for c in D2 for x in ("kbe", "vb", "kd")])

        block = stack.enter_context(nc.Block())
        pk_d, gb_d = d["pk"], d["gb"].rearrange("(t c h) i -> t c (h i)", c=2, h=HEADS)
        chunk = lambda c, t: t if c == 0 else TILES - 1 - t
        col = lambda h: slice(h * P, (h + 1) * P)

        def steps(engine, body, peel_first=False):
            def turn(i, peeled):
                for b in D2:
                    body(i, b, 2 * i + b, 1 - b, 32 * i + (64 if b else 32), peeled and b == 1)
            if peel_first:
                turn(0, False)
            with engine.Fori(1 if peel_first else 0, TILES // 2 - 1) as i:
                turn(i, False)
            turn(TILES // 2 - 1, True)

        @block.sync
        def _(sp):
            def load(t, b):
                for c in D2:
                    sp.dma_start(inp[c][b][:], pk_d[bass.ds(chunk(c, t), 1)].rearrange("t p k c -> p (t k) c")).then_inc(loaded[c][b], 16)
                    sp.dma_start(gb[c][b][:], gb_d[bass.ds(chunk(c, t), 1), c].partition_broadcast(P)).then_inc(loaded[c][b], 16)

            load(0, 0)
            load(1, 1)
            sp.wait_ge(loaded[0][0], 32)
            with sp.Fori(1, TILES // 2) as i:
                for b in D2:
                    wait_alone(sp, (loaded[0][0], 32), *pe.at(2 * i + b - 2, "S1"))
                    load(2 * i + b, b)

        @block.gpsimd
        def _(gp):
            gp.iota(rowi[:], pattern=[[0, 1]], base=0, channel_multiplier=1).then_inc(iotas, 1)
            gp.iota(coli[:], pattern=[[1, P]], base=0, channel_multiplier=0).then_inc(iotas, 1)
            gp.memset(far[0][:], 0.0).then_inc(iotas, 1)
            gp.memset(far[1][:], 0.0).then_inc(iotas, 1)
            gp.wait_ge(iotas, 4)
            gp.affine_select(out=far[0][:], in_=far[0][:], pattern=[[-1, P]], compare_op=ALU.is_ge, fill=BIG, base=0, channel_multiplier=1).then_inc(far_ready, 1)
            gp.affine_select(out=far[1][:], in_=far[1][:], pattern=[[1, P]], compare_op=ALU.is_ge, fill=BIG, base=0, channel_multiplier=-1).then_inc(far_ready, 1)
            gp.wait_ge(masks, MASK_OPS)
            pool.start(gp)

            def first_merge(t, nb):
                for c in D2:
                    gp.wait_ge(*dve_prep.at(t, f"A{c}.{HEADS - 1}"))
                    gp.tensor_tensor(heads(T0[c][:]), heads(A[c][nb][:]), over_heads(M[c][:, 0]), ALU.mult).then_inc(*pool_prep.mark(f"A0.{c}"))

            def body(i, b, t, nb, loads, last):
                gp.wait_ge(*pe.at(t - 1, "S1"))
                for c in D2:
                    gp.wait_ge(*dve_prep.at(t - 1, f"sc{c}"))
                    gp.wait_ge(loaded[c][b], 32 * i + 32)
                    for name, out, kind, by in (("kbe", kbe, 2, NBE), ("vb", vb, 3, BETA), ("kd", kd, 2, KD)):
                        gp.tensor_tensor(heads(out[c][:]), heads(inp[c][b][:, kind]), bcast(sc_[c][b][:, by], P), ALU.mult).then_inc(*pool.mark(f"{name}{c}"))
                if not last:
                    first_merge(t, nb)

            first_merge(-1, 0)
            steps(gp, body)

        @block.tensor
        def _(te):
            pe.start(te)
            te.wait_ge(s_zero, 2)

            def quad(c, bank, done, lhsT, rhs):
                for h in H4:
                    m = te.matmul(ps[:, 4 * c + bank, col(h)], lhsT[:, col(h)], rhs[:, col(h)], start=True, stop=True)
                m.then_inc(*done)

            def turned(c, done, src):
                for h in H4:
                    m = te.transpose(ps[:, 4 * c + 2, col(h)], src[:, col(h)], ident[:])
                m.then_inc(*done)

            def prep_g(nb, loads, free):
                for c in D2:
                    te.wait_ge(loaded[c][nb], loads)
                    free(c)
                    quad(c, 3, pe_prep.mark(f"G{c}"), inp[c][nb][:, 0], inp[c][nb][:, 0])

            def prep_kq(t, nb):
                for c in D2:
                    te.wait_ge(*dve_prep.at(t, f"A{c}.3"))
                    quad(c, 3, pe_prep.mark(f"KQ{c}"), inp[c][nb][:, 0], inp[c][nb][:, 1])

            def prep_t(t, free):
                for c in D2:
                    free(c)
                    te.wait_ge(*dve_prep.at(t, f"T0.{c}"))
                    turned(c, pe_prep.mark(f"Tt{c}"), T0[c])

            def body(i, b, t, nb, loads, last):
                for l in L:
                    for c in D2:
                        te.wait_ge(*(act_prep.at(t - 1, f"Tt{c}") if l == 1 else act.at(t, f"T{l - 1}.{c}")))
                        quad(c, 0, pe.mark(f"P{l}.{c}"), A[c][b], (Tt0 if l == 1 else Tt)[c])
                    if not last and l == 3:
                        prep_g(nb, loads, lambda c: te.wait_ge(*dve_end.at(t - 1, f"o{c}.3")))
                    if not last and l == 5:
                        prep_kq(t, nb)
                    if not last and l == 6:
                        prep_t(t, lambda c: te.wait_ge(*act.at(t, f"T5.{c}")))
                    for c in D2:
                        te.wait_ge(*dve.at(t, f"P{l}.{c}"))
                        if l == 1:
                            te.wait_ge(*act.at(t - 1, f"qv{c}"))
                        quad(c, 1, pe.mark(f"X{l}.{c}"), (T0 if l == 1 else T)[c], Pm[c])
                    if l < LEVELS - 1:
                        for c in D2:
                            te.wait_ge(*dve.at(t, f"X{l}.{c}"))
                            if l == 1:
                                te.wait_ge(*dve_end.at(t - 1, f"S{c}.3"))
                            turned(c, pe.mark(f"T{l}.{c}"), Tt[c])
                for c in D2:
                    te.wait_ge(*dve.at(t, f"X{LEVELS - 1}.{c}"))
                    te.wait_ge(*pool.at(t, f"kd{c}"))
                    te.wait_ge(*(dve_end.at(t - 1, f"o{c}.3") if last else dve_prep.at(t, f"QK{c}")))
                    quad(c, 3, pe.mark(f"wT{c}"), kbe[c], Tt[c])
                for c in D2:
                    te.wait_ge(*act.at(t, f"wT{c}"))
                    te.wait_ge(*dve_end.at(t - 1, f"S{c}.3"))
                    for h in H4:
                        te.matmul(ps[:, 4 * c, col(h)], Tt[c][:, col(h)], vb[c][:, col(h)], start=True, stop=False)
                        m = te.matmul(ps[:, 4 * c, col(h)], wT[c][:, col(h)], S[c][:, col(h)], start=False, stop=True)
                    m.then_inc(*pe.mark(f"U{c}"))
                for c in D2:
                    quad(c, 3, pe.mark(f"qS{c}"), inp[c][b][:, 1], S[c])
                for c in D2:
                    te.wait_ge(*act.at(t, f"vn{c}"))
                    quad(c, 1, pe.mark(f"QV{c}"), QK[c][b], vn[c])
                for c in D2:
                    if not last:
                        te.wait_ge(*act_prep.at(t, f"Tt{c}"))
                    quad(c, 2, pe.mark(f"S{c}"), kd[c], vn[c])

            prep_g(0, 32, lambda c: None)
            prep_kq(-1, 0)
            prep_t(-1, lambda c: None)
            steps(te, body)

        @block.scalar
        def _(sc):
            act.start(sc)

            def copy(c, bank, out, done, made):
                sc.wait_ge(*made)
                sc.activation(out[:], ps[:, 4 * c + bank], ACT.Copy).then_inc(*done)

            def prep_e(t, which, tmp, scale):
                for c in D2:
                    sc.wait_ge(*dve_prep.at(t, f"tmp{which}.{c}.3"))
                    sc.activation(tmp[c][:], tmp[c][:], ACT.Exp, scale=scale).then_inc(*act_prep.mark(f"E{which}.{c}"))

            def prep_t(t):
                for c in D2:
                    copy(c, 2, Tt0[c], act_prep.mark(f"Tt{c}"), pe_prep.at(t, f"Tt{c}"))

            def body(i, b, t, nb, loads, last):
                for l in L[:-1]:
                    for c in D2:
                        copy(c, 2, T[c], act.mark(f"T{l}.{c}"), pe.at(t, f"T{l}.{c}"))
                    if not last and l == 2:
                        prep_e(t, 1, tmp1, -1.0)
                    if not last and l == 3:
                        prep_e(t, 2, tmp2, 1.0)
                if not last:
                    prep_t(t)
                for c in D2:
                    copy(c, 3, wT[c], act.mark(f"wT{c}"), pe.at(t, f"wT{c}"))
                for c in D2:
                    copy(c, 0, vn[c], act.mark(f"vn{c}"), pe.at(t, f"U{c}"))
                for c in D2:
                    sc.wait_ge(*dve_end.at(t - 1, f"o{c}.3"))
                    copy(c, 1, qv[c], act.mark(f"qv{c}"), pe.at(t, f"QV{c}"))

            prep_e(-1, 1, tmp1, -1.0)
            prep_e(-1, 2, tmp2, 1.0)
            prep_t(-1)
            steps(sc, body)

        @block.vector
        def _(ve):
            for c in D2:
                ve.memset(S[c][:], 0.0).then_inc(s_zero, 1)
            ve.wait_ge(iotas, 4)
            n = [0]

            def made(ins, need=True):
                n[0] += 1
                ins.then_inc(masks, 1)
                if need:
                    ve.wait_ge(masks, n[0])

            for l in range(LEVELS):
                made(ve.tensor_scalar(shr[:, l:l + 1], rowi[:], l, None, ALU.logical_shift_right), False)
                made(ve.tensor_scalar(shc[:, l], coli[:], l, None, ALU.logical_shift_right), l == LEVELS - 1)
            made(ve.tensor_scalar(bit[:], shr[:], 1, None, ALU.bitwise_and))
            ve.tensor_copy(bitf[:], bit[:])
            made(ve.tensor_copy(shrf[:], shr[:]), False)
            made(ve.tensor_copy(shcf[:], shc[:]))
            made(ve.tensor_scalar(side[:, 0], shrf[:], -1.0, None, ALU.add), False)
            made(ve.tensor_scalar(side[:, 1], shrf[:], 1.0, None, ALU.add), False)
            ve.tensor_copy(keep[:, 0], bitf[:])
            made(ve.tensor_scalar(keep[:, 1], bitf[:], -1.0, 1.0, ALU.mult, ALU.add))
            for c in D2:
                for l in range(LEVELS):
                    made(ve.tensor_scalar(M[c][:, l], shcf[:, l], side[:, c, l:l + 1], keep[:, c, l:l + 1], ALU.is_equal, ALU.mult), l == LEVELS - 1)
            for c in D2:
                made(ve.tensor_scalar(M[c][:, 0], M[c][:, 0], -1.0, None, ALU.mult), False)
            assert n[0] == MASK_OPS
            ve.wait_ge(far_ready, 2)
            dve.start(ve)
            dve_end.start(ve)

            def prep_sc(t, nb, free):
                free()
                for c in D2:
                    ve.tensor_copy(sc_[c][nb][:], GS[:, bass.ds(chunk(c, t + 1), 1), :, c * HEADS:(c + 1) * HEADS].rearrange("p t k h -> p (t k) h")).then_inc(*dve_prep.mark(f"sc{c}"))

            def prep_tmp(t, nb, loads, which, tmp, masks_, op):
                for c in D2:
                    ve.wait_ge(*dve_prep.at(t, f"sc{c}"))
                    ve.wait_ge(loaded[c][nb], loads)
                    for h in H4:
                        ve.scalar_tensor_tensor(out=tmp[c][:, col(h)], in0=gb[c][nb][:, col(h)], scalar=sc_[c][nb][:, GC, h:h + 1], in1=masks_[c][:],
                                                op0=ALU.subtract, op1=op).then_inc(*dve_prep.mark(f"tmp{which}.{c}.{h}"))

            def prep_a(t, nb):
                for c in D2:
                    ve.wait_ge(*pe_prep.at(t, f"G{c}"))
                    ve.wait_ge(*act_prep.at(t, f"E1.{c}"))
                    for h in H4:
                        ve.scalar_tensor_tensor(out=A[c][nb][:, col(h)], in0=ps[:, 4 * c + 3, col(h)], scalar=sc_[c][nb][:, BETA, h:h + 1], in1=tmp1[c][:, col(h)],
                                                op0=ALU.mult, op1=ALU.mult).then_inc(*dve_prep.mark(f"A{c}.{h}"))

            def prep_t(t):
                for c in D2:
                    ve.wait_ge(*pool_prep.at(t, f"A0.{c}"))
                    ve.tensor_tensor(heads(T0[c][:]), heads(T0[c][:]), over_heads(ident[:]), ALU.add).then_inc(*dve_prep.mark(f"T0.{c}"))

            def prep_qk(t, nb):
                for c in D2:
                    ve.wait_ge(*pe_prep.at(t, f"KQ{c}"))
                    ve.wait_ge(*act_prep.at(t, f"E2.{c}"))
                    ve.tensor_tensor(QK[c][nb][:], ps[:, 4 * c + 3], tmp2[c][:], ALU.mult).then_inc(*dve_prep.mark(f"QK{c}"))

            def update_state(t, b):
                for c in D2:
                    ve.wait_ge(*pe.at(t, f"S{c}"))
                    for h in H4:
                        ve.scalar_tensor_tensor(out=S[c][:, col(h)], in0=S[c][:, col(h)], scalar=sc_[c][b][:, EL, h:h + 1], in1=ps[:, 4 * c + 2, col(h)],
                                                op0=ALU.mult, op1=ALU.add).then_inc(*dve_end.mark(f"S{c}.{h}"))

            def output(t, b):
                for c in D2:
                    wait_alone(ve, (s_zero, 2), *act.at(t, f"qv{c}"))
                    for h in H4:
                        ve.scalar_tensor_tensor(out=outs[c][:, bass.ds(chunk(c, t), 1), col(h)].rearrange("p t m -> p (t m)"), in0=ps[:, 4 * c + 3, col(h)],
                                                scalar=sc_[c][b][:, EG, h:h + 1], in1=qv[c][:, col(h)], op0=ALU.mult, op1=ALU.add).then_inc(*dve_end.mark(f"o{c}.{h}"))

            def body(i, b, t, nb, loads, last):
                first = isinstance(t, int) and t == 0
                for l in L:
                    for c in D2:
                        ve.wait_ge(*pe.at(t, f"P{l}.{c}"))
                        ve.tensor_tensor(heads(Pm[c][:]), heads(ps[:, 4 * c]), over_heads(M[1 - c][:, l]), ALU.mult).then_inc(*dve.mark(f"P{l}.{c}"))
                    if l == 1 and not first:
                        update_state(t - 1, nb)
                    for c in D2:
                        ve.wait_ge(*pe.at(t, f"X{l}.{c}"))
                        ve.tensor_tensor(Tt[c][:], (Tt0 if l == 1 else Tt)[c][:], ps[:, 4 * c + 1], ALU.subtract).then_inc(*dve.mark(f"X{l}.{c}"))
                    if l == 1 and not first:
                        output(t - 1, nb)
                    if last:
                        continue
                    if l == 1:
                        def free():
                            wait_alone(ve, (s_zero, 2), *pool.at(t - 1, "kd1"))
                            wait_alone(ve, (s_zero, 2), *dve_end.at(t - 1, "o1.3"))
                            wait_alone(ve, (s_zero, 2), *dve_prep.at(t - 1, "QK1"))
                        prep_sc(t, nb, free)
                    if l == 2:
                        prep_tmp(t, nb, loads, 1, tmp1, far, ALU.add)
                    if l == 3:
                        prep_tmp(t, nb, loads, 2, tmp2, far[::-1], ALU.subtract)
                    if l == 4:
                        prep_a(t, nb)
                    if l == 5:
                        prep_t(t)
                        prep_qk(t, nb)
            prep_sc(-1, 0, lambda: None)
            prep_tmp(-1, 0, 32, 1, tmp1, far, ALU.add)
            prep_tmp(-1, 0, 32, 2, tmp2, far[::-1], ALU.subtract)
            prep_a(-1, 0)
            prep_t(-1)
            prep_qk(-1, 0)
            steps(ve, body, peel_first=True)
            update_state(TILES - 1, 1)
            output(TILES - 1, 1)


def mix(nc, d, ident, outs, logits):
    with ExitStack() as stack:
        s = Scope(nc, stack, "m_")
        RAW = 4
        raw = [s.sb(f"raw{r}", [P, D_MODEL]) for r in range(RAW)]
        whi, wlo = s.sb("whi", [P, KC, D_MODEL], F32R), s.sb("wlo", [P, KC, D_MODEL], F32R)
        ks = [*range(HEADS, KC), *range(HEADS)]
        wr = s.sb("wr", [P, KC, N_EXPERTS])
        x, z, sgu = s.sb("x", [P, D_MODEL]), s.sb("z", [P, QUAD]), s.sb("sgu", [P, QUAD])
        nw, lng, lnb = s.sb("nw", [P, P]), s.sb("lng", [P, D_MODEL]), s.sb("lnb", [P, D_MODEL])
        osum, sq, zn, oz = (s.sb(n, [P, QUAD]) for n in ("osum", "sq", "zn", "oz"))
        ohi, olo, shi, slo = (s.sb(n, [P, QUAD], F32R) for n in ("ohi", "olo", "shi", "slo"))
        ss, rms, rr = (s.sb(n, [P, HEADS]) for n in ("ss", "rms", "rr"))
        y, x1, x1T = s.sb("y", [P, D_MODEL]), s.sb("x1", [P, D_MODEL]), s.sb("x1T", [P, D_MODEL])
        stats, mv, var, std, rs = s.sb("stats", [P, 2, 6]), s.sb("mv", [P, 2]), s.sb("var", [P, 1]), s.sb("std", [P, 1]), s.sb("rs", [P, 1])
        spare = s.sb("spare", [P, 1])
        ps = s.ps("ps", [P, 8, QUAD])
        w_loaded, small_loaded, nw_loaded, whi_ready, wlo_ready = [s.sem(f"w_loaded{r}") for r in range(RAW)], *(s.sem(n) for n in ("small_loaded", "nw_loaded", "whi_ready", "wlo_ready"))
        x_loaded, z_loaded, sgu_loaded, x1_stored = (s.sem(n) for n in ("x_loaded", "z_loaded", "sgu_loaded", "x1_stored"))
        pre_dve = Steps(s.sem("pre_dve"), ["add", "ss", "ms", "rr", "on", "oz"])
        pre_act = Steps(s.sem("pre_act"), ["sq", "rms"])
        pre_pool = Steps(s.sem("pre_pool"), ["zn"])
        pe_y = Steps(s.sem("pe_y"), ["oT", "sgu", "y0", "y1"])
        act_oT, dve_oT = Steps(s.sem("act_oT"), ["hi"]), Steps(s.sem("dve_oT"), ["lo"])
        act_s, dve_s = Steps(s.sem("act_s"), ["hi"]), Steps(s.sem("dve_s"), ["lo"])
        post_dve = Steps(s.sem("post_dve"), ["y0", "y1", "st0", "st1", "mv", "ve", "rs", "nm"])
        post_act = Steps(s.sem("post_act"), ["std"])
        post_pool = Steps(s.sem("post_pool"), ["g", "b"])
        pe_r = Steps(s.sem("pe_r"), ["x1T0", "x1T1", "rt"])
        act_r = Steps(s.sem("act_r"), ["x1T0", "x1T1"])
        dve_r = Steps(s.sem("dve_r"), ["lg"])
        block = stack.enter_context(nc.Block())
        x_d = d["x"].rearrange("b (t p) c -> p (b t) c", p=P)
        row = lambda t: bass.ds(t, 1)

        @block.sync
        def _(sp):
            def loads(t):
                wait_alone(sp, (nw_loaded, 16), *pre_pool.at(t - 1, "zn"))
                sp.dma_start(z[:], d["z"][row(t)].rearrange("t p c -> p (t c)")).then_inc(z_loaded, 16)
                wait_alone(sp, (nw_loaded, 16), *dve_s.at(t - 1, "lo"))
                sp.dma_start(sgu[:], d["sgu"][row(t)].rearrange("t p c -> p (t c)")).then_inc(sgu_loaded, 16)
                wait_alone(sp, (nw_loaded, 16), *post_dve.at(t - 1, "y1"))
                sp.dma_start(x[:], x_d[:, row(t)].rearrange("p t c -> p (t c)")).then_inc(x_loaded, 16)

            def store(t):
                wait_alone(sp, (nw_loaded, 16), *post_pool.at(t, "b"))
                sp.dma_start(d["x1"][row(t)].rearrange("t p c -> p (t c)"), x1[:]).then_inc(x1_stored, 16)

            w_d = d["w_out"].rearrange("l (k p) c -> p (l k) c", p=P)
            for i, k in enumerate(ks):
                if i >= RAW:
                    sp.wait_ge(whi_ready, i - RAW + 1)
                    sp.wait_ge(wlo_ready, i - RAW + 1)
                sp.dma_start(raw[i % RAW][:], w_d[:, k]).then_inc(w_loaded[i % RAW], 16)
                if i == 0:
                    sp.wait_ge(nw_loaded, 16)
                    loads(0)
            sp.sem_inc(x1_stored, 16)
            with sp.Fori(1, TILES) as t:
                loads(t)
                store(t - 1)
            store(TILES - 1)
            sp.wait_ge(x1_stored, 16 * TILES + 16)

        @block.gpsimd
        def _(gp):
            for steps in (pre_pool, post_pool):
                steps.start(gp)
            gp.wait_ge(nw_loaded, 16)

            def pre(t):
                gp.wait_ge(z_loaded, t * 16 + 16)
                gp.wait_ge(*pre_dve.at(t - 1, "oz"))
                gp.tensor_tensor(heads(zn[:]), heads(z[:]), over_heads(nw[:]), ALU.mult).then_inc(*pre_pool.mark("zn"))

            def post(t):
                gp.wait_ge(small_loaded, 48)
                gp.wait_ge(*post_dve.at(t, "nm"))
                gp.tensor_tensor(x1[:], x1[:], lng[:], ALU.mult).then_inc(*post_pool.mark("g"))
                gp.wait_ge(*post_pool.at(t, "g"))
                gp.tensor_tensor(x1[:], x1[:], lnb[:], ALU.add).then_inc(*post_pool.mark("b"))

            pre(0)
            with gp.Fori(1, TILES) as t:
                pre(t)
                post(t - 1)
            post(TILES - 1)

        @block.tensor
        def _(te):
            pe_y.start(te)
            pe_r.start(te)
            def main(t):
                te.wait_ge(*pre_dve.at(t, "oz"))
                te.wait_ge(*act_oT.at(t - 1, "hi"))
                te.wait_ge(*dve_oT.at(t - 1, "lo"))
                for h in range(HEADS):
                    m = te.transpose(ps[:, 0, h * P:(h + 1) * P], oz[:, h * P:(h + 1) * P], ident[:])
                m.then_inc(*pe_y.mark("oT"))
                te.wait_ge(*dve_s.at(t, "lo"))
                te.wait_ge(*post_dve.at(t - 1, "y1"))
                first = isinstance(t, int) and t == 0

                def product(i, n, hi, lo):
                    k = ks[i]
                    h, cols = k % HEADS, slice(n * QUAD, (n + 1) * QUAD)
                    if first:
                        te.wait_ge(whi_ready, i + 1)
                        te.wait_ge(wlo_ready, i + 1)
                    return three_passes(te, ps[:, 1 + n], hi[:, h * P:(h + 1) * P], lo[:, h * P:(h + 1) * P], whi[:, k, cols], wlo[:, k, cols], i == 0, i == KC - 1)

                for i in range(HEADS):
                    for n in range(2):
                        m = product(i, n, shi, slo)
                m.then_inc(*pe_y.mark("sgu"))
                te.wait_ge(*dve_oT.at(t, "lo"))
                for n in range(2):
                    for i in range(HEADS, KC):
                        m = product(i, n, ohi, olo)
                    m.then_inc(*pe_y.mark(f"y{n}"))

            def router(t):
                te.wait_ge(small_loaded, 48)
                te.wait_ge(*post_pool.at(t, "b"))
                te.wait_ge(*act_r.at(t - 1, "x1T1"))
                for half in range(2):
                    for k in range(4):
                        c = half * 4 + k
                        m = te.transpose(ps[:, 5 + half, k * P:(k + 1) * P], x1[:, c * P:(c + 1) * P], ident[:])
                    m.then_inc(*pe_r.mark(f"x1T{half}"))
                te.wait_ge(*act_r.at(t, "x1T1"))
                te.wait_ge(*dve_r.at(t - 1, "lg"))
                for k in range(KC):
                    m = te.matmul(ps[:, 7, 0:N_EXPERTS], x1T[:, k * P:(k + 1) * P], wr[:, k], start=(k == 0), stop=(k == KC - 1))
                m.then_inc(*pe_r.mark("rt"))

            main(0)
            with te.Fori(1, TILES) as t:
                main(t)
                router(t - 1)
            router(TILES - 1)

        @block.scalar
        def _(sc):
            sc.dma_start(nw[:], d["delta_norm_w"].partition_broadcast(P)).then_inc(nw_loaded, 16)
            sc.dma_start(lng[:], d["ln1_g"].partition_broadcast(P)).then_inc(small_loaded, 16)
            sc.dma_start(lnb[:], d["ln1_b"].partition_broadcast(P)).then_inc(small_loaded, 16)
            sc.dma_start(wr[:], d["w_router"].rearrange("(k p) e -> p k e", p=P)).then_inc(small_loaded, 16)
            for steps in (pre_act, act_oT, act_s, post_act, act_r):
                steps.start(sc)

            def split_s(t):
                sc.wait_ge(sgu_loaded, t * 16 + 16)
                sc.wait_ge(*pe_y.at(t - 1, "sgu"))
                sc.wait_ge(*dve_s.at(t - 1, "lo"))
                sc.activation(shi[:], sgu[:], ACT.Copy).then_inc(*act_s.mark("hi"))

            def pre(t):
                sc.wait_ge(*pre_dve.at(t, "add"))
                sc.activation(sq[:], osum[:], ACT.Square).then_inc(*pre_act.mark("sq"))
                sc.wait_ge(*pre_dve.at(t, "ms"))
                sc.activation(rms[:], ss[:], ACT.Sqrt).then_inc(*pre_act.mark("rms"))

            def turned(t):
                sc.wait_ge(*pe_y.at(t, "oT"))
                sc.activation(ohi[:], ps[:, 0], ACT.Copy).then_inc(*act_oT.mark("hi"))

            def router(t):
                for half in range(2):
                    sc.wait_ge(*pe_r.at(t, f"x1T{half}"))
                    sc.activation(x1T[:, half * QUAD:(half + 1) * QUAD], ps[:, 5 + half], ACT.Copy).then_inc(*act_r.mark(f"x1T{half}"))

            def post(t):
                sc.wait_ge(*post_dve.at(t, "ve"))
                sc.activation(std[:], var[:], ACT.Sqrt).then_inc(*post_act.mark("std"))

            pre(0)
            split_s(0)
            for i, k in enumerate(ks):
                sc.wait_ge(w_loaded[i % RAW], 16 * (i // RAW + 1))
                sc.activation(whi[:, k], raw[i % RAW][:], ACT.Copy).then_inc(whi_ready, 1)
                if i == HEADS - 1:
                    turned(0)
            pre(1)
            split_s(1)
            post(0)
            with sc.Fori(1, TILES - 1) as t:
                turned(t)
                pre(t + 1)
                split_s(t + 1)
                router(t - 1)
                post(t)
            turned(TILES - 1)
            router(TILES - 2)
            post(TILES - 1)
            router(TILES - 1)

        @block.vector
        def _(ve):
            for steps in (pre_dve, dve_oT, dve_s, post_dve, dve_r):
                steps.start(ve)

            def split_s(t):
                ve.wait_ge(*act_s.at(t, "hi"))
                ve.tensor_tensor(slo[:], sgu[:], shi[:], ALU.subtract).then_inc(*dve_s.mark("lo"))

            def split_o(t):
                ve.wait_ge(*act_oT.at(t, "hi"))
                ve.tensor_tensor(olo[:], ps[:, 0], ohi[:], ALU.subtract).then_inc(*dve_oT.mark("lo"))

            def pre(t):
                ve.wait_ge(*pre_dve.at(t - 1, "oz"))
                ve.wait_ge(*pre_act.at(t - 1, "sq"))
                ve.tensor_tensor(osum[:], outs[0][:, row(t)].rearrange("p t c -> p (t c)"), outs[1][:, row(t)].rearrange("p t c -> p (t c)"), ALU.add).then_inc(*pre_dve.mark("add"))
                ve.wait_ge(*pre_act.at(t, "sq"))
                ve.tensor_reduce(ss[:], heads(sq[:]), AX.X, ALU.add).then_inc(*pre_dve.mark("ss"))
                ve.wait_ge(*pre_dve.at(t, "ss"))
                ve.tensor_scalar(ss[:], ss[:], 1.0 / P, RMS_EPS, ALU.mult, ALU.add).then_inc(*pre_dve.mark("ms"))
                ve.wait_ge(*pre_act.at(t, "rms"))
                ve.reciprocal(rr[:], rms[:]).then_inc(*pre_dve.mark("rr"))
                ve.wait_ge(*pre_dve.at(t, "rr"))
                ve.tensor_tensor(heads(osum[:]), heads(osum[:]), bcast(rr[:], P), ALU.mult).then_inc(*pre_dve.mark("on"))
                ve.wait_ge(*pre_dve.at(t, "on"))
                ve.wait_ge(*pre_pool.at(t, "zn"))
                ve.wait_ge(*pe_y.at(t - 1, "oT"))
                ve.tensor_tensor(oz[:], osum[:], zn[:], ALU.mult).then_inc(*pre_dve.mark("oz"))

            def post(t):
                ve.wait_ge(x_loaded, t * 16 + 16)
                ve.wait_ge(*post_dve.at(t - 1, "nm"))
                for half in range(2):
                    cols = slice(half * QUAD, (half + 1) * QUAD)
                    ve.wait_ge(*pe_y.at(t, f"y{half}"))
                    ve.scalar_tensor_tensor(out=y[:, cols], in0=x[:, cols], scalar=ALPHA, in1=ps[:, 1 + half], op0=ALU.mult, op1=ALU.add).then_inc(*post_dve.mark(f"y{half}"))
                for half in range(2):
                    ve.wait_ge(*post_dve.at(t, f"y{half}"))
                    ve.bn_stats(stats[:, half], y[:, half * QUAD:(half + 1) * QUAD]).then_inc(*post_dve.mark(f"st{half}"))
                ve.wait_ge(*post_dve.at(t, "st1"))
                ve.memset(spare[:], 0.0)
                ve.bn_aggr(mv[:], stats[:]).then_inc(*post_dve.mark("mv"))
                ve.wait_ge(*post_dve.at(t, "mv"))
                ve.tensor_scalar(var[:], mv[:, 1:2], LN_EPS, None, ALU.add).then_inc(*post_dve.mark("ve"))
                ve.wait_ge(*post_act.at(t, "std"))
                ve.reciprocal(rs[:], std[:]).then_inc(*post_dve.mark("rs"))
                ve.wait_ge(*post_dve.at(t, "rs"))
                ve.wait_ge(*pe_r.at(t - 1, "x1T1"))
                ve.wait_ge(x1_stored, t * 16 + 16)
                ve.tensor_scalar(x1[:], y[:], mv[:, 0:1], rs[:], ALU.subtract, ALU.mult).then_inc(*post_dve.mark("nm"))

            def router(t):
                ve.wait_ge(*pe_r.at(t, "rt"))
                ve.tensor_copy(logits[:, row(t)].rearrange("p t e -> p (t e)"), ps[:, 7, 0:N_EXPERTS]).then_inc(*dve_r.mark("lg"))

            pre(0)
            split_s(0)
            for i, k in enumerate(ks):
                ve.wait_ge(whi_ready, i + 1)
                ve.tensor_tensor(wlo[:, k], raw[i % RAW][:], whi[:, k], ALU.subtract).then_inc(wlo_ready, 1)
                if i == HEADS - 1:
                    split_o(0)
            pre(1)
            split_s(1)
            post(0)
            with ve.Fori(1, TILES - 1) as t:
                split_o(t)
                pre(t + 1)
                split_s(t + 1)
                post(t)
                router(t - 1)
            split_o(TILES - 1)
            post(TILES - 1)
            router(TILES - 2)
            router(TILES - 1)


PASS_SLOTS = 4
PASS_ROWS = PASS_SLOTS * P
PASS_SHIFT = PASS_ROWS.bit_length() - 1
SIZES = range(2 * P, PASS_ROWS + 1, P // 2)
PASSES = PAIRS // PASS_ROWS + N_EXPERTS - 1
COLS_P = PASSES + 1
COLS_T = COLS_P * PASS_SLOTS
E_NOW, FIELDS = 0, 1 + len(SIZES)


def route(nc, d, logits, gates, scatter, gather, plan, n_passes):
    with ExitStack() as stack:
        s = Scope(nc, stack, "r_")
        E = N_EXPERTS
        full = lambda name: s.sb(name, [P, TILES, E])
        sc, sel, cand, eq, mul, oh1, oh2, member, pos, inc, inc2, work = map(full, ("sc", "sel", "cand", "eq", "mul", "oh1", "oh2", "member", "pos", "inc", "inc2", "work"))
        rb = s.sb("rb", [P, E])
        pairmax, pairsum = s.sb("pairmax", [P, TILES * EXP_GROUPS]), s.sb("pairsum", [P, TILES * EXP_GROUPS])
        gsel, geq = s.sb("gsel", [P, TILES, EXP_GROUPS]), s.sb("geq", [P, TILES, EXP_GROUPS])
        gmax = s.sb("gmax", [P, TILES])
        wt16, wt4 = s.sb("wt16", [P, E]), s.sb("wt4", [P, EXP_GROUPS])
        iota_i = s.sb("iota_i", [P, P], I32)
        cols_f, cols_i = s.sb("cols_f", [P, P]), iota_i
        pid_i, pid = s.sb("pid_i", [P, TOP_K, TILES], I32), s.sb("pid", [P, TOP_K, TILES])
        part_i, part = s.sb("part_i", [P, 1], I32), s.sb("part", [P, 1])
        tri_lt, ones = s.sb("tri_lt", [P, P]), s.sb("ones", [P, P])
        s12 = s.sb("s12", [P, TOP_K, TILES])
        den, rden = s.sb("den", [P, TILES]), s.sb("rden", [P, TILES])
        cnt_i, cnt = s.sb("cnt_i", [P, E], I32), s.sb("cnt", [P, E])
        passes_n, pass_inc, pass_inc2, base = (s.sb(n, [P, E]) for n in ("passes_n", "pass_inc", "pass_inc2", "base"))
        posk, posk_i, row_i, slot_i = s.sb("posk", [P, TOP_K, TILES]), *(s.sb(n, [P, TOP_K, TILES], I32) for n in ("posk_i", "row_i", "slot_i"))
        row_f, slot_f = s.sb("row_f", [P, TOP_K * TILES]), s.sb("slot_f", [P, TOP_K * TILES])
        in_row, in_slot = s.sb("in_row", [P, TOP_K * TILES, P]), s.sb("in_slot", [P, TOP_K * TILES, COLS_T])
        empty, val, sc_f = s.sb("empty", [P, COLS_T]), s.sb("val", [P, COLS_T]), s.sb("sc_f", [P, COLS_T])
        past, mine, work_p = (s.sb(n, [P, COLS_P, E]) for n in ("past", "mine", "work_p"))
        spill_i, spill = s.sb("spill_i", [P, COLS_T], I32), s.sb("spill", [P, COLS_T])
        fields, rest, e_now = s.sb("fields", [P, COLS_P, FIELDS]), s.sb("rest", [P, COLS_P]), s.sb("e_now", [P, COLS_P])
        upto, all_rows = s.sb("upto", [P, COLS_P, len(SIZES)]), s.sb("all_rows", [P, E])
        ps = s.ps("ps", [P, 3, QUAD])
        loaded, shapes, scores_ready, step, sums, lists = (s.sem(n) for n in ("loaded", "shapes", "scores_ready", "step", "sums", "lists"))
        READY_MEMBER, READY_HOT = [None], [None]
        block = stack.enter_context(nc.Block())

        @block.sync
        def _(sp):
            sp.dma_start(rb[:], d["router_bias"].rearrange("(o e) -> o e", o=1).partition_broadcast(P)).then_inc(loaded, 16)
            sp.wait_ge(loaded, 16)

        @block.gpsimd
        def _(gp):
            gp.iota(iota_i[:], pattern=[[1, P]], base=0, channel_multiplier=0).then_inc(shapes, 1)
            gp.iota(pid_i[:], pattern=[[SEQ, TOP_K], [P, TILES]], base=1, channel_multiplier=1).then_inc(shapes, 1)
            gp.iota(part_i[:], pattern=[[0, 1]], base=PAIRS + 1, channel_multiplier=1).then_inc(shapes, 1)
            gp.memset(ones[:], 1.0).then_inc(shapes, 1)
            gp.wait_ge(shapes, 4)
            gp.affine_select(out=tri_lt[:], in_=ones[:], pattern=[[1, P]], compare_op=ALU.is_gt, fill=0.0, base=0, channel_multiplier=-1).then_inc(shapes, 1)

        @block.scalar
        def _(ac):
            ac.activation(sc[:], logits[:], ACT.Sigmoid).then_inc(scores_ready, 1)

        @block.vector
        def _(ve):
            n = [0]

            def do(ins):
                n[0] += 1
                ins.then_inc(step, 1)
                ve.wait_ge(step, n[0])

            def tt(out, a, b, op):
                do(ve.tensor_tensor(out, a, b, op))

            def ts(out, a, s1, op0, s2=None, op1=None):
                do(ve.tensor_scalar(out, a, s1, s2, op0) if op1 is None else ve.tensor_scalar(out, a, s1, s2, op0, op1))

            tiled = lambda ap: over_heads(ap, TILES)
            ve.wait_ge(shapes, 5)
            ve.wait_ge(loaded, 16)
            do(ve.tensor_copy(cols_f[:], cols_i[:]))
            do(ve.tensor_copy(pid[:], pid_i[:]))
            do(ve.tensor_copy(part[:], part_i[:]))
            ts(wt16[:], cols_f[:, 0:E], -1.0, ALU.mult, float(E), ALU.add)
            ts(wt4[:], cols_f[:, 0:EXP_GROUPS], -1.0, ALU.mult, float(EXP_GROUPS), ALU.add)
            ve.wait_ge(scores_ready, 1)
            tt(sel[:], sc[:], tiled(rb[:]), ALU.add)
            member4 = sel[:].rearrange("p t (g m) -> p (t g) m", m=PER_GROUP)
            first = True
            for i in range(PER_GROUP):
                for j in range(i + 1, PER_GROUP):
                    out = pairmax if first else pairsum
                    tt(out[:], member4[:, :, i], member4[:, :, j], ALU.add)
                    if not first:
                        tt(pairmax[:], pairmax[:], pairsum[:], ALU.max)
                    first = False
            group4 = pairmax[:].rearrange("p (t g) -> p t g", g=EXP_GROUPS)

            def first_max(values, weights, width, eq_, out, top):
                do(ve.tensor_reduce(top[:], values, AX.X, ALU.max))
                tt(eq_, values, bcast(top[:], width), ALU.is_equal)
                tt(eq_, eq_, tiled(weights), ALU.mult)
                do(ve.tensor_reduce(top[:], eq_, AX.X, ALU.max))
                tt(out, eq_, bcast(top[:], width), ALU.is_equal)

            first_max(group4, wt4[:], EXP_GROUPS, geq[:], gsel[:], gmax)
            in_group = bcast(gsel[:].rearrange("p t g -> p (t g)"), PER_GROUP)
            flat4 = lambda ap: ap.rearrange("p t (g m) -> p (t g) m", m=PER_GROUP)
            tt(flat4(cand[:]), flat4(sel[:]), in_group, ALU.mult)
            do(ve.tensor_copy(flat4(mul[:]), in_group))
            ts(mul[:], mul[:], BIG, ALU.mult, -BIG, ALU.add)
            tt(cand[:], cand[:], mul[:], ALU.add)
            first_max(cand[:], wt16[:], E, eq[:], oh1[:], gmax)
            do(ve.scalar_tensor_tensor(out=cand[:], in0=oh1[:], scalar=-4.0 * BIG, in1=cand[:], op0=ALU.mult, op1=ALU.add))
            first_max(cand[:], wt16[:], E, eq[:], oh2[:], gmax)
            for k, oh in enumerate((oh1, oh2)):
                tt(work[:], sc[:], oh[:], ALU.mult)
                do(ve.tensor_reduce(s12[:, k], work[:], AX.X, ALU.add))
            tt(den[:], s12[:, 0], s12[:, 1], ALU.add)
            do(ve.reciprocal(rden[:], den[:]))
            for k in range(TOP_K):
                tt(gates[:, k], s12[:, k], rden[:], ALU.mult)
            tt(member[:], oh1[:], oh2[:], ALU.add)
            READY_MEMBER[0] = n[0]
            ve.wait_ge(sums, 1)
            do(ve.tensor_copy(inc[:].rearrange("p t e -> p (t e)"), ps[:, 1, 0:TILES * E]))
            a, b = inc, inc2
            shift = 1
            while shift < TILES:
                do(ve.tensor_copy(b[:, 0:shift], a[:, 0:shift]))
                tt(b[:, shift:], a[:, shift:], a[:, 0:TILES - shift], ALU.add)
                a, b = b, a
                shift *= 2
            ts(cnt[:], a[:, TILES - 1], float(PASS_ROWS - 1), ALU.add)
            do(ve.tensor_copy(cnt_i[:], cnt[:]))
            ts(cnt_i[:], cnt_i[:], PASS_SHIFT, ALU.logical_shift_right)
            do(ve.tensor_copy(passes_n[:], cnt_i[:]))
            do(ve.tensor_copy(pass_inc[:], passes_n[:]))
            c, c2 = pass_inc, pass_inc2
            shift = 1
            while shift < E:
                do(ve.tensor_copy(c2[:, 0:shift], c[:, 0:shift]))
                tt(c2[:, shift:], c[:, shift:], c[:, 0:E - shift], ALU.add)
                c, c2 = c2, c
                shift *= 2
            tt(base[:], c[:], passes_n[:], ALU.subtract)
            ts(base[:], base[:], float(PASS_ROWS), ALU.mult)
            tt(all_rows[:], base[:], a[:, TILES - 1], ALU.add)
            tt(pos[:].rearrange("p t e -> p (t e)"), a[:].rearrange("p t e -> p (t e)"), ps[:, 1, 0:TILES * E], ALU.subtract)
            tt(pos[:].rearrange("p t e -> p (t e)"), pos[:].rearrange("p t e -> p (t e)"), ps[:, 0, 0:TILES * E], ALU.add)
            tt(pos[:], pos[:], tiled(base[:]), ALU.add)
            for k, oh in enumerate((oh1, oh2)):
                tt(work[:], pos[:], oh[:], ALU.mult)
                do(ve.tensor_reduce(posk[:, k], work[:], AX.X, ALU.add))
            do(ve.tensor_copy(posk_i[:], posk[:]))
            ts(row_i[:], posk_i[:], P - 1, ALU.bitwise_and)
            ts(slot_i[:], posk_i[:], 7, ALU.logical_shift_right)
            do(ve.tensor_copy(row_f[:], row_i[:].rearrange("p k t -> p (k t)")))
            do(ve.tensor_copy(slot_f[:], slot_i[:].rearrange("p k t -> p (k t)")))
            every = TOP_K * TILES
            tt(in_row[:], over_heads(cols_f[:], every), bcast(row_f[:], P), ALU.is_equal)
            tt(in_slot[:], over_heads(cols_f[:, 0:COLS_T], every), bcast(slot_f[:], COLS_T), ALU.is_equal)
            tt(in_slot[:], in_slot[:], bcast(pid[:].rearrange("p k t -> p (k t)"), COLS_T), ALU.mult)
            READY_HOT[0] = n[0]
            passes = cols_f[:, 0:COLS_P]
            tt(past[:], over_heads(c[:], COLS_P), bcast(passes, E), ALU.is_le)
            do(ve.tensor_reduce(e_now[:], past[:], AX.X, ALU.add))
            do(ve.tensor_scalar(fields[:, :, E_NOW], e_now[:], float(E - 1), None, ALU.min))
            tt(mine[:], over_heads(cols_f[:, 0:E], COLS_P), bcast(e_now[:], E), ALU.is_equal)
            tt(mine[:], mine[:], over_heads(all_rows[:], COLS_P), ALU.mult)
            do(ve.tensor_reduce(rest[:], mine[:], AX.X, ALU.add))
            do(ve.scalar_tensor_tensor(out=rest[:], in0=passes, scalar=-float(PASS_ROWS), in1=rest[:], op0=ALU.mult, op1=ALU.add))
            for i, size in enumerate(SIZES[:-1]):
                ts(upto[:, :, i], rest[:], float(size), ALU.is_le)
            ts(upto[:, :, len(SIZES) - 1], rest[:], BIG, ALU.is_le)
            do(ve.tensor_copy(fields[:, :, 1], upto[:, :, 0]))
            tt(fields[:, :, 2:], upto[:, :, 1:], upto[:, :, 0:len(SIZES) - 1], ALU.subtract)
            do(ve.tensor_copy(plan[:], fields[:]))
            do(ve.tensor_copy(n_passes[:], c[:, E - 1:E]))
            ts(spill_i[:], cols_i[:, 0:COLS_T], PASS_SLOTS - 1, ALU.bitwise_and)
            do(ve.tensor_copy(spill[:], spill_i[:]))
            ts(spill[:], spill[:], float(P), ALU.mult, part[:], ALU.add)
            ve.wait_ge(lists, 1)
            do(ve.tensor_copy(val[:], ps[:, 2, 0:COLS_T]))
            ts(empty[:], val[:], 0.0, ALU.is_equal)
            ts(val[:], val[:], -1.0, ALU.add)
            tt(sc_f[:], empty[:], spill[:], ALU.mult)
            tt(sc_f[:], sc_f[:], val[:], ALU.add)
            do(ve.tensor_copy(scatter[:], sc_f[:]))
            ts(gather[:], scatter[:], SEQ - 1, ALU.bitwise_and)

        @block.tensor
        def _(te):
            te.wait_ge(shapes, 5)
            te.wait_ge(step, ROUTE_MEMBER)
            te.matmul(ps[:, 0, 0:TILES * E], tri_lt[:], member[:], start=True, stop=True)
            te.matmul(ps[:, 1, 0:TILES * E], ones[:], member[:], start=True, stop=True).then_inc(sums, 1)
            te.wait_ge(step, ROUTE_HOT)
            every = TOP_K * TILES
            for i in range(every):
                m = te.matmul(ps[:, 2, 0:COLS_T], in_row[:, i], in_slot[:, i], start=(i == 0), stop=(i == every - 1))
            m.then_inc(lists, 1)

        assert (READY_MEMBER[0], READY_HOT[0]) == (ROUTE_MEMBER, ROUTE_HOT), (READY_MEMBER, READY_HOT)


ROUTE_MEMBER, ROUTE_HOT = 46, 86


def experts(nc, d, ident, scatter, gather, plan, n_passes):
    with ExitStack() as stack:
        s = Scope(nc, stack, "e_")
        CW = 2 * P
        GU = 2 * D_MODEL // CW
        CHUNKS = 3 * D_MODEL // CW
        RAW, SPLIT = 4, 4
        F = range(D_MODEL // CW)
        S4, K8 = range(PASS_SLOTS), range(KC)
        raw = [s.sb(f"raw{r}", [P, KC, CW]) for r in range(RAW)]
        whi = [s.sb(f"whi{r}", [P, KC, CW], F32R) for r in range(SPLIT)]
        wlo = [s.sb(f"wlo{r}", [P, KC, CW], F32R) for r in range(SPLIT)]
        xhi, xlo = s.sb("xhi", [P, KC, PASS_ROWS], F32R), s.sb("xlo", [P, KC, PASS_ROWS], F32R)
        hhi, hlo = s.sb("hhi", [P, KC, PASS_ROWS], F32R), s.sb("hlo", [P, KC, PASS_ROWS], F32R)
        hs, h = ([s.sb(f"{n}{b}", [P, PASS_ROWS]) for b in range(2)] for n in ("hs", "h"))
        xg, y = s.sb("xg", [P, PASS_SLOTS, D_MODEL]), s.sb("y", [P, PASS_SLOTS, D_MODEL])
        g_now, s_now = s.sb("g_now", [P, PASS_SLOTS], I32), s.sb("s_now", [P, PASS_SLOTS], I32)
        spare = s.sb("spare", [P, 1])
        ps = s.ps("ps", [P, 8, QUAD])
        raw_loaded = [s.sem(f"raw_loaded{r}") for r in range(RAW)]
        gathered, scattered, idx_g, idx_s, y_zero = (s.sem(n) for n in ("gathered", "scattered", "idx_g", "idx_s", "y_zero"))
        ps_zero = s.sem("ps_zero")
        order = [*range(SPLIT, CHUNKS), *range(SPLIT)]
        xs = [f"x{c}" for c in K8]
        pe = Steps(s.sem("pe_done"), [f"{m}{2 * f + i}" for f in F for m in "gu" for i in range(2)] + [f"y{c}" for c in F])
        pe_x = Steps(s.sem("pe_x"), xs)
        act_split, dve_split = Steps(s.sem("act_split"), [f"w{i}" for i in order]), Steps(s.sem("dve_split"), [f"w{i}" for i in order])
        act_x, dve_x = Steps(s.sem("act_x"), xs), Steps(s.sem("dve_x"), xs)
        act = Steps(s.sem("act_done"), [f"{n}{2 * f + i}" for f in F for n in ("silu", "hi") for i in range(2)] + ["ya0", "ya1", "yb0", "yb1"])
        dve = Steps(s.sem("dve_done"), [f"{n}{2 * f + i}" for f in F for n in ("h", "lo") for i in range(2)] + ["ya2", "ya3", "yb2", "yb3"])
        block = stack.enter_context(nc.Block())
        w_d = [d[n].rearrange("l e (k p) f -> p (l e) k f", p=P) for n in ("w_gate", "w_up", "w_down")]
        x1_d = d["x1"].rearrange("t p c -> (t p) c")

        def count(engine):
            return engine.value_load(n_passes[0:1, 0:1], min_val=1, max_val=PASSES)

        def field(engine, p, f, top):
            return engine.value_load(plan[0:1, bass.ds(p, 1), f:f + 1].rearrange("p t f -> p (t f)"), min_val=0, max_val=top)

        def turn_of(p, i):
            return p - 1 if i < SPLIT else p

        def freed(p, i):
            return pe.at(p, f"g{i + 1}" if i < GU and i % 2 == 0 else f"u{i}" if i < GU else f"y{i - GU}")

        def used_before(p, i):
            return freed(p, i - SPLIT) if i >= SPLIT else freed(p - 1, i + CHUNKS - SPLIT)

        @block.sync
        def _(sp):
            passes = count(sp)
            met = (raw_loaded[0], 16)

            def load(e, i):
                src = w_d[i % 2] if i < GU else w_d[2]
                c = i // 2 if i < GU else i - GU
                sp.dma_start(raw[i % RAW][:], src[:, bass.ds(e, 1), :, c * CW:(c + 1) * CW].rearrange("p e k f -> p (e k) f")).then_inc(raw_loaded[i % RAW], 16)

            e0 = field(sp, 0, E_NOW, N_EXPERTS - 1)
            load(e0, 0)
            sp.wait_ge(gathered, 64)
            for i in range(1, RAW):
                load(e0, i)
            sp.wait_ge(*met)
            with sp.Fori(0, passes) as p:
                now, nxt = field(sp, p, E_NOW, N_EXPERTS - 1), field(sp, p + 1, E_NOW, N_EXPERTS - 1)
                for i in order:
                    ahead = 0 if i >= SPLIT else 1
                    j, q = (i - RAW, p) if i >= RAW else (i - RAW + CHUNKS, p)
                    wait_alone(sp, met, *act_split.at(turn_of(q, j), f"w{j}"))
                    wait_alone(sp, met, *dve_split.at(turn_of(q, j), f"w{j}"))
                    load(nxt if ahead else now, i)

        @block.gpsimd
        def _(gp):
            passes = count(gp)

            def rows(out, lists, p, sem):
                gp.tensor_copy(out[:], lists[:, bass.ds(p * PASS_SLOTS, PASS_SLOTS)]).then_inc(sem, 1)

            def gather_rows():
                for j in S4:
                    gp.indirect_dma_start(out=xg[:, j], out_offset=None, in_=x1_d, in_offset=bass.IndirectOffsetOnAxis(ap=g_now[:, j:j + 1], axis=0)).then_inc(gathered, 16)

            rows(g_now, gather, 0, idx_g)
            gp.wait_ge(idx_g, 1)
            gather_rows()
            gp.memset(y[:, 0], 0.0).then_inc(y_zero, 1)
            gp.wait_ge(y_zero, 1)
            gp.indirect_dma_start(out=d["ybuf"], out_offset=bass.IndirectOffsetOnAxis(ap=scatter[:, COLS_T - 1:COLS_T], axis=0), in_=y[:, 0], in_offset=None).then_inc(scattered, 16)
            first = (gathered, 64)
            gp.wait_ge(*first)
            with gp.Fori(0, passes) as p:
                wait_alone(gp, first, gathered, p * 64 + 64)
                rows(g_now, gather, p + 1, idx_g)
                wait_alone(gp, first, *pe_x.at(p - 1, "x7"))
                wait_alone(gp, first, idx_g, p + 2)
                gather_rows()
                wait_alone(gp, first, scattered, p * 64 + 16)
                rows(s_now, scatter, p, idx_s)
                wait_alone(gp, first, idx_s, p + 1)
                wait_alone(gp, first, *act.at(p, "yb1"))
                wait_alone(gp, first, *dve.at(p, "yb3"))
                for j in S4:
                    gp.indirect_dma_start(out=d["ybuf"], out_offset=bass.IndirectOffsetOnAxis(ap=s_now[:, j:j + 1], axis=0), in_=y[:, j], in_offset=None).then_inc(scattered, 16)

        @block.tensor
        def _(te):
            passes = count(te)
            pe.start(te)
            te.wait_ge(ps_zero, 1)

            def turn_x(p, cs):
                if cs[0] == 0 and len(cs) < KC:
                    te.wait_ge(*act.at(p, "ya1"))
                    te.wait_ge(*dve.at(p, "ya3"))
                for c in cs:
                    if c >= 4:
                        te.wait_ge(*act_x.at(p, f"x{c - 4}"))
                        te.wait_ge(*dve_x.at(p, f"x{c - 4}"))
                    for j in S4:
                        m = te.transpose(ps[:, 4 + c % 4, j * P:(j + 1) * P], xg[:, j, c * P:(c + 1) * P], ident[:])
                    m.then_inc(*pe_x.mark(f"x{c}"))

            def split_ready(p, i):
                te.wait_ge(*act_split.at(turn_of(p, i), f"w{i}"))
                te.wait_ge(*dve_split.at(turn_of(p, i), f"w{i}"))

            def gate_up(p, n):
                for f in F:
                    for mat, name in enumerate("gu"):
                        i = 2 * f + mat
                        split_ready(p, i)
                        for sub in range(2):
                            if f:
                                te.wait_ge(*(act.at(p, f"silu{2 * f - 2 + sub}") if mat == 0 else dve.at(p, f"h{2 * f - 2 + sub}")))
                            else:
                                te.wait_ge(*(act if mat == 0 else dve).at(p - 1, f"yb{2 * mat + sub}"))
                            cols = slice(sub * P, (sub + 1) * P)
                            for k in K8:
                                if i == 0 and sub == 0:
                                    te.wait_ge(*act_x.at(p - 1, f"x{k}"))
                                    te.wait_ge(*dve_x.at(p - 1, f"x{k}"))
                                m = three_passes(te, ps[:, 2 * mat + sub, 0:n], whi[i % SPLIT][:, k, cols], wlo[i % SPLIT][:, k, cols], xhi[:, k, 0:n], xlo[:, k, 0:n], k == 0, k == KC - 1)
                            m.then_inc(*pe.mark(f"{name}{2 * f + sub}"))

            def down(p, size, c):
                i = GU + c
                split_ready(p, i)
                for k in K8:
                    if c == 0:
                        te.wait_ge(*act.at(p, f"hi{k}"))
                        te.wait_ge(*dve.at(p, f"lo{k}"))
                    for j in range(-(-size // P)):
                        rows = slice(j * P, (j + 1) * P)
                        m = three_passes(te, ps[:, (4 if c < 2 else 0) + j, (c % 2) * CW:(c % 2 + 1) * CW], hhi[:, k, rows], hlo[:, k, rows], whi[i % SPLIT][:, k], wlo[i % SPLIT][:, k], k == 0, k == KC - 1)
                m.then_inc(*pe.mark(f"y{c}"))

            def by_size(flags, body):
                n = pe.n
                for size, flag in zip(SIZES, flags):
                    pe.n = n
                    with te.If(flag):
                        body(size)

            te.wait_ge(gathered, 64)
            turn_x(-1, K8)
            with te.Fori(0, passes) as p:
                flags = [field(te, p, 1 + i, 1) for i in range(len(SIZES))]
                by_size(flags, lambda size: gate_up(p, size))
                by_size(flags, lambda size: (down(p, size, 0), down(p, size, 1), down(p, size, 2)))
                te.wait_ge(gathered, p * 64 + 128)
                turn_x(p, K8[0:4])
                by_size(flags, lambda size: down(p, size, 3))
                turn_x(p, K8[4:8])

        def raw_ready(engine, p, i):
            engine.wait_ge(raw_loaded[i % RAW], (p * (CHUNKS // RAW) + i // RAW + 1) * 16)
            engine.wait_ge(*used_before(p, i))

        def copy_y(engine, p, part, steps, tiles, copy):
            engine.wait_ge(*pe.at(p, "y1" if part == "a" else "y3"))
            if part == "a":
                engine.wait_ge(scattered, p * 64 + 16)
            for j in tiles:
                bank, half = (4 + j, 0) if part == "a" else (j, 1)
                copy(y[:, j, half * QUAD:(half + 1) * QUAD], ps[:, bank]).then_inc(*steps.mark(f"y{part}{j}"))

        @block.scalar
        def _(sc):
            passes = count(sc)
            act.start(sc)
            act_split.start(sc, but=SPLIT)

            def split(p, i):
                raw_ready(sc, p, i)
                q, j = (p, i - SPLIT) if i >= SPLIT else (p - 1, i + CHUNKS - SPLIT)
                sc.wait_ge(*dve_split.at(turn_of(q, j), f"w{j}"))
                sc.activation(whi[i % SPLIT][:], raw[i % RAW][:], ACT.Copy).then_inc(*act_split.mark(f"w{i}"))

            def split_x(p, cs):
                for c in cs:
                    sc.wait_ge(*pe_x.at(p, f"x{c}"))
                    sc.activation(xhi[:, c], ps[:, 4 + c % 4], ACT.Copy).then_inc(*act_x.mark(f"x{c}"))

            for i in range(SPLIT):
                if i == 1:
                    split_x(-1, K8)
                sc.wait_ge(raw_loaded[i], 16)
                sc.activation(whi[i][:], raw[i][:], ACT.Copy).then_inc(*act_split.mark(f"w{i}"))
            with sc.Fori(0, passes) as p:
                for f in F:
                    for n in (2 * f, 2 * f + 1):
                        sc.wait_ge(*pe.at(p, f"g{n}"))
                        sc.wait_ge(*(dve.at(p, f"h{n - 2}") if n >= 2 else dve.at(p - 1, f"h{n + 6}")))
                        sc.activation(hs[n % 2][:], ps[:, n % 2], ACT.Silu).then_inc(*act.mark(f"silu{n}"))
                    split(p, 2 * f + SPLIT)
                    for n in (2 * f, 2 * f + 1):
                        sc.wait_ge(*dve.at(p, f"h{n}"))
                        sc.activation(hhi[:, n], h[n % 2][:], ACT.Copy).then_inc(*act.mark(f"hi{n}"))
                    split(p, 2 * f + 1 + SPLIT)
                split(p + 1, 0)
                copy_y(sc, p, "a", act, (0, 1), lambda *io: sc.activation(*io, ACT.Copy))
                split(p + 1, 1)
                split_x(p, K8[0:4])
                split(p + 1, 2)
                copy_y(sc, p, "b", act, (0, 1), lambda *io: sc.activation(*io, ACT.Copy))
                split_x(p, K8[4:8])
                split(p + 1, 3)

        @block.vector
        def _(ve):
            passes = count(ve)
            dve.start(ve)
            dve_split.start(ve, but=SPLIT)
            ve.memset(ps[:], 0.0).then_inc(ps_zero, 1)

            def split(p, i):
                raw_ready(ve, p, i)
                ve.wait_ge(*act_split.at(turn_of(p, i), f"w{i}"))
                ve.tensor_tensor(wlo[i % SPLIT][:], raw[i % RAW][:], whi[i % SPLIT][:], ALU.subtract).then_inc(*dve_split.mark(f"w{i}"))

            def split_x(p, cs):
                for c in cs:
                    ve.wait_ge(*act_x.at(p, f"x{c}"))
                    ve.tensor_tensor(xlo[:, c], ps[:, 4 + c % 4], xhi[:, c], ALU.subtract).then_inc(*dve_x.mark(f"x{c}"))

            for i in range(SPLIT):
                if i == 1:
                    split_x(-1, K8)
                ve.wait_ge(*act_split.at(-1, f"w{i}"))
                ve.tensor_tensor(wlo[i][:], raw[i][:], whi[i][:], ALU.subtract).then_inc(*dve_split.mark(f"w{i}"))
            with ve.Fori(0, passes) as p:
                for f in F:
                    split(p, 2 * f + SPLIT)
                    for n in (2 * f, 2 * f + 1):
                        ve.wait_ge(*pe.at(p, f"u{n}"))
                        ve.wait_ge(*act.at(p, f"silu{n}"))
                        ve.wait_ge(*(dve.at(p, f"lo{n - 2}") if n >= 2 else dve.at(p - 1, f"lo{n + 6}")))
                        ve.tensor_tensor(h[n % 2][:], hs[n % 2][:], ps[:, 2 + n % 2], ALU.mult).then_inc(*dve.mark(f"h{n}"))
                    for n in (2 * f, 2 * f + 1):
                        ve.wait_ge(*act.at(p, f"hi{n}"))
                        ve.tensor_tensor(hlo[:, n], h[n % 2][:], hhi[:, n], ALU.subtract).then_inc(*dve.mark(f"lo{n}"))
                    split(p, 2 * f + 1 + SPLIT)
                split(p + 1, 0)
                copy_y(ve, p, "a", dve, (2, 3), ve.tensor_copy)
                split(p + 1, 1)
                split_x(p, K8[0:4])
                split(p + 1, 2)
                copy_y(ve, p, "b", dve, (2, 3), ve.tensor_copy)
                split_x(p, K8[4:8])
                split(p + 1, 3)
            ve.wait_ge(scattered, passes * 64 + 16)
            ve.wait_ge(gathered, passes * 64 + 64)
            ve.memset(spare[:], 0.0)


def combine(nc, d, gates, out):
    with ExitStack() as stack:
        s = Scope(nc, stack, "c_")
        NB = 4
        B = range(NB)
        buf = lambda name, shape: [s.sb(f"{name}{b}", shape) for b in B]
        x1, y0, y1, acc, res = (buf(n, [P, D_MODEL]) for n in ("x1", "y0", "y1", "acc", "res"))
        stats, mv, var, std, rs, shift = (buf(n, sh) for n, sh in (("stats", [P, 2, 6]), ("mv", [P, 2]), ("var", [P, 1]), ("std", [P, 1]), ("rs", [P, 1]), ("shift", [P, 1])))
        lng, lnb = s.sb("lng", [P, D_MODEL]), s.sb("lnb", [P, D_MODEL])
        spare = s.sb("spare", [P, 1])
        small_loaded = s.sem("small_loaded")
        loaded, stored = [s.sem(f"loaded{b}") for b in B], [s.sem(f"stored{b}") for b in B]
        act_0, act_n, act_s = Steps(s.sem("act_0"), ["gated0"]), Steps(s.sem("act_n"), ["norm"]), Steps(s.sem("act_s"), ["std"])
        dve = Steps(s.sem("dve_done"), ["gated1", "sum", "st0", "st1", "mv", "ve"])
        dve_r, dve_g = Steps(s.sem("dve_r"), ["rs", "shift"]), Steps(s.sem("dve_g"), ["g"])
        pool = Steps(s.sem("pool_done"), ["b"])
        block = stack.enter_context(nc.Block())
        out_d = out.rearrange("b (t p) c -> (b t) p c", p=P)
        y_d = d["ybuf"][0:PAIRS].rearrange("(k t p) c -> k t p c", k=TOP_K, p=P)
        row = lambda t: bass.ds(t, 1)

        def tiles(engine, body, last=None):
            for b in B:
                body(0, b, b, b == 0)
            with engine.Fori(1, TILES // NB) as i:
                for b in B:
                    body(i, i * NB + b, b, False)
            if last is not None:
                last(TILES - 1, NB - 1)

        @block.sync
        def _(sp):
            def load(t, b):
                for dst, src in ((y0, y_d[0]), (y1, y_d[1]), (x1, d["x1"])):
                    sp.dma_start(dst[b][:], src[row(t)].rearrange("t p c -> p (t c)")).then_inc(loaded[b], 16)

            def store(t, b):
                wait_alone(sp, (small_loaded, 32), *pool.at(t, "b"))
                sp.dma_start(out_d[row(t)].rearrange("t p c -> p (t c)"), res[b][:]).then_inc(stored[b], 16)

            for b in B:
                sp.sem_inc(stored[b], 16)
                load(b, b)
            sp.wait_ge(small_loaded, 32)
            with sp.Fori(1, TILES // NB) as i:
                for b in B:
                    wait_alone(sp, (small_loaded, 32), *dve.at(i * NB + b - NB, "sum"))
                    load(i * NB + b, b)
                    store(i * NB + b - NB, b)
            for b in B:
                store(TILES - NB + b, b)
            for b in B:
                sp.wait_ge(stored[b], 16 * (TILES // NB + 1))

        @block.gpsimd
        def _(gp):
            gp.dma_start(lng[:], d["ln2_g"].partition_broadcast(P)).then_inc(small_loaded, 16)
            gp.dma_start(lnb[:], d["ln2_b"].partition_broadcast(P)).then_inc(small_loaded, 16)
            pool.start(gp)
            gp.wait_ge(small_loaded, 32)
            with gp.Fori(0, TILES // NB) as i:
                for b in B:
                    gp.wait_ge(*dve_g.at(i * NB + b, "g"))
                    gp.tensor_tensor(res[b][:], res[b][:], lnb[:], ALU.add).then_inc(*pool.mark("b"))

        @block.scalar
        def _(sc):
            for steps in (act_0, act_n, act_s):
                steps.start(sc)

            def norm(t, b, i):
                sc.wait_ge(*dve_r.at(t, "shift"))
                sc.wait_ge(stored[b], i * 16 + 16)
                sc.activation(res[b][:], acc[b][:], ACT.Identity, scale=rs[b][:], bias=shift[b][:]).then_inc(*act_n.mark("norm"))

            def tile(i, t, b, first):
                sc.wait_ge(loaded[b], i * 48 + 48)
                sc.activation(y0[b][:], y0[b][:], ACT.Copy, scale=gates[:, 0, row(t)]).then_inc(*act_0.mark("gated0"))
                if not first:
                    norm(t - 1, (b - 1) % NB, i - 1 if b == 0 else i)
                sc.wait_ge(*dve.at(t, "ve"))
                sc.activation(std[b][:], var[b][:], ACT.Sqrt).then_inc(*act_s.mark("std"))

            tiles(sc, tile, lambda t, b: norm(t, b, TILES // NB - 1))

        @block.vector
        def _(ve):
            for steps in (dve, dve_r, dve_g):
                steps.start(ve)
            ve.wait_ge(small_loaded, 32)

            def gain(t, b):
                ve.wait_ge(*act_n.at(t, "norm"))
                ve.tensor_tensor(res[b][:], res[b][:], lng[:], ALU.mult).then_inc(*dve_g.mark("g"))

            def tile(i, t, b, first):
                ve.wait_ge(*act_0.at(t, "gated0"))
                if not isinstance(i, int):
                    ve.wait_ge(*act_n.at(t - NB, "norm"))
                ve.scalar_tensor_tensor(out=acc[b][:], in0=y1[b][:], scalar=gates[:, 1, row(t)], in1=y0[b][:], op0=ALU.mult, op1=ALU.add).then_inc(*dve.mark("gated1"))
                ve.wait_ge(*dve.at(t, "gated1"))
                ve.scalar_tensor_tensor(out=acc[b][:], in0=x1[b][:], scalar=ALPHA, in1=acc[b][:], op0=ALU.mult, op1=ALU.add).then_inc(*dve.mark("sum"))
                ve.wait_ge(*dve.at(t, "sum"))
                for half in range(2):
                    ve.bn_stats(stats[b][:, half], acc[b][:, half * QUAD:(half + 1) * QUAD]).then_inc(*dve.mark(f"st{half}"))
                ve.wait_ge(*dve.at(t, "st1"))
                ve.memset(spare[:], 0.0)
                ve.bn_aggr(mv[b][:], stats[b][:]).then_inc(*dve.mark("mv"))
                ve.wait_ge(*dve.at(t, "mv"))
                ve.tensor_scalar(var[b][:], mv[b][:, 1:2], LN_EPS, None, ALU.add).then_inc(*dve.mark("ve"))
                if not first:
                    gain(t - 1, (b - 1) % NB)
                ve.wait_ge(*act_s.at(t, "std"))
                ve.reciprocal(rs[b][:], std[b][:]).then_inc(*dve_r.mark("rs"))
                ve.wait_ge(*dve_r.at(t, "rs"))
                ve.tensor_scalar(shift[b][:], mv[b][:, 0:1], rs[b][:], -1.0, ALU.mult, ALU.mult).then_inc(*dve_r.mark("shift"))

            tiles(ve, tile, gain)


INPUTS = ["x", "w_in", "conv_w", "a_log_f", "dt_bias_f", "a_log_b", "dt_bias_b", "delta_norm_w", "sgu_ln_g", "sgu_ln_b",
          "w_spatial", "b_spatial", "w_out", "ln1_g", "ln1_b", "w_router", "router_bias", "w_gate", "w_up", "w_down",
          "ln2_g", "ln2_b"]


def build(nc, d, out):
    scratch = {
        "raw": [P, 3, HEADS, SEQ + 2 * HALO], "z": [TILES, P, QUAD], "sgu": [TILES, P, QUAD],
        "pk": [TILES, P, 4, QUAD], "gb": [TILES * CHAINS, P], "x1": [TILES, P, D_MODEL],
        "ybuf": [PAIRS + PASS_ROWS, D_MODEL],
    }
    for name, shape in scratch.items():
        d[name] = nc.dram_tensor("s_" + name, shape, F32, kind="Internal").ap()
    with ExitStack() as stack:
        sb = lambda name, shape, dt=F32: stack.enter_context(nc.sbuf_tensor(name, shape, dt))
        ident = sb("ident", [P, P])
        gates = sb("gates", [P, TOP_K, TILES])
        logits = sb("logits", [P, TILES, N_EXPERTS])
        scatter, gather = sb("scatter", [P, COLS_T], I32), sb("gather", [P, COLS_T], I32)
        plan, n_passes = sb("plan", [P, COLS_P, FIELDS], I32), sb("n_passes", [P, 1], I32)
        constants(nc, ident)
        with ExitStack() as first:
            sb1 = lambda name, shape: first.enter_context(nc.sbuf_tensor(name, shape, F32))
            GS = sb1("gate_scalars", [P, TILES, KINDS, CHAINS])
            with nc.sbuf_tensor("gates_raw", [P, TILES, 16], F32) as graw:
                project(nc, d, ident, graw)
                gates_and_conv(nc, d, ident, graw, GS)
            outs = [sb1("out_f", [P, TILES, QUAD]), sb1("out_b", [P, TILES, QUAD])]
            delta(nc, d, ident, GS, outs)
            mix(nc, d, ident, outs, logits)
        route(nc, d, logits, gates, scatter, gather, plan, n_passes)
        experts(nc, d, ident, scatter, gather, plan, n_passes)
        combine(nc, d, gates, out)


def kernel(**inputs):
    import numpy as np
    import concourse.bacc as bacc
    from concourse.bass_utils import run_bass_kernel_spmd

    nc = bacc.Bacc("TRN2", target_bir_lowering=False, num_devices=1)
    arrays, d = {}, {}
    for name in INPUTS:
        a = np.ascontiguousarray(inputs[name])
        arrays["in_" + name] = a
        d[name] = nc.dram_tensor("in_" + name, a.shape, mybir.dt.from_np(a.dtype), kind="ExternalInput").ap()
    out = nc.dram_tensor("out", (1, SEQ, D_MODEL), F32, kind="ExternalOutput").ap()
    build(nc, d, out)
    return run_bass_kernel_spmd(nc, [arrays], core_ids=[0]).results[0]["out"]
```
